# Optimizing a Trainium2 kernel written in Bass

```python
import math
import jax, jax.numpy as jnp
from jax import lax
import numpy as np

D_MODEL = 1024
BATCH = 1
SEQ = 256
DEPTH = 2

GRID_W = 64
CTX_LEN = 256
F32 = jnp.float32
EPS = 1e-6

HY_WIDTH = 256
POOL_WINDOWS = (2, 4, 8, 16)
POOL_WIDTH = 256
POOL_GROUP = POOL_WIDTH // len(POOL_WINDOWS)
MLA_HEADS = 8
QK_NOPE = 64
QK_ROPE = 32
V_DIM = 64
Q_LORA = 384
KV_LORA = 256
MLA_WIDTH = MLA_HEADS * V_DIM
D_MIX = HY_WIDTH + POOL_WIDTH + MLA_WIDTH
IN_WIDTH = 3 * HY_WIDTH + POOL_WIDTH + Q_LORA + KV_LORA + QK_ROPE
IN_SPLITS = (3 * HY_WIDTH,
             3 * HY_WIDTH + POOL_WIDTH,
             3 * HY_WIDTH + POOL_WIDTH + Q_LORA,
             3 * HY_WIDTH + POOL_WIDTH + Q_LORA + KV_LORA)
SM_SCALE = (QK_NOPE + QK_ROPE) ** -0.5
ROPE_THETA = 10000.0
Q_BLOCK = 128

SHORT_CONV = 3
FILT_EMB = 33
FILT_BANDS = (FILT_EMB - 1) // 2
FILT_HIDDEN = 64
DECAY_TARGET = 1e-2
FAST_DECAY_PCT = 0.3
SLOW_DECAY_PCT = 1.5

D_FF = 2816
N_EXPERTS = 8
TOP_K = 2
EXPERT_FF = 2816
N_DENSE = (DEPTH + 1) // 2
N_MOE = DEPTH // 2

kernel_name = 'hybrid_hyena_pool_mla_moe_dit'

def rmsnorm(x, g):
    x32 = x.astype(F32)
    y = x32 * lax.rsqrt(jnp.mean(x32 * x32, axis=-1, keepdims=True) + EPS)
    return (y * g.astype(F32)).astype(x.dtype)

def modulate(h, shift, scale):
    return h * (1 + scale) + shift

def short_conv(u, w, b):
    L = u.shape[1]
    p = SHORT_CONV // 2
    up = jnp.pad(u, ((0, 0), (p, p), (0, 0)))
    out = up[:, 0:L] * w[0]
    for j in range(1, SHORT_CONV):
        out = out + up[:, j:j + L] * w[j]
    return out + b

def implicit_filter(L, w1, b1, freq1, w2, b2, freq2, w3):
    pos = jnp.arange(L, dtype=F32)
    t = (pos / max(L - 1, 1))[:, None]
    w = 2.0 * math.pi * pos[:, None] / L
    f = jnp.linspace(1e-4, FILT_BANDS - 1, FILT_BANDS, dtype=F32)[None, :]
    feat = jnp.concatenate([t, jnp.cos(f * w), -jnp.sin(f * w)], axis=-1)
    hdn = jnp.sin(freq1.astype(F32) * (feat @ w1.astype(F32) + b1.astype(F32)))
    hdn = jnp.sin(freq2.astype(F32) * (hdn @ w2.astype(F32) + b2.astype(F32)))
    h = hdn @ w3.astype(F32)
    max_decay = math.log(DECAY_TARGET) / FAST_DECAY_PCT
    min_decay = math.log(DECAY_TARGET) / SLOW_DECAY_PCT
    deltas = jnp.linspace(min_decay, max_decay, HY_WIDTH, dtype=F32)
    decay = jnp.exp(-t * jnp.abs(deltas))
    h = h * jnp.concatenate([decay, decay], axis=-1)
    h_fwd, h_bwd = h[:, :HY_WIDTH], h[:, HY_WIDTH:]
    filt2 = jnp.concatenate([h_fwd, jnp.zeros((1, HY_WIDTH), F32), h_bwd[1:][::-1]], axis=0)
    return filt2 / jnp.sum(jnp.abs(filt2), axis=0, keepdims=True)

def fft_conv(z, filt2):
    L = z.shape[1]
    zf = jnp.fft.rfft(z, n=2 * L, axis=1)
    hf = jnp.fft.rfft(filt2, n=2 * L, axis=0)
    return jnp.fft.irfft(zf * hf[None], n=2 * L, axis=1)[:, :L]

def hyena_mix(u, sw, sb, filt, bias):
    uc = short_conv(u, sw, sb)
    x0, x1, v = jnp.split(uc, 3, axis=-1)
    z = (x1 * v).astype(F32)
    h = implicit_filter(u.shape[1], *filt)
    y = fft_conv(z, h) + bias.astype(F32) * z
    return (x0.astype(F32) * y).astype(u.dtype)

def pool_mix(p, pool_w, pool_scale):
    B, L, _ = p.shape
    p32 = p.astype(F32)
    cs = jnp.concatenate([jnp.zeros((B, 1, POOL_WIDTH), F32), jnp.cumsum(p32, axis=1)], axis=1)
    t = jnp.arange(L)
    parts = []
    for g, win in enumerate(POOL_WINDOWS):
        lo = jnp.clip(t - win // 2, 0, L)
        hi = jnp.clip(t + win // 2, 0, L)
        sl = slice(g * POOL_GROUP, (g + 1) * POOL_GROUP)
        cg = cs[..., sl]
        mean = (cg[:, hi] - cg[:, lo]) / (hi - lo).astype(F32)[None, :, None]
        parts.append(mean - p32[..., sl])
    d = jnp.stack(parts, axis=2)
    y = jnp.einsum('blgc,gcd->blgd', d, pool_w.astype(F32)).reshape(B, L, POOL_WIDTH)
    return (y * pool_scale.astype(F32)).astype(p.dtype)

def axial_rope(rows):
    n_freq = QK_ROPE // 4
    inv_freq = 1.0 / (ROPE_THETA ** (jnp.arange(n_freq, dtype=F32) / n_freq))
    row = jnp.repeat(jnp.arange(rows, dtype=F32), GRID_W)
    col = jnp.tile(jnp.arange(GRID_W, dtype=F32), rows)
    ang = jnp.concatenate([row[:, None] * inv_freq, col[:, None] * inv_freq], axis=-1)
    return jnp.cos(ang), jnp.sin(ang)

def apply_rope(x, cos, sin):
    x32 = x.astype(F32)
    half = x.shape[-1] // 2
    x1, x2 = x32[..., :half], x32[..., half:]
    return jnp.concatenate([x1 * cos - x2 * sin, x1 * sin + x2 * cos], axis=-1).astype(x.dtype)

def mla_q(cq, g, w_uq, rope):
    B, L, _ = cq.shape
    q = (rmsnorm(cq, g) @ w_uq).reshape(B, L, MLA_HEADS, QK_NOPE + QK_ROPE)
    q_nope, q_pe = q[..., :QK_NOPE], q[..., QK_NOPE:]
    if rope is not None:
        q_pe = apply_rope(q_pe, rope[0][:, None], rope[1][:, None])
    return jnp.concatenate([q_nope, q_pe], axis=-1)

def mla_kv(ckv, kpe, g, w_ukv, rope):
    B, L, _ = ckv.shape
    kv = (rmsnorm(ckv, g) @ w_ukv).reshape(B, L, MLA_HEADS, QK_NOPE + V_DIM)
    k_nope, v = kv[..., :QK_NOPE], kv[..., QK_NOPE:]
    if rope is not None:
        kpe = apply_rope(kpe, rope[0], rope[1])
    k_pe = jnp.broadcast_to(kpe[:, :, None, :], (B, L, MLA_HEADS, QK_ROPE))
    return jnp.concatenate([k_nope, k_pe], axis=-1), v

def attention(q, k, v):
    s = jnp.einsum('bqhd,bkhd->bhqk', q.astype(F32), k.astype(F32)) * SM_SCALE
    p = jax.nn.softmax(s, axis=-1)
    return jnp.einsum('bhqk,bkhd->bqhd', p, v.astype(F32)).astype(v.dtype)

def blocked_attention(q, k, v):
    B, L, H, Dq = q.shape
    nb = L // Q_BLOCK
    qb = q.reshape(B, nb, Q_BLOCK, H, Dq).swapaxes(0, 1)
    ob = lax.map(lambda qi: attention(qi, k, v), qb)
    return ob.swapaxes(0, 1).reshape(B, L, H, V_DIM)

def swiglu(h, wg, wu, wd):
    return (jax.nn.silu(h @ wg) * (h @ wu)) @ wd

def moe_swiglu(h, w_router, wg, wu, wd):
    logits = (h @ w_router).astype(F32)
    top_val, top_idx = lax.top_k(logits, TOP_K)
    gates = jax.nn.softmax(top_val, axis=-1)
    comb = jnp.sum(jax.nn.one_hot(top_idx, N_EXPERTS, dtype=F32) * gates[..., None], axis=-2)
    out = jnp.zeros(h.shape, F32)
    for e in range(N_EXPERTS):
        out = out + comb[..., e:e + 1] * swiglu(h, wg[e], wu[e], wd[e]).astype(F32)
    return out.astype(h.dtype)

def channel_mix(h, layer, ffn_wg, ffn_wu, ffn_wd, moe_router, moe_wg, moe_wu, moe_wd):
    i = layer // 2
    if layer % 2 == 0:
        return swiglu(h, ffn_wg[i], ffn_wu[i], ffn_wd[i])
    return moe_swiglu(h, moe_router[i], moe_wg[i], moe_wu[i], moe_wd[i])

def setup_inputs(seed: int = 0) -> dict:
    key = jax.random.key(seed)
    keys = iter(jax.random.split(key, 48))
    D = D_MODEL

    def normal(shape, scale=1.0):
        return jax.random.normal(next(keys), shape, F32) * scale

    def gain(shape):
        return 1.0 + normal(shape, 0.02)

    return {
        'x': normal((BATCH, SEQ, D)),
        'c': normal((BATCH, D)),
        'ctx': normal((BATCH, CTX_LEN, D)),
        'c_ctx': normal((D,)),
        'norm1_g': gain((DEPTH, D)),
        'norm2_g': gain((DEPTH, D)),
        'w_ada': normal((DEPTH, D, 6 * D), 0.5 * D ** -0.5),
        'b_ada': normal((DEPTH, 6 * D), 0.02),
        'w_in': normal((DEPTH, D, IN_WIDTH), D ** -0.5),
        'hy_short_w': normal((DEPTH, SHORT_CONV, 3 * HY_WIDTH), SHORT_CONV ** -0.5),
        'hy_short_b': normal((DEPTH, 3 * HY_WIDTH), 0.02),
        'filt_w1': normal((DEPTH, FILT_EMB, FILT_HIDDEN), FILT_EMB ** -0.5),
        'filt_b1': normal((DEPTH, FILT_HIDDEN), 0.02),
        'filt_freq1': gain((DEPTH, FILT_HIDDEN)),
        'filt_w2': normal((DEPTH, FILT_HIDDEN, FILT_HIDDEN), FILT_HIDDEN ** -0.5),
        'filt_b2': normal((DEPTH, FILT_HIDDEN), 0.02),
        'filt_freq2': gain((DEPTH, FILT_HIDDEN)),
        'filt_w3': normal((DEPTH, FILT_HIDDEN, 2 * HY_WIDTH), FILT_HIDDEN ** -0.5),
        'hy_bias': normal((DEPTH, HY_WIDTH), 0.5),
        'pool_w': normal((DEPTH, len(POOL_WINDOWS), POOL_GROUP, POOL_GROUP), POOL_GROUP ** -0.5),
        'pool_scale': gain((DEPTH, POOL_WIDTH)),
        'q_norm_g': gain((DEPTH, Q_LORA)),
        'w_uq': normal((DEPTH, Q_LORA, MLA_HEADS * (QK_NOPE + QK_ROPE)), Q_LORA ** -0.5),
        'kv_norm_g': gain((DEPTH, KV_LORA)),
        'w_ukv': normal((DEPTH, KV_LORA, MLA_HEADS * (QK_NOPE + V_DIM)), KV_LORA ** -0.5),
        'w_out': normal((DEPTH, D_MIX, D), D_MIX ** -0.5),
        'ffn_wg': normal((N_DENSE, D, D_FF), D ** -0.5),
        'ffn_wu': normal((N_DENSE, D, D_FF), D ** -0.5),
        'ffn_wd': normal((N_DENSE, D_FF, D), D_FF ** -0.5),
        'moe_router': normal((N_MOE, D, N_EXPERTS), D ** -0.5),
        'moe_wg': normal((N_MOE, N_EXPERTS, D, EXPERT_FF), D ** -0.5),
        'moe_wu': normal((N_MOE, N_EXPERTS, D, EXPERT_FF), D ** -0.5),
        'moe_wd': normal((N_MOE, N_EXPERTS, EXPERT_FF, D), EXPERT_FF ** -0.5),
        'final_g': gain((D,)),
    }

def reference(x, c, ctx, c_ctx, norm1_g, norm2_g, w_ada, b_ada, w_in, hy_short_w, hy_short_b,
              filt_w1, filt_b1, filt_freq1, filt_w2, filt_b2, filt_freq2, filt_w3, hy_bias,
              pool_w, pool_scale, q_norm_g, w_uq, kv_norm_g, w_ukv, w_out,
              ffn_wg, ffn_wu, ffn_wd, moe_router, moe_wg, moe_wu, moe_wd, final_g):
    B, L, _ = x.shape
    ROWS = L // GRID_W
    rope = axial_rope(ROWS)
    silu_c = jax.nn.silu(c)
    silu_ctx = jax.nn.silu(c_ctx)
    xl, xc = x, ctx
    for l in range(DEPTH):
        last = l == DEPTH - 1
        mod_l = jnp.split((silu_c @ w_ada[l] + b_ada[l])[:, None, :], 6, axis=-1)
        mod_c = jnp.split(silu_ctx @ w_ada[l] + b_ada[l], 6, axis=-1)
        filt = (filt_w1[l], filt_b1[l], filt_freq1[l], filt_w2[l], filt_b2[l], filt_freq2[l], filt_w3[l])

        def mix_heads(hy, pool, att):
            y_hy = hyena_mix(hy, hy_short_w[l], hy_short_b[l], filt, hy_bias[l])
            y_pool = pool_mix(pool, pool_w[l], pool_scale[l])
            y_att = att.reshape(att.shape[0], att.shape[1], MLA_WIDTH)
            return jnp.concatenate([y_hy, y_pool, y_att], axis=-1) @ w_out[l]

        hl = modulate(rmsnorm(xl, norm1_g[l]), mod_l[0], mod_l[1])
        hc = modulate(rmsnorm(xc, norm1_g[l]), mod_c[0], mod_c[1])
        hy_l, pool_l, cq_l, ckv_l, kpe_l = jnp.split(hl @ w_in[l], IN_SPLITS, axis=-1)
        hy_c, pool_c, cq_c, ckv_c, kpe_c = jnp.split(hc @ w_in[l], IN_SPLITS, axis=-1)
        k_c, v_c = mla_kv(ckv_c, kpe_c, kv_norm_g[l], w_ukv[l], None)
        k_l, v_l = mla_kv(ckv_l, kpe_l, kv_norm_g[l], w_ukv[l], rope)
        q_l = mla_q(cq_l, q_norm_g[l], w_uq[l], rope)
        att_l = blocked_attention(q_l, jnp.concatenate([k_c, k_l], axis=1),
                                  jnp.concatenate([v_c, v_l], axis=1))
        xl = xl + mod_l[2] * mix_heads(hy_l, pool_l, att_l)
        if not last:
            att_c = attention(mla_q(cq_c, q_norm_g[l], w_uq[l], None), k_c, v_c)
            xc = xc + mod_c[2] * mix_heads(hy_c, pool_c, att_c)
            hc = modulate(rmsnorm(xc, norm2_g[l]), mod_c[3], mod_c[4])
            xc = xc + mod_c[5] * channel_mix(hc, l, ffn_wg, ffn_wu, ffn_wd, moe_router, moe_wg, moe_wu, moe_wd)
        hl = modulate(rmsnorm(xl, norm2_g[l]), mod_l[3], mod_l[4])
        xl = xl + mod_l[5] * channel_mix(hl, l, ffn_wg, ffn_wu, ffn_wd, moe_router, moe_wg, moe_wu, moe_wd)
    return rmsnorm(xl, final_g)


_drawn_inputs = setup_inputs


def setup_inputs(seed=0):
    import zlib

    import numpy as np

    out = dict(_drawn_inputs(seed))
    spreads = {}
    factors = {'ctx': 3.325,
     'norm1_g': 6.291,
     'norm2_g': 22.029,
     'hy_short_b': 6.849,
     'filt_b1': 8.0,
     'filt_freq1': 8.0,
     'filt_b2': 8.0,
     'filt_freq2': 8.0,
     'pool_scale': 35.8,
     'q_norm_g': 24.228,
     'kv_norm_g': 24.015,
     'final_g': 7.992}
    for name, (base, spread) in spreads.items():
        noise = np.random.default_rng([zlib.crc32(name.encode()), seed]).standard_normal(out[name].shape)
        drawn = base * np.exp(spread * noise) if base else spread * noise
        out[name] = __import__('jax').numpy.asarray(drawn.astype(out[name].dtype))
    for name, factor in factors.items():
        out[name] = (out[name] * factor).astype(out[name].dtype)
    return out
```

```python
import math
from contextlib import ExitStack

import concourse.bass as bass
import numpy as np
from concourse import mybir

F32 = mybir.dt.float32
F32R = mybir.dt.float32r
U32 = mybir.dt.uint32
ALU = mybir.AluOpType
ACT = mybir.ActivationFunctionType
AX = mybir.AxisListType

P = 128
D = 1024
L = 256
DEPTH = 2
KD = D // P
NT = 4
HY = 256
POOLW = 256
WINDOWS = (2, 4, 8, 16)
GROUP = 64
HEADS = 8
NOPE, ROPE, VD = 64, 32, 64
QL, KVL = 384, 256
KQ, KKV = QL // P, KVL // P
SM_SCALE = (NOPE + ROPE) ** -0.5
INB = POOLW + QL + KVL + 2 * ROPE
HB = INB // 2
EPS = 1e-6
FF = 2816
NE = 8
FC = FF // 256
FH = 64
FE = 33
GRAN = 2048
RING = 3
TWO_PI_A = 6.28125
TWO_PI_B = 2 * math.pi - TWO_PI_A
ROUND = 1.5 * 2 ** 23

PAR = {}
_at = 0
for _n, _w in (("g1", KD), ("g2", KD), ("bada", 48), ("qg", KQ), ("kvg", KKV), ("sw", 18), ("sb", 6), ("hyb", 2),
               ("psc", 2), ("b1", 1), ("f1", 1), ("b2", 1), ("f2", 1)):
    PAR[_n] = (_at, _at + _w)
    _at += _w
NPAR = _at


def stream_plan():
    plan = []
    for l in range(DEPTH):
        plan += [("ada", l, i) for i in range(24)]
        plan += [("ina", l, i) for i in range(3)]
        plan += [("inb", l, i) for i in range(4)]
        plan += [("out", l, i) for i in range(4)]
        passes = [("ffn", 0), ("ffn", 0)] if l == 0 else [("moe", e) for e in range(NE)]
        for kind, e in passes:
            plan += [(kind, e, i) for i in range(3 * FC)]
    return plan


def ffn_order():
    order = []
    for s in range(FC):
        order += [("gu", s, 0), ("gu", s, 1)]
        if s:
            order.append(("d", s - 1, 0))
    return order + [("d", FC - 1, 0)]


class Steps:

    def __init__(self, table, key):
        self.table, self.key, self.count = table, key, 0

    def __call__(self, *names):
        self.count += 1
        for n in names:
            self.name(n)
        return self.count

    def name(self, n):
        if not self.table["final"]:
            self.table["count"][n] = (self.key, self.count)


def build(nc, io, table):
    with ExitStack() as ctx:
        def sb(name, shape, dt=F32):
            return ctx.enter_context(nc.sbuf_tensor(name, shape, dt))

        X = sb("X", [P, NT, D])
        hT_hi = sb("hT_hi", [P, KD, 512], F32R)
        hT_lo = sb("hT_lo", [P, KD, 512], F32R)
        raw = sb("raw", [P, RING, GRAN])
        w_hi = sb("w_hi", [P, RING, GRAN], F32R)
        w_lo = sb("w_lo", [P, RING, GRAN], F32R)
        f_hi = sb("f_hi", [P, 512], F32R)
        f_lo = sb("f_lo", [P, 512], F32R)
        par = sb("par", [P, DEPTH, NPAR])
        ident = sb("ident", [P, P])
        ones = sb("ones", [P, P])
        sel = sb("sel", [4, 2])
        cvec = sb("cvec", [P, KD, 2])
        csil = sb("csil", [P, KD, 2])
        mod = sb("mod", [P, 48, 2])
        gsc = sb("gsc", [P, 2, KD, 2])
        small = sb("small", [P, 256])
        router = sb("router", [P, KD, NE])
        r_hi = sb("r_hi", [P, KD, NE], F32R)
        r_lo = sb("r_lo", [P, KD, NE], F32R)
        iota8 = sb("iota8", [P, NE])
        idx8 = sb("idx8", [P, NE], U32)
        comb = sb("comb", [P, 2, NE])
        NA = 20352
        arena = sb("arena", [P, NA])
        PS = ctx.enter_context(nc.psum_tensor("PS", [P, 8, 512], F32))

        def sem(name):
            return ctx.enter_context(nc.semaphore(name))

        pe_done, act_done, dve_done = sem("pe_done"), sem("act_done"), sem("dve_done")
        raw_full = [sem(f"raw_full{i}") for i in range(RING)]
        loaded = {"start": (sem("start_loaded"), 16 * 11), "final": (sem("final_gain_loaded"), 16),
                "stored": (sem("stored"), 32)}
        for l in range(DEPTH):
            loaded[f"hy {l}"] = (sem(f"hyena_tables_loaded{l}"), 32)
            loaded[f"pool {l}"] = (sem(f"pool_tables_loaded{l}"), 32)
            loaded[f"mla {l}"] = (sem(f"attention_weights_loaded{l}"), 64)

        def after(name):
            return table["count"].get(name, (None, 1))[1]

        def reader_of(job):
            return act_done if table["count"].get("read " + job, ("act", 1))[0] == "act" else dve_done

        def bank_of(job):
            return PS[:, table["bank"][job], :]

        def A(off, *shape):
            n = int(np.prod(shape))
            assert off + n <= NA
            v = arena[:, off:off + n]
            if len(shape) == 1:
                return v
            letters = "abcd"[:len(shape)]
            kw = {c: s for c, s in zip(letters[1:], shape[1:])}
            return v.rearrange(f"p ({' '.join(letters)}) -> p {' '.join(letters)}", **kw)

        xn = A(0, NT, D)
        tn = A(4096, 2, 512)
        Bm = A(4096, NT, INB)
        uc = A(7936, 6, 512)
        upad = A(11008, 2, 2, 258)
        hyc = A(12040, 3840)
        Cf = A(12040, 2, 256)
        Sf = A(12552, 2, 256)
        Sz0 = A(13064, 2, 128)
        Cn0 = A(13320, 2, 128)
        IC = A(13576, 2, 256)
        IS = A(14088, 2, 256)
        decay = A(14600, 2, 512)
        featT = A(15624, 256)
        fw = A(15880, 640)
        fw1, fw2, fw3 = A(15880, 64), A(15944, 64), A(16008, 512)
        hfil = A(16520, 2, 512)
        hp, hm = A(17544, 2, 256), A(18056, 2, 256)
        HA, HBs = A(18568, 2, 256), A(19080, 2, 256)
        HD0 = A(19592, 256)
        farg = A(0, 2, 256)
        fsc = A(512, 2, 256)
        zT = A(0, 2, 512)
        Yc, Ys = A(1024, 2, 512), A(2048, 2, 512)
        ytmp = A(3072, 2, 512)
        pm = A(0, 4, 2, 256)
        dT = A(2048, 2, 512)
        junk = A(3072, QL)
        pwts = A(3456, 4, GROUP)
        row4 = arena[0:4, 11008:12032].rearrange("p (a b) -> p a b", b=512)
        wuq = A(7936, KQ, HEADS, P)
        wukv = A(11008, KKV, 1024)
        cqT = A(13056, KQ, 512)
        ckvT = A(14592, KKV, 512)
        qT = A(15616, HEADS, 512)
        ropeq = A(19712, 512)
        ropek = A(20224, 2, 64)
        KT = A(0, HEADS, 512)
        V = A(4096, NT, 512)
        qtmp = A(6144, 256)
        att = A(7936, NT, 512)
        prob = A(9984, 2, 512)
        probT = A(11008, 2, 512)
        gbc = A(12032, 2, D)
        diag = A(14080, 8, P)
        rtmp = A(15104, 2, 512)
        sg = A(4096, 2, 256)
        hh = A(4608, 2, 256)
        acc = A(5120, 2, D)
        gbf = A(7168, D)
        fdiag = A(8192, 8, P)
        ftmp = A(9216, 2, 512)
        fing = A(10240, D)
        acc2 = A(10240, 2, D)

        plan = stream_plan()
        gindex = {}
        counts = {}
        for g, (kind, e, i) in enumerate(plan):
            n = counts.get((kind, e, i), 0)
            counts[(kind, e, i)] = n + 1
            gindex[(kind, e, i, n)] = g
        NG = len(plan)
        order = ffn_order()
        fpos = {x: i for i, x in enumerate(order)}

        def width(kind):
            return 4 * HB if kind == "inb" else GRAN

        def source(kind, e, i):
            return io[kind][e, i]

        blk = ctx.enter_context(nc.Block())
        layer_streams = {0: (0, 1), 1: (1,)}

        def tiles_of(streams):
            return [2 * s + j for s in streams for j in range(2)]

        def span(streams):
            return slice(256 * streams[0], 512)

        @blk.tensor
        def _(eng):
            did = Steps(table, "pe")
            state = {"next": 0, "last": [None] * 8}

            def bank(job, b=None):
                if b is None:
                    b = state["next"]
                    state["next"] = (b + 1) % 8
                if state["last"][b]:
                    eng.wait_ge(reader_of(state["last"][b]), after("read " + state["last"][b]))
                state["last"][b] = job
                table["bank"][job] = b
                return PS[:, b, :]

            mm = nc.tensor.matmul

            def granule(g):
                eng.wait_ge(dve_done, after(f"lo {g}"))
                return w_hi[:, g % RING, :], w_lo[:, g % RING, :]

            def split3(out, s_hi, s_lo, m_hi, m_lo, start, stop):
                mm(out, s_hi, m_hi, start=start, stop=False)
                mm(out, s_hi, m_lo, start=False, stop=False)
                return mm(out, s_lo, m_hi, start=False, stop=stop)

            def modulation(l):
                eng.wait_ge(dve_done, after(f"cs {l}"))
                for n in range(12):
                    o = bank(f"ada {l} {n}")
                    for half in range(2):
                        g = gindex[("ada", l, 2 * n + half, 0)]
                        hi, lo = granule(g)
                        for k in range(4):
                            kk = 4 * half + k
                            mm(o, hT_hi[:, kk, 0:P], hi[:, 512 * k:512 * k + 512], start=kk == 0, stop=False)
                            i = mm(o, hT_hi[:, kk, 0:P], lo[:, 512 * k:512 * k + 512], start=False, stop=kk == 7)
                        i.then_inc(pe_done, 1)
                        did(f"used {g}", f"ada {l} {n}")
                    if n:
                        turn(l, n - 1)
                turn(l, 11)

            def turn(l, n):
                eng.wait_ge(act_done, after(f"row {l} {n}"))
                o = bank(f"modT {l} {n}")
                for j in range(4):
                    i = mm(o[:, 2 * j:2 * j + 2], row4[:, n % 2, P * j:P * j + P], sel[:, :], start=True, stop=True)
                i.then_inc(pe_done, 1)
                did(f"modT {l} {n}")

            def filters(l):
                eng.wait_ge(*loaded[f"hy {l}"])
                mm(bank(f"f1 {l}")[0:FH, 0:L], fw1[0:FE, :], featT[0:FE, :], start=True, stop=True).then_inc(pe_done, 1)
                did(f"f1 {l}")
                eng.wait_ge(act_done, after(f"sin1 {l}"))
                mm(bank(f"f2 {l}")[0:FH, 0:L], fw2[0:FH, :], farg[0:FH, 0, :], start=True, stop=True).then_inc(pe_done, 1)
                did(f"f2 {l}")
                eng.wait_ge(act_done, after(f"sin2 {l}"))
                for t in range(2):
                    mm(bank(f"f3 {l} {t}"), farg[0:FH, 1, P * t:P * t + P], fw3[0:FH, :], start=True, stop=True).then_inc(pe_done, 1)
                    did(f"f3 {l} {t}")
                eng.wait_ge(dve_done, after(f"habs {l}"))
                o = bank(f"fn {l}")
                for ct in range(2):
                    for t in range(2):
                        i = mm(o[:, ct:ct + 1], fsc[:, t, P * ct:P * ct + P], ones[:, 0:1], start=t == 0, stop=t == 1)
                i.then_inc(pe_done, 1)
                did(f"fn {l}")
                for ft in range(2):
                    s = slice(P * ft, P * ft + P)
                    o = bank(f"fA {l} {ft}")
                    for t in range(2):
                        mm(o[:, 0:L], Cf[:, t, s], hp[:, t, :], start=t == 0, stop=t == 1)
                    for t in range(2):
                        basis = Sz0[:, t, :] if ft == 0 else Sf[:, t, s]
                        i = mm(o[:, L:2 * L], basis, hm[:, t, :], start=t == 0, stop=t == 1)
                    i.then_inc(pe_done, 1)
                    did(f"fA {l} {ft}")
                o = bank(f"fD {l}")
                for t in range(2):
                    i = mm(o[:, 0:L], Cn0[:, t, :], hp[:, t, :], start=t == 0, stop=t == 1)
                i.then_inc(pe_done, 1)
                did(f"fD {l}")

            def norm_turn(l, w, streams):
                for k in range(KD):
                    for t in tiles_of(streams):
                        eng.wait_ge(dve_done, after(f"xn {l} {w} {t}"))
                    o = bank(f"nT {l} {w} {k}")
                    for t in tiles_of(streams):
                        i = nc.tensor.transpose(o[:, P * t:P * t + P], xn[:, t, P * k:P * k + P], ident[:, :])
                    i.then_inc(pe_done, 1)
                    did(f"nT {l} {w} {k}")

            def project_in(l, streams):
                sp = span(streams)
                for ct in range(6):
                    g = gindex[("ina", l, ct // 2, 0)]
                    hi, lo = granule(g)
                    o = bank(f"u {l} {ct}")
                    for k in range(KD):
                        if ct == 0:
                            eng.wait_ge(dve_done, after(f"hT {l} 1 {k}"))
                        s = slice(256 * k + P * (ct % 2), 256 * k + P * (ct % 2) + P)
                        i = split3(o[:, sp], hi[:, s], lo[:, s], hT_hi[:, k, sp], hT_lo[:, k, sp], k == 0, k == 7)
                    i.then_inc(pe_done, 1)
                    did(f"u {l} {ct}", f"used {g}")
                for b in range(2):
                    ts = tiles_of(streams) if b == 0 else range(NT)
                    os = {t: bank(f"B {l} {b} {t}") for t in ts}
                    for half in range(2):
                        g = gindex[("inb", l, 2 * b + half, 0)]
                        hi, lo = granule(g)
                        for t in ts:
                            for k in range(4):
                                kk, s = 4 * half + k, slice(HB * k, HB * k + HB)
                                i = split3(os[t][:, 0:HB], hT_hi[:, kk, P * t:P * t + P], hT_lo[:, kk, P * t:P * t + P],
                                           hi[:, s], lo[:, s], kk == 0, kk == 7)
                            if half:
                                i.then_inc(pe_done, 1)
                                did(f"B {l} {b} {t}")
                        if half:
                            did.name(f"used {g}")
                        else:
                            i.then_inc(pe_done, 1)
                            did(f"used {g}")

            def hyena(l, streams):
                sp = span(streams)
                n = 256 * len(streams)
                for ct in range(2):
                    eng.wait_ge(dve_done, after(f"z {l} {ct}"))
                    o = bank(f"zT {l} {ct}")
                    for j, s in enumerate(streams):
                        for t in range(2):
                            i = nc.tensor.transpose(o[:, 256 * s + P * t:256 * s + P * t + P],
                                                    uc[:, 2 + ct, 256 * s + P * t:256 * s + P * t + P], ident[:, :])
                    i.then_inc(pe_done, 1)
                    did(f"zT {l} {ct}")
                for ft in range(2):
                    for nm, basis in (("c", Cf), ("s", Sf)):
                        eng.wait_ge(act_done, after(f"zTs {l} 0"))
                        eng.wait_ge(act_done, after(f"zTs {l} 1"))
                        o = bank(f"Z{nm} {l} {ft}")
                        for t in range(2):
                            i = mm(o[:, sp], basis[:, t, P * ft:P * ft + P], zT[:, t, sp], start=t == 0, stop=t == 1)
                        i.then_inc(pe_done, 1)
                        did(f"Z{nm} {l} {ft}")
                eng.wait_ge(dve_done, after(f"Y {l}"))
                for ct in range(2):
                    o = bank(f"y {l} {ct}")
                    for s in streams:
                        for ft in range(2):
                            a = slice(256 * s + P * ct, 256 * s + P * ct + P)
                            mm(o[:, 256 * s:256 * s + 256], Yc[:, ft, a], IC[:, ft, :], start=ft == 0, stop=False)
                            i = mm(o[:, 256 * s:256 * s + 256], Ys[:, ft, a], IS[:, ft, :], start=False, stop=ft == 1)
                    i.then_inc(pe_done, 1)
                    did(f"y {l} {ct}")

            def pooling(l, streams):
                eng.wait_ge(*loaded[f"pool {l}"])
                sp = span(streams)
                for t in tiles_of(streams):
                    eng.wait_ge(act_done, after(f"Bs {l} 0 {t}"))
                for g in range(4):
                    o = bank(f"d {l} {g}")
                    for s in streams:
                        for t in range(2):
                            i = mm(o[0:GROUP, 256 * s:256 * s + 256], Bm[:, 2 * s + t, GROUP * g:GROUP * g + GROUP],
                                   pm[:, g, t, :], start=t == 0, stop=t == 1)
                    i.then_inc(pe_done, 1)
                    did(f"d {l} {g}")
                for pair in range(2):
                    o = bank(f"yp {l} {pair}")
                    for j in range(2):
                        g = 2 * pair + j
                        eng.wait_ge(act_done, after(f"dT {l} {g}"))
                        i = mm(o[GROUP * j:GROUP * j + GROUP, sp], pwts[0:GROUP, g, :], dT[0:GROUP, g % 2, sp],
                               start=True, stop=True)
                        i.then_inc(pe_done, 1)
                        did(f"yp {l} {pair}", f"yp {l} {pair} {j}")

            def latents(l, streams):
                sp = span(streams)
                eng.wait_ge(*loaded[f"mla {l}"])
                for k in range(KQ):
                    o = bank(f"cqT {l} {k}")
                    for t in tiles_of(streams):
                        eng.wait_ge(dve_done, after(f"cqn {l} {t}"))
                        i = nc.tensor.transpose(o[:, P * t:P * t + P], Bm[:, t, 256 + P * k:256 + P * k + P], ident[:, :])
                    i.then_inc(pe_done, 1)
                    did(f"cqT {l} {k}")
                for k in range(KKV):
                    o = bank(f"ckvT {l} {k}")
                    for t in range(NT):
                        eng.wait_ge(dve_done, after(f"ckvn {l} {t}"))
                        i = nc.tensor.transpose(o[:, P * t:P * t + P], Bm[:, t, 640 + P * k:640 + P * k + P], ident[:, :])
                    i.then_inc(pe_done, 1)
                    did(f"ckvT {l} {k}")
                o = bank(f"kpT {l}")
                for t in range(NT):
                    eng.wait_ge(dve_done, after(f"kpe {l}"))
                    i = nc.tensor.transpose(o[0:ROPE, P * t:P * t + P], Bm[:, t, 896:896 + ROPE], ident[:, :])
                i.then_inc(pe_done, 1)
                did(f"kpT {l}")
                for k in range(KQ):
                    eng.wait_ge(act_done, after(f"cqTs {l} {k}"))
                for h in range(HEADS):
                    o = bank(f"q {l} {h}")
                    for k in range(KQ):
                        i = mm(o[:, sp], wuq[:, k, h, :], cqT[:, k, sp], start=k == 0, stop=k == KQ - 1)
                    i.then_inc(pe_done, 1)
                    did(f"q {l} {h}")
                for k in range(KKV):
                    eng.wait_ge(act_done, after(f"ckvTs {l} {k}"))
                for pr in range(4):
                    o = bank(f"k {l} {pr}")
                    for k in range(KKV):
                        i = mm(o, wukv[:, k, P * pr:P * pr + P], ckvT[:, k, :], start=k == 0, stop=k == KKV - 1)
                    i.then_inc(pe_done, 1)
                    did(f"k {l} {pr}")
                for t in range(NT):
                    o = bank(f"v {l} {t}")
                    for k in range(KKV):
                        i = mm(o, ckvT[:, k, P * t:P * t + P], wukv[:, k, 512:1024], start=k == 0, stop=k == KKV - 1)
                    i.then_inc(pe_done, 1)
                    did(f"v {l} {t}")

            def attention(l, streams):
                units = [(t, h) for t in tiles_of(streams) for h in range(HEADS)]

                def score(n):
                    t, h = units[n]
                    eng.wait_ge(dve_done, after(f"qTs {l} {h}"))
                    eng.wait_ge(act_done, after(f"KTs {l}"))
                    nk = 256 if t < 2 else 512
                    o = bank(f"s {l} {n}", n % 3)
                    mm(o[:, 0:nk], qT[0:96, h, P * t:P * t + P], KT[0:96, h, 0:nk], start=True, stop=True).then_inc(pe_done, 1)
                    did(f"s {l} {n}")

                def turn_p(n):
                    t, h = units[n]
                    eng.wait_ge(act_done, after(f"p {l} {n}"))
                    o = bank(f"pT {l} {n}", 3 + n % 3)
                    for b in range(2 if t < 2 else 4):
                        i = nc.tensor.transpose(o[:, P * b:P * b + P], prob[:, n % 2, P * b:P * b + P], ident[:, :])
                    i.then_inc(pe_done, 1)
                    did(f"pT {l} {n}")

                def pv(n):
                    t, h = units[n]
                    eng.wait_ge(dve_done, after(f"pTs {l} {n}"))
                    eng.wait_ge(act_done, after(f"Vs {l}"))
                    if h == 0:
                        state["pv"] = bank(f"pv {l} {t}", 6 + t % 2)
                    o = state["pv"]
                    nb = 2 if t < 2 else 4
                    for b in range(nb):
                        i = mm(o[:, VD * h:VD * h + VD], probT[:, n % 2, P * b:P * b + P], V[:, b, VD * h:VD * h + VD],
                               start=b == 0, stop=b == nb - 1)
                    i.then_inc(pe_done, 1)
                    did(f"pvn {l} {n}", *([f"pv {l} {t}"] if h == HEADS - 1 else []))

                score(0)
                for n in range(len(units)):
                    if n + 1 < len(units):
                        score(n + 1)
                    turn_p(n)
                    if n:
                        pv(n - 1)
                pv(len(units) - 1)
                for k in range(4):
                    o = bank(f"aT {l} {k}")
                    for t in tiles_of(streams):
                        eng.wait_ge(dve_done, after(f"att {l} {t}"))
                        i = nc.tensor.transpose(o[:, P * t:P * t + P], att[:, t, P * k:P * k + P], ident[:, :])
                    i.then_inc(pe_done, 1)
                    did(f"aT {l} {k}")

            def gates(l, w, s):
                for half in range(2):
                    eng.wait_ge(dve_done, after(f"diag {l} {w} {s}"))
                    o = bank(f"gate {l} {w} {s} {half}")
                    for j in range(4):
                        k = 4 * half + j
                        dg = diag if w == 0 else fdiag
                        i = mm(o[:, P * j:P * j + P], ones[:, :], dg[:, k, :], start=True, stop=True)
                    i.then_inc(pe_done, 1)
                    did(f"gate {l} {w} {s} {half}")

            def project_out(l, streams):
                for s in streams:
                    gates(l, 0, s)
                for k in range(KD):
                    eng.wait_ge(dve_done, after(f"mix {l} {k}"))
                ts = tiles_of(streams)
                for n in range(2):
                    os = {t: bank(f"o {l} {n} {t}") for t in ts}
                    for half in range(2):
                        g = gindex[("out", l, 2 * n + half, 0)]
                        hi, lo = granule(g)
                        for t in ts:
                            for k in range(4):
                                kk, s = 4 * half + k, slice(512 * k, 512 * k + 512)
                                i = split3(os[t], hT_hi[:, kk, P * t:P * t + P], hT_lo[:, kk, P * t:P * t + P],
                                           hi[:, s], lo[:, s], kk == 0, kk == 7)
                            if half:
                                i.then_inc(pe_done, 1)
                                did(f"o {l} {n} {t}")
                        if half:
                            did.name(f"used {g}")
                        else:
                            i.then_inc(pe_done, 1)
                            did(f"used {g}")

            def feed_forward(name, g0, stream):
                y = {(tt, n): bank(f"y {name} {tt} {n}", 4 + 2 * tt + n) for tt in range(2) for n in range(2)}

                def gate_up(s, half, os):
                    g = g0 + fpos[("gu", s, half)]
                    hi, lo = granule(g)
                    for tt in range(2):
                        t = 2 * stream + tt
                        for k in range(4):
                            kk, cs = 4 * half + k, slice(512 * k, 512 * k + 512)
                            i = split3(os[tt], hT_hi[:, kk, P * t:P * t + P], hT_lo[:, kk, P * t:P * t + P],
                                       hi[:, cs], lo[:, cs], kk == 0, kk == 7)
                        if half:
                            i.then_inc(pe_done, 1)
                            did(f"gu {name} {s} {tt}")
                    if half:
                        did.name(f"used {g}")
                    else:
                        i.then_inc(pe_done, 1)
                        did(f"used {g}")

                def turn_h(s):
                    o = bank(f"hh {name} {s}", 2)
                    for tt in range(2):
                        eng.wait_ge(dve_done, after(f"h {name} {s} {tt}"))
                        for f in range(2):
                            i = nc.tensor.transpose(o[:, 256 * f + P * tt:256 * f + P * tt + P],
                                                    hh[:, tt, P * f:P * f + P], ident[:, :])
                    i.then_inc(pe_done, 1)
                    did(f"hh {name} {s}")

                def down(s):
                    g = g0 + fpos[("d", s, 0)]
                    hi, lo = granule(g)
                    eng.wait_ge(dve_done, after(f"fs {name} {s}"))
                    for f in range(2):
                        for tt in range(2):
                            a = slice(256 * f + P * tt, 256 * f + P * tt + P)
                            for n in range(2):
                                cs = slice(1024 * f + 512 * n, 1024 * f + 512 * n + 512)
                                i = split3(y[(tt, n)], f_hi[:, a], f_lo[:, a], hi[:, cs], lo[:, cs],
                                           s == 0 and f == 0, s == FC - 1 and f == 1)
                    i.then_inc(pe_done, 1)
                    did(f"used {g}", f"down {name} {s}")

                for s in range(FC):
                    os = [bank(f"gu {name} {s} {tt}", tt) for tt in range(2)]
                    gate_up(s, 0, os)
                    if s:
                        turn_h(s - 1)
                    gate_up(s, 1, os)
                    if s:
                        down(s - 1)
                turn_h(FC - 1)
                down(FC - 1)

            def route():
                eng.wait_ge(dve_done, after("router split"))
                for k in range(KD):
                    eng.wait_ge(dve_done, after(f"hT 1 2 {k}"))
                o = bank("logits")
                for tt in range(2):
                    t = 2 + tt
                    for k in range(KD):
                        a = slice(P * t, P * t + P)
                        q = o[:, NE * tt:NE * tt + NE]
                        split3(q, hT_hi[:, k, a], hT_lo[:, k, a], r_hi[:, k, :], r_lo[:, k, :], k == 0, False)
                        i = mm(q, hT_lo[:, k, a], r_lo[:, k, :], start=False, stop=k == 7)
                i.then_inc(pe_done, 1)
                did("logits")

            eng.wait_ge(*loaded["start"])
            g = 0
            for l in range(DEPTH):
                streams = layer_streams[l]
                modulation(l)
                filters(l)
                norm_turn(l, 1, (0, 1))
                project_in(l, streams)
                hyena(l, streams)
                pooling(l, streams)
                latents(l, streams)
                attention(l, streams)
                project_out(l, streams)
                norm_turn(l, 2, streams)
                for k in range(KD):
                    eng.wait_ge(dve_done, after(f"hT {l} 2 {k}"))
                if l == 0:
                    for s in (0, 1):
                        feed_forward(f"f{s}", gindex[("ffn", 0, 0, s)], s)
                    for s in (0, 1):
                        gates(l, 1, s)
                else:
                    route()
                    for e in range(NE):
                        feed_forward(f"m{e}", gindex[("moe", e, 0, 0)], 1)
                    gates(l, 1, 1)

        @blk.scalar
        def _(eng):
            did = Steps(table, "act")
            act = nc.scalar.activation
            split = {"next": 0}

            def upto(g):
                while split["next"] <= min(g, NG - 1):
                    n = split["next"]
                    w = width(plan[n][0])
                    if n >= RING:
                        eng.wait_ge(pe_done, after(f"used {n - RING}"))
                    eng.wait_ge(raw_full[n % RING], 16 * (n // RING + 1))
                    nc.scalar.copy(w_hi[:, n % RING, 0:w], raw[:, n % RING, 0:w]).then_inc(act_done, 1)
                    did(f"hi {n}")
                    split["next"] += 1


            def modulation(l):
                if l == 0:
                    eng.wait_ge(*loaded["start"])
                    act(csil[:, :, :], cvec[:, :, :], ACT.Silu).then_inc(act_done, 1)
                    did("csil")
                    eng.wait_ge(act_done, did.count)
                if l:
                    eng.wait_ge(dve_done, after("layer 0"))
                eng.wait_ge(dve_done, after(f"cs0 {l}"))
                nc.scalar.copy(hT_hi[:, :, 0:2], csil[:, :, :]).then_inc(act_done, 1)
                did(f"cshi {l}")
                for n in range(12):
                    upto(gindex[("ada", l, 2 * n + 1, 0)])
                    eng.wait_ge(pe_done, after(f"ada {l} {n}"))
                    o = bank_of(f"ada {l} {n}")
                    if n >= 2:
                        eng.wait_ge(pe_done, after(f"modT {l} {n - 2}"))
                    nc.scalar.copy(row4[:, n % 2, :], o[0:4, :]).then_inc(act_done, 1)
                    did(f"row {l} {n}", f"read ada {l} {n}")

            def filters(l):
                for i in (1, 2):
                    eng.wait_ge(dve_done, after(f"arg{i} {l}"))
                    act(farg[0:FH, i - 1, :], fsc[0:FH, 0, :], ACT.Sin).then_inc(act_done, 1)
                    did(f"sin{i} {l}")
                eng.wait_ge(dve_done, after(f"hfil {l}"))
                for t in range(2):
                    act(fsc[:, t, :], hfil[:, t, 0:L], ACT.Abs).then_inc(act_done, 1)
                    did(f"abs {l} {t}")
                    act(farg[:, t, :], hfil[:, t, L:2 * L], ACT.Abs).then_inc(act_done, 1)
                    did(f"abs {l} {t}")
                for ft in range(2):
                    eng.wait_ge(pe_done, after(f"fA {l} {ft}"))
                    o = bank_of(f"fA {l} {ft}")
                    nc.scalar.copy(HA[:, ft, :], o[:, 0:L]).then_inc(act_done, 1)
                    did()
                    nc.scalar.copy(HBs[:, ft, :], o[:, L:2 * L]).then_inc(act_done, 1)
                    did(f"read fA {l} {ft}")
                eng.wait_ge(pe_done, after(f"fD {l}"))
                o = bank_of(f"fD {l}")
                nc.scalar.copy(HD0, o[:, 0:L]).then_inc(act_done, 1)
                did(f"read fD {l}", f"H {l}")

            def norm(l, w, streams):
                eng.wait_ge(dve_done, after(f"ss {l} {w}"))
                ts = tiles_of(streams)
                a, b = ts[0], ts[-1] + 1
                act(small[:, 8 + a:8 + b], small[:, a:b], ACT.Sqrt, bias=epsb[:, 0:1], scale=1.0 / D).then_inc(act_done, 1)
                did(f"std {l} {w}")
                for k in range(KD):
                    eng.wait_ge(pe_done, after(f"nT {l} {w} {k}"))
                    o = bank_of(f"nT {l} {w} {k}")
                    if k == 0:
                        eng.wait_ge(dve_done, after(f"gs {l}"))
                    for s in streams:
                        q = slice(256 * s, 256 * s + 256)
                        j = 3 * (w - 1)
                        act(hT_hi[:, k, q], o[:, q], ACT.Identity, bias=mod[:, 8 * j + k, s:s + 1],
                                 scale=gsc[:, w - 1, k, s:s + 1]).then_inc(act_done, 1)
                        did(f"hThi {l} {w} {k}")

            def project_in(l, streams):
                sp = span(streams)
                for ct in range(6):
                    upto(gindex[("ina", l, ct // 2, 0)])
                    eng.wait_ge(pe_done, after(f"u {l} {ct}"))
                    o = bank_of(f"u {l} {ct}")
                    if ct == 0:
                        eng.wait_ge(dve_done, after(f"upad {l}"))
                    if ct >= 2:
                        eng.wait_ge(dve_done, after(f"conv {l} {ct - 2}"))
                    for s in streams:
                        nc.scalar.copy(upad[:, ct % 2, s, 1:257], o[:, 256 * s:256 * s + 256]).then_inc(act_done, 1)
                        did(f"us {l} {ct}", f"read u {l} {ct}")
                for b in range(2):
                    upto(gindex[("inb", l, 2 * b + 1, 0)])
                    for t in (tiles_of(streams) if b == 0 else range(NT)):
                        eng.wait_ge(pe_done, after(f"B {l} {b} {t}"))
                        o = bank_of(f"B {l} {b} {t}")
                        nc.scalar.copy(Bm[:, t, HB * b:HB * b + HB], o[:, 0:HB]).then_inc(act_done, 1)
                        did(f"Bs {l} {b} {t}", f"read B {l} {b} {t}")

            def hyena(l, streams):
                sp = span(streams)
                for ct in range(2):
                    eng.wait_ge(pe_done, after(f"zT {l} {ct}"))
                    o = bank_of(f"zT {l} {ct}")
                    for s in streams:
                        for t in range(2):
                            nc.scalar.copy(zT[:, t, 256 * s + P * ct:256 * s + P * ct + P],
                                                o[:, 256 * s + P * t:256 * s + P * t + P]).then_inc(act_done, 1)
                            did(f"zTs {l} {ct}", f"read zT {l} {ct}")
                for ct in range(2):
                    eng.wait_ge(dve_done, after(f"yh {l} {ct}"))
                    nc.scalar.copy(hT_hi[:, ct, sp], ytmp[:, ct, sp]).then_inc(act_done, 1)
                    did(f"mixhi {l} {ct}")

            def pooling(l, streams):
                sp = span(streams)
                for g in range(4):
                    eng.wait_ge(pe_done, after(f"d {l} {g}"))
                    o = bank_of(f"d {l} {g}")
                    if g >= 2:
                        eng.wait_ge(pe_done, after(f"yp {l} {(g - 2) // 2} {g % 2}"))
                    nc.scalar.copy(dT[0:GROUP, g % 2, sp], o[0:GROUP, sp]).then_inc(act_done, 1)
                    did(f"dT {l} {g}", f"read d {l} {g}")
                for pair in range(2):
                    eng.wait_ge(pe_done, after(f"yp {l} {pair}"))
                    o = bank_of(f"yp {l} {pair}")
                    a = PAR["psc"][0] + pair
                    act(hT_hi[:, 2 + pair, sp], o[:, sp], ACT.Copy, scale=par[:, l, a:a + 1]).then_inc(act_done, 1)
                    did(f"mixhi {l} {2 + pair}")

            def latents(l, streams):
                sp = span(streams)
                eng.wait_ge(dve_done, after(f"ssq {l}"))
                act(small[:, 24:28], small[:, 16:20], ACT.Sqrt, bias=epsb[:, 0:1], scale=1.0 / QL).then_inc(act_done, 1)
                did()
                act(small[:, 28:32], small[:, 20:24], ACT.Sqrt, bias=epsb[:, 0:1], scale=1.0 / KVL).then_inc(act_done, 1)
                did(f"stdq {l}")
                for k in range(KQ):
                    eng.wait_ge(pe_done, after(f"cqT {l} {k}"))
                    o = bank_of(f"cqT {l} {k}")
                    a = PAR["qg"][0] + k
                    act(cqT[:, k, sp], o[:, sp], ACT.Copy, scale=par[:, l, a:a + 1]).then_inc(act_done, 1)
                    did(f"cqTs {l} {k}", f"read cqT {l} {k}")
                for k in range(KKV):
                    eng.wait_ge(pe_done, after(f"ckvT {l} {k}"))
                    o = bank_of(f"ckvT {l} {k}")
                    a = PAR["kvg"][0] + k
                    act(ckvT[:, k, :], o, ACT.Copy, scale=par[:, l, a:a + 1]).then_inc(act_done, 1)
                    did(f"ckvTs {l} {k}", f"read ckvT {l} {k}")
                eng.wait_ge(pe_done, after(f"kpT {l}"))
                o = bank_of(f"kpT {l}")
                for h in range(HEADS):
                    nc.scalar.copy(KT[64:96, h, :], o[0:ROPE, :]).then_inc(act_done, 1)
                    did(f"KTpe {l}", f"read kpT {l}")
                for pr in range(4):
                    eng.wait_ge(pe_done, after(f"k {l} {pr}"))
                    o = bank_of(f"k {l} {pr}")
                    for j in range(2):
                        nc.scalar.copy(KT[0:64, 2 * pr + j, :], o[64 * j:64 * j + 64, :]).then_inc(act_done, 1)
                        did(f"KTs {l}", f"read k {l} {pr}")
                for t in range(NT):
                    eng.wait_ge(pe_done, after(f"v {l} {t}"))
                    o = bank_of(f"v {l} {t}")
                    nc.scalar.copy(V[:, t, :], o).then_inc(act_done, 1)
                    did(f"Vs {l}", f"read v {l} {t}")

            def attention(l, streams):
                units = [(t, h) for t in tiles_of(streams) for h in range(HEADS)]
                for n, (t, h) in enumerate(units):
                    nk = 256 if t < 2 else 512
                    eng.wait_ge(pe_done, after(f"s {l} {n}"))
                    o = bank_of(f"s {l} {n}")
                    eng.wait_ge(dve_done, after(f"nmax {l} {n}"))
                    if n >= 2:
                        eng.wait_ge(pe_done, after(f"pT {l} {n - 2}"))
                    if n == 0:
                        eng.wait_ge(pe_done, after(f"q {l} {HEADS - 1}"))
                    act(prob[:, n % 2, 0:nk], o[:, 0:nk], ACT.Exp, bias=small[:, 64 + n:65 + n], scale=SM_SCALE,
                             accum_out=small[:, 128 + n:129 + n]).then_inc(act_done, 1)
                    did(f"p {l} {n}", f"read s {l} {n}")
                for k in range(4):
                    eng.wait_ge(pe_done, after(f"aT {l} {k}"))
                    o = bank_of(f"aT {l} {k}")
                    sp = span(streams)
                    nc.scalar.copy(hT_hi[:, 4 + k, sp], o[:, sp]).then_inc(act_done, 1)
                    did(f"mixhi {l} {4 + k}")

            def gates(l, w, s):
                for half in range(2):
                    eng.wait_ge(pe_done, after(f"gate {l} {w} {s} {half}"))
                    o = bank_of(f"gate {l} {w} {s} {half}")
                    dst = gbc[:, s, 512 * half:512 * half + 512] if w == 0 else gbf[:, 512 * half:512 * half + 512]
                    if w == 1 and s == 1 and l == 0:
                        eng.wait_ge(dve_done, after(f"res {l} 1 0"))
                    nc.scalar.copy(dst, o).then_inc(act_done, 1)
                    did(f"gb {l} {w} {s}", f"read gate {l} {w} {s} {half}")

            def project_out(l, streams):
                for s in streams:
                    gates(l, 0, s)
                upto(gindex[("out", l, 3, 0)])

            def feed_forward(name, g0):
                upto(g0 + 2)
                for s in range(FC):
                    if s:
                        eng.wait_ge(pe_done, after(f"hh {name} {s - 1}"))
                        o = bank_of(f"hh {name} {s - 1}")
                        if s > 1:
                            eng.wait_ge(pe_done, after(f"down {name} {s - 2}"))
                        nc.scalar.copy(f_hi[:, :], o).then_inc(act_done, 1)
                        did(f"fhi {name} {s - 1}")
                    if s + 1 < FC:
                        upto(g0 + fpos[("gu", s + 1, 1)])
                    for tt in range(2):
                        eng.wait_ge(pe_done, after(f"gu {name} {s} {tt}"))
                        o = bank_of(f"gu {name} {s} {tt}")
                        act(sg[:, tt, :], o[:, 0:256], ACT.Silu).then_inc(act_done, 1)
                        did(f"sg {name} {s} {tt}")
                    upto(g0 + fpos[("d", s, 0)])
                eng.wait_ge(pe_done, after(f"hh {name} {FC - 1}"))
                o = bank_of(f"hh {name} {FC - 1}")
                eng.wait_ge(pe_done, after(f"down {name} {FC - 2}"))
                nc.scalar.copy(f_hi[:, :], o).then_inc(act_done, 1)
                did(f"fhi {name} {FC - 1}")

            epsb = small[:, 250:251]
            for l in range(DEPTH):
                streams = layer_streams[l]
                if l == 0:
                    eng.wait_ge(dve_done, after("eps"))
                modulation(l)
                filters(l)
                norm(l, 1, (0, 1))
                project_in(l, streams)
                hyena(l, streams)
                pooling(l, streams)
                latents(l, streams)
                attention(l, streams)
                project_out(l, streams)
                norm(l, 2, streams)
                if l == 0:
                    for s in (0, 1):
                        feed_forward(f"f{s}", gindex[("ffn", 0, 0, s)])
                    for s in (0, 1):
                        gates(l, 1, s)
                else:
                    nc.scalar.copy(r_hi[:, :, :], router[:, :, :]).then_inc(act_done, 1)
                    did("rhi")
                    eng.wait_ge(dve_done, after("dlogit"))
                    act(small[:, 40:42], small[:, 38:40], ACT.Exp).then_inc(act_done, 1)
                    did("elogit")
                    for e in range(NE):
                        feed_forward(f"m{e}", gindex[("moe", e, 0, 0)])
                    gates(l, 1, 1)
            eng.wait_ge(dve_done, after("ssf"))
            act(small[:, 36:38], small[:, 34:36], ACT.Sqrt, bias=epsb[:, 0:1], scale=1.0 / D).then_inc(act_done, 1)
            did("stdf")

        @blk.vector
        def _(eng):
            did = Steps(table, "dve")
            v = nc.vector
            split = {"next": 0}

            def upto(g):
                while split["next"] <= min(g, NG - 1):
                    n = split["next"]
                    w = width(plan[n][0])
                    eng.wait_ge(act_done, after(f"hi {n}"))
                    v.tensor_tensor(w_lo[:, n % RING, 0:w], raw[:, n % RING, 0:w],
                                         w_hi[:, n % RING, 0:w].bitcast(F32), ALU.subtract).then_inc(dve_done, 1)
                    did(f"lo {n}")
                    split["next"] += 1



            def modulation(l):
                if l == 0:
                    v.memset(small[:, :], 0.0).then_inc(dve_done, 1)
                    eng.wait_ge(dve_done, did())
                    v.memset(small[:, 250:251], EPS).then_inc(dve_done, 1)
                    did("eps")
                if l:
                    eng.wait_ge(pe_done, after("used %d" % (gindex[("ffn", 0, 0, 1)] + 3 * FC - 1)))
                v.memset(hT_hi[:, :, 0:P].bitcast(F32), 0.0).then_inc(dve_done, 1)
                did(f"cs0 {l}")
                eng.wait_ge(act_done, after(f"cshi {l}"))
                eng.wait_ge(*loaded["start"])
                eng.wait_ge(act_done, after("csil"))
                v.tensor_tensor(hT_hi[:, :, 2:4], csil[:, :, :], hT_hi[:, :, 0:2].bitcast(F32), ALU.subtract).then_inc(dve_done, 1)
                did(f"cs {l}")
                b = PAR["bada"][0]
                for n in range(12):
                    upto(gindex[("ada", l, 2 * n + 1, 0)])
                    if n:
                        bias_mod(l, n - 1)
                bias_mod(l, 11)
                eng.wait_ge(dve_done, did.count)
                for w in range(2):
                    g0 = PAR["g1"][0] + KD * w
                    j = 3 * w + 1
                    for s in range(2):
                        v.scalar_tensor_tensor(out=gsc[:, w, :, s], in0=mod[:, 8 * j:8 * j + 8, s], scalar=1.0,
                                                    in1=par[:, l, g0:g0 + KD], op0=ALU.add, op1=ALU.mult).then_inc(dve_done, 1)
                        did(f"gs {l}")

            def bias_mod(l, n):
                eng.wait_ge(pe_done, after(f"modT {l} {n}"))
                o = bank_of(f"modT {l} {n}")
                b = PAR["bada"][0] + 4 * n
                for s in range(2):
                    q = o[:, 0:8].rearrange("p (j s) -> p j s", s=2)
                    v.tensor_tensor(mod[:, 4 * n:4 * n + 4, s], q[:, :, s], par[:, l, b:b + 4], ALU.add).then_inc(dve_done, 1)
                    did(f"read modT {l} {n}")

            def filters(l):
                for i, nm in ((1, "f1"), (2, "f2")):
                    eng.wait_ge(pe_done, after(f"{nm} {l}"))
                    o = bank_of(f"{nm} {l}")[0:FH, 0:L]
                    b, f = PAR[f"b{i}"][0], PAR[f"f{i}"][0]
                    ar, rt = fsc[0:FH, 0, :], fsc[0:FH, 1, :]
                    v.tensor_scalar(ar, o, par[0:FH, l, b:b + 1], par[0:FH, l, f:f + 1], ALU.add, ALU.mult).then_inc(dve_done, 1)
                    eng.wait_ge(dve_done, did(f"read {nm} {l}"))
                    v.tensor_scalar(rt, ar, 1 / (2 * math.pi), ROUND, ALU.mult, ALU.add).then_inc(dve_done, 1)
                    eng.wait_ge(dve_done, did())
                    v.tensor_scalar(rt, rt, ROUND, None, ALU.subtract).then_inc(dve_done, 1)
                    eng.wait_ge(dve_done, did())
                    v.scalar_tensor_tensor(out=ar, in0=rt, scalar=-TWO_PI_A, in1=ar, op0=ALU.mult, op1=ALU.add).then_inc(dve_done, 1)
                    eng.wait_ge(dve_done, did())
                    v.scalar_tensor_tensor(out=ar, in0=rt, scalar=-TWO_PI_B, in1=ar, op0=ALU.mult, op1=ALU.add).then_inc(dve_done, 1)
                    eng.wait_ge(dve_done, did())
                    v.tensor_scalar(ar, ar, 3.1415925, -3.1415925, ALU.min, ALU.max).then_inc(dve_done, 1)
                    eng.wait_ge(dve_done, did(f"arg{i} {l}"))
                eng.wait_ge(act_done, after(f"sin2 {l}"))
                for t in range(2):
                    eng.wait_ge(pe_done, after(f"f3 {l} {t}"))
                    o = bank_of(f"f3 {l} {t}")
                    v.tensor_tensor(hfil[:, t, :], o, decay[:, t, :], ALU.mult).then_inc(dve_done, 1)
                    eng.wait_ge(dve_done, did(f"read f3 {l} {t}", f"hfil {l}"))
                    v.tensor_tensor(hp[:, t, :], hfil[:, t, 0:L], hfil[:, t, L:2 * L], ALU.add).then_inc(dve_done, 1)
                    did()
                    v.tensor_tensor(hm[:, t, :], hfil[:, t, 0:L], hfil[:, t, L:2 * L], ALU.subtract).then_inc(dve_done, 1)
                    did()
                eng.wait_ge(act_done, after(f"abs {l} 1"))
                for t in range(2):
                    v.tensor_tensor(fsc[:, t, :], fsc[:, t, :], farg[:, t, :], ALU.add).then_inc(dve_done, 1)
                    did(f"habs {l}")
                eng.wait_ge(pe_done, after(f"fn {l}"))
                o = bank_of(f"fn {l}")
                v.reciprocal(small[:, 32:34], o[:, 0:2]).then_inc(dve_done, 1)
                eng.wait_ge(dve_done, did(f"read fn {l}", f"rn {l}"))

            def norm(l, w, streams):
                ts = tiles_of(streams)
                if w == 1:
                    eng.wait_ge(pe_done, after(f"fn {l}"))
                for t in ts:
                    v.tensor_tensor_reduce(xn[:, t, :], X[:, t, :], X[:, t, :], 1.0, 0.0, ALU.mult, ALU.add,
                                                small[:, t:t + 1]).then_inc(dve_done, 1)
                    did(f"ss {l} {w}")
                a, b = ts[0], ts[-1] + 1
                eng.wait_ge(act_done, after(f"std {l} {w}"))
                v.reciprocal(small[:, 12:12 + b - a], small[:, 8 + a:8 + b]).then_inc(dve_done, 1)
                eng.wait_ge(dve_done, did())
                for t in ts:
                    v.tensor_scalar(xn[:, t, :], X[:, t, :], small[:, 12 + t - a:13 + t - a], None, ALU.mult).then_inc(dve_done, 1)
                    did(f"xn {l} {w} {t}")
                for k in range(KD):
                    eng.wait_ge(act_done, after(f"hThi {l} {w} {k}"))
                    eng.wait_ge(pe_done, after(f"nT {l} {w} {k}"))
                    o = bank_of(f"nT {l} {w} {k}")
                    j = 3 * (w - 1)
                    for s in streams:
                        q = slice(256 * s, 256 * s + 256)
                        v.tensor_scalar(tn[:, k % 2, q], o[:, q], gsc[:, w - 1, k, s:s + 1],
                                             mod[:, 8 * j + k, s:s + 1], ALU.mult, ALU.add).then_inc(dve_done, 1)
                        did(f"read nT {l} {w} {k}")
                    eng.wait_ge(dve_done, did.count)
                    q = span(streams)
                    v.tensor_tensor(hT_lo[:, k, q], tn[:, k % 2, q], hT_hi[:, k, q].bitcast(F32), ALU.subtract).then_inc(dve_done, 1)
                    did(f"hT {l} {w} {k}")

            def project_in(l, streams):
                for b in range(2):
                    for s in streams:
                        v.memset(upad[:, b, s, 0:1], 0.0).then_inc(dve_done, 1)
                        did()
                        v.memset(upad[:, b, s, 257:258], 0.0).then_inc(dve_done, 1)
                        did(f"upad {l}")
                a0, b0 = PAR["sw"][0], PAR["sb"][0]
                for ct in range(6):
                    upto(gindex[("ina", l, ct // 2, 0)])
                    eng.wait_ge(act_done, after(f"us {l} {ct}"))
                    for s in streams:
                        q = uc[:, ct, 256 * s:256 * s + 256]
                        u = lambda j: upad[:, ct % 2, s, j:j + 256]
                        w = lambda j: par[:, l, a0 + 6 * j + ct:a0 + 6 * j + ct + 1]
                        v.tensor_scalar(q, u(0), w(0), None, ALU.mult).then_inc(dve_done, 1)
                        eng.wait_ge(dve_done, did())
                        v.scalar_tensor_tensor(out=q, in0=u(1), scalar=w(1), in1=q, op0=ALU.mult, op1=ALU.add).then_inc(dve_done, 1)
                        eng.wait_ge(dve_done, did())
                        v.scalar_tensor_tensor(out=q, in0=u(2), scalar=w(2), in1=q, op0=ALU.mult, op1=ALU.add).then_inc(dve_done, 1)
                        eng.wait_ge(dve_done, did())
                        v.tensor_scalar(q, q, par[:, l, b0 + ct:b0 + ct + 1], None, ALU.add).then_inc(dve_done, 1)
                        eng.wait_ge(dve_done, did(f"conv {l} {ct}"))
                        if ct >= 4:
                            z = uc[:, ct - 2, 256 * s:256 * s + 256]
                            v.tensor_tensor(z, z, q, ALU.mult).then_inc(dve_done, 1)
                            did(f"z {l} {ct - 4}")
                upto(gindex[("inb", l, 3, 0)])

            def hyena(l, streams):
                sp = span(streams)
                eng.wait_ge(act_done, after(f"H {l}"))
                t1, t2 = ytmp[:, 0, :], ytmp[:, 1, :]
                for ft in range(2):
                    eng.wait_ge(pe_done, after(f"Zs {l} {ft}"))
                    zc, zs = bank_of(f"Zc {l} {ft}"), bank_of(f"Zs {l} {ft}")
                    dd = HD0 if ft == 0 else HA[:, 1, :]
                    for s in streams:
                        q = slice(256 * s, 256 * s + 256)
                        v.tensor_tensor(Yc[:, ft, q], zc[:, q], HA[:, ft, :], ALU.mult).then_inc(dve_done, 1)
                        did()
                        v.tensor_tensor(t1[:, q], zs[:, q], HBs[:, ft, :], ALU.mult).then_inc(dve_done, 1)
                        did()
                        v.tensor_tensor(Ys[:, ft, q], zc[:, q], HBs[:, ft, :], ALU.mult).then_inc(dve_done, 1)
                        did(f"read Zc {l} {ft}")
                        v.tensor_tensor(t2[:, q], zs[:, q], dd, ALU.mult).then_inc(dve_done, 1)
                        eng.wait_ge(dve_done, did(f"read Zs {l} {ft}"))
                    v.tensor_tensor(Yc[:, ft, sp], Yc[:, ft, sp], t1[:, sp], ALU.subtract).then_inc(dve_done, 1)
                    did()
                    v.tensor_tensor(Ys[:, ft, sp], Ys[:, ft, sp], t2[:, sp], ALU.add).then_inc(dve_done, 1)
                    eng.wait_ge(dve_done, did(f"Y {l}"))
                b0 = PAR["hyb"][0]
                for ct in range(2):
                    eng.wait_ge(pe_done, after(f"y {l} {ct}"))
                    o = bank_of(f"y {l} {ct}")
                    y = ytmp[:, ct, sp]
                    z = uc[:, 2 + ct, sp]
                    v.tensor_scalar(z, z, par[:, l, b0 + ct:b0 + ct + 1], None, ALU.mult).then_inc(dve_done, 1)
                    eng.wait_ge(dve_done, did())
                    v.scalar_tensor_tensor(out=y, in0=o[:, sp], scalar=small[:, 32 + ct:33 + ct], in1=z,
                                                op0=ALU.mult, op1=ALU.add).then_inc(dve_done, 1)
                    eng.wait_ge(dve_done, did(f"read y {l} {ct}"))
                    v.tensor_tensor(y, y, uc[:, ct, sp], ALU.mult).then_inc(dve_done, 1)
                    eng.wait_ge(dve_done, did(f"yh {l} {ct}"))
                    eng.wait_ge(act_done, after(f"mixhi {l} {ct}"))
                    v.tensor_tensor(hT_lo[:, ct, sp], y, hT_hi[:, ct, sp].bitcast(F32), ALU.subtract).then_inc(dve_done, 1)
                    did(f"mix {l} {ct}")
                did.name(f"hyena {l}")

            def pooling(l, streams):
                sp = span(streams)
                for pair in range(2):
                    eng.wait_ge(act_done, after(f"mixhi {l} {2 + pair}"))
                    eng.wait_ge(pe_done, after(f"yp {l} {pair}"))
                    o = bank_of(f"yp {l} {pair}")
                    a = PAR["psc"][0] + pair
                    v.scalar_tensor_tensor(out=hT_lo[:, 2 + pair, sp], in0=o[:, sp], scalar=par[:, l, a:a + 1],
                                                in1=hT_hi[:, 2 + pair, sp].bitcast(F32), op0=ALU.mult,
                                                op1=ALU.subtract).then_inc(dve_done, 1)
                    did(f"mix {l} {2 + pair}", f"read yp {l} {pair}")

            def latents(l, streams):
                sp = span(streams)
                eng.wait_ge(*loaded[f"mla {l}"])
                for t in range(NT):
                    eng.wait_ge(act_done, after(f"Bs {l} 1 {t}"))
                    if t in tiles_of(streams):
                        v.tensor_tensor_reduce(junk, Bm[:, t, 256:640], Bm[:, t, 256:640], 1.0, 0.0, ALU.mult,
                                                    ALU.add, small[:, 16 + t:17 + t]).then_inc(dve_done, 1)
                        eng.wait_ge(dve_done, did())
                    v.tensor_tensor_reduce(junk[:, 0:KVL], Bm[:, t, 640:896], Bm[:, t, 640:896], 1.0, 0.0,
                                                ALU.mult, ALU.add, small[:, 20 + t:21 + t]).then_inc(dve_done, 1)
                    eng.wait_ge(dve_done, did(f"ssq {l}"))
                eng.wait_ge(act_done, after(f"stdq {l}"))
                v.reciprocal(small[:, 24:32], small[:, 24:32]).then_inc(dve_done, 1)
                eng.wait_ge(dve_done, did())
                for t in range(NT):
                    if t in tiles_of(streams):
                        v.tensor_scalar(Bm[:, t, 256:640], Bm[:, t, 256:640], small[:, 24 + t:25 + t], None,
                                             ALU.mult).then_inc(dve_done, 1)
                        did(f"cqn {l} {t}")
                    v.tensor_scalar(Bm[:, t, 640:896], Bm[:, t, 640:896], small[:, 28 + t:29 + t], None,
                                         ALU.mult).then_inc(dve_done, 1)
                    did(f"ckvn {l} {t}")
                for j in range(2):
                    k1, k2 = Bm[:, 2 + j, 896:928], Bm[:, 2 + j, 928:960]
                    v.tensor_tensor(k1, k1, ropek[:, j, 0:32], ALU.mult).then_inc(dve_done, 1)
                    did()
                    v.tensor_tensor(k2, k2, ropek[:, j, 32:64], ALU.mult).then_inc(dve_done, 1)
                    eng.wait_ge(dve_done, did())
                    v.tensor_tensor(k1, k1, k2, ALU.add).then_inc(dve_done, 1)
                    did(f"kpe {l}")
                for h in range(HEADS):
                    eng.wait_ge(pe_done, after(f"q {l} {h}"))
                    o = bank_of(f"q {l} {h}")
                    if 0 in streams:
                        v.tensor_copy(qT[0:96, h, 0:256], o[0:96, 0:256]).then_inc(dve_done, 1)
                        did()
                    q = slice(256, 512)
                    v.tensor_copy(qT[0:64, h, q], o[0:64, q]).then_inc(dve_done, 1)
                    did()
                    v.tensor_tensor(qT[64:96, h, q], o[64:96, q], ropeq[64:96, 0:256], ALU.mult).then_inc(dve_done, 1)
                    did()
                    v.tensor_tensor(qtmp[64:96, :], o[96:128, q], ropeq[96:128, 256:512], ALU.mult).then_inc(dve_done, 1)
                    eng.wait_ge(dve_done, did(f"read q {l} {h}"))
                    v.tensor_tensor(qT[64:96, h, q], qT[64:96, h, q], qtmp[64:96, :], ALU.add).then_inc(dve_done, 1)
                    eng.wait_ge(dve_done, did(f"qTs {l} {h}"))

            def attention(l, streams):
                units = [(t, h) for t in tiles_of(streams) for h in range(HEADS)]
                N = len(units)

                def copy_p(n):
                    eng.wait_ge(pe_done, after(f"pT {l} {n}"))
                    o = bank_of(f"pT {l} {n}")
                    nk = 256 if units[n][0] < 2 else 512
                    if n >= 2:
                        eng.wait_ge(pe_done, after(f"pvn {l} {n - 2}"))
                    v.tensor_copy(probT[:, n % 2, 0:nk], o[:, 0:nk]).then_inc(dve_done, 1)
                    did(f"pTs {l} {n}", f"read pT {l} {n}")

                def finish(t):
                    eng.wait_ge(pe_done, after(f"pv {l} {t}"))
                    o = bank_of(f"pv {l} {t}")
                    n0 = units.index((t, 0))
                    v.reciprocal(small[:, 192:200], small[:, 128 + n0:136 + n0]).then_inc(dve_done, 1)
                    eng.wait_ge(dve_done, did())
                    for h in range(HEADS):
                        v.tensor_scalar(att[:, t, VD * h:VD * h + VD], o[:, VD * h:VD * h + VD],
                                             small[:, 192 + h:193 + h], None, ALU.mult).then_inc(dve_done, 1)
                        did(f"att {l} {t}", f"read pv {l} {t}")

                for n in range(N + 2):
                    if n < N:
                        t, h = units[n]
                        nk = 256 if t < 2 else 512
                        eng.wait_ge(pe_done, after(f"s {l} {n}"))
                        o = bank_of(f"s {l} {n}")
                        v.reduce_max(small[:, 64 + n:65 + n], o[:, 0:nk], AX.X).then_inc(dve_done, 1)
                        eng.wait_ge(dve_done, did())
                        v.tensor_scalar(small[:, 64 + n:65 + n], small[:, 64 + n:65 + n], -SM_SCALE, None, ALU.mult).then_inc(dve_done, 1)
                        did(f"nmax {l} {n}")
                    if 1 <= n <= N:
                        copy_p(n - 1)
                    if n >= 2 and units[n - 2][1] == HEADS - 1:
                        finish(units[n - 2][0])
                sp = span(streams)
                for k in range(4):
                    eng.wait_ge(act_done, after(f"mixhi {l} {4 + k}"))
                    eng.wait_ge(pe_done, after(f"aT {l} {k}"))
                    o = bank_of(f"aT {l} {k}")
                    v.tensor_tensor(hT_lo[:, 4 + k, sp], o[:, sp], hT_hi[:, 4 + k, sp].bitcast(F32),
                                         ALU.subtract).then_inc(dve_done, 1)
                    did(f"mix {l} {4 + k}", f"read aT {l} {k}")

            def diagonal(l, w, s):
                dg = diag if w == 0 else fdiag
                j = 16 if w == 0 else 40
                for k in range(KD):
                    v.tensor_scalar(dg[:, k, :], ident[:, :], mod[:, j + k, s:s + 1], None, ALU.mult).then_inc(dve_done, 1)
                    did(f"diag {l} {w} {s}")

            def project_out(l, streams):
                for s in streams:
                    if s == 1 and 0 in streams:
                        eng.wait_ge(pe_done, after(f"gate {l} 0 0 1"))
                    diagonal(l, 0, s)
                upto(gindex[("out", l, 3, 0)])
                eng.wait_ge(act_done, after(f"gb {l} 0 {streams[-1]}"))
                for n in range(2):
                    for j, t in enumerate(tiles_of(streams)):
                        eng.wait_ge(pe_done, after(f"o {l} {n} {t}"))
                        o = bank_of(f"o {l} {n} {t}")
                        q = slice(512 * n, 512 * n + 512)
                        v.tensor_tensor(rtmp[:, j % 2, :], o, gbc[:, t // 2, q], ALU.mult).then_inc(dve_done, 1)
                        eng.wait_ge(dve_done, did(f"read o {l} {n} {t}"))
                        v.tensor_tensor(X[:, t, q], X[:, t, q], rtmp[:, j % 2, :], ALU.add).then_inc(dve_done, 1)
                        did()
                eng.wait_ge(dve_done, did.count)

            def feed_forward(name, g0):
                def turned(s):
                    eng.wait_ge(act_done, after(f"fhi {name} {s}"))
                    eng.wait_ge(pe_done, after(f"hh {name} {s}"))
                    o = bank_of(f"hh {name} {s}")
                    v.tensor_tensor(f_lo[:, :], o, f_hi[:, :].bitcast(F32), ALU.subtract).then_inc(dve_done, 1)
                    did(f"fs {name} {s}", f"read hh {name} {s}")

                upto(g0 + 2)
                for s in range(FC):
                    if s:
                        turned(s - 1)
                    if s + 1 < FC:
                        upto(g0 + fpos[("gu", s + 1, 1)])
                    for tt in range(2):
                        eng.wait_ge(act_done, after(f"sg {name} {s} {tt}"))
                        eng.wait_ge(pe_done, after(f"gu {name} {s} {tt}"))
                        o = bank_of(f"gu {name} {s} {tt}")
                        v.tensor_tensor(hh[:, tt, :], o[:, 256:512], sg[:, tt, :], ALU.mult).then_inc(dve_done, 1)
                        did(f"h {name} {s} {tt}", f"read gu {name} {s} {tt}")
                    upto(g0 + fpos[("d", s, 0)])
                turned(FC - 1)

            def choose():
                eng.wait_ge(act_done, after("rhi"))
                v.tensor_tensor(r_lo[:, :, :], router[:, :, :], r_hi[:, :, :].bitcast(F32), ALU.subtract).then_inc(dve_done, 1)
                did("router split")
                eng.wait_ge(pe_done, after("logits"))
                o = bank_of("logits")
                lg = small[:, 204:220]
                v.tensor_copy(lg, o[:, 0:16]).then_inc(dve_done, 1)
                eng.wait_ge(dve_done, did("read logits"))
                for tt in range(2):
                    v.max(small[:, 220:228], lg[:, 8 * tt:8 * tt + 8]).then_inc(dve_done, 1)
                    eng.wait_ge(dve_done, did())
                    v.max_index(idx8[:, :], small[:, 220:228], lg[:, 8 * tt:8 * tt + 8]).then_inc(dve_done, 1)
                    eng.wait_ge(dve_done, did())
                    v.tensor_copy(small[:, 42 + 2 * tt:44 + 2 * tt], idx8[:, 0:2]).then_inc(dve_done, 1)
                    eng.wait_ge(dve_done, did())
                    v.tensor_tensor(small[:, 38 + tt:39 + tt], small[:, 221:222], small[:, 220:221],
                                         ALU.subtract).then_inc(dve_done, 1)
                    eng.wait_ge(dve_done, did("dlogit"))
                eng.wait_ge(act_done, after("elogit"))
                v.tensor_scalar(small[:, 46:48], small[:, 40:42], 1.0, None, ALU.add).then_inc(dve_done, 1)
                eng.wait_ge(dve_done, did())
                v.reciprocal(small[:, 46:48], small[:, 46:48]).then_inc(dve_done, 1)
                eng.wait_ge(dve_done, did())
                v.tensor_tensor(small[:, 48:50], small[:, 40:42], small[:, 46:48], ALU.mult).then_inc(dve_done, 1)
                eng.wait_ge(dve_done, did())
                for tt in range(2):
                    v.tensor_scalar(comb[:, tt, :], iota8[:, :], small[:, 42 + 2 * tt:43 + 2 * tt],
                                         small[:, 46 + tt:47 + tt], ALU.is_equal, ALU.mult).then_inc(dve_done, 1)
                    eng.wait_ge(dve_done, did())
                    v.tensor_scalar(small[:, 228:236], iota8[:, :], small[:, 43 + 2 * tt:44 + 2 * tt],
                                         small[:, 48 + tt:49 + tt], ALU.is_equal, ALU.mult).then_inc(dve_done, 1)
                    eng.wait_ge(dve_done, did())
                    v.tensor_tensor(comb[:, tt, :], comb[:, tt, :], small[:, 228:236], ALU.add).then_inc(dve_done, 1)
                    eng.wait_ge(dve_done, did())

            def combine(name, e):
                for tt in range(2):
                    for n in range(2):
                        eng.wait_ge(pe_done, after(f"down {name} {FC - 1}"))
                        o = PS[:, 4 + 2 * tt + n, :]
                        a = acc[:, tt, 512 * n:512 * n + 512]
                        if e == 0:
                            ins = v.tensor_scalar(a, o, comb[:, tt, 0:1], None, ALU.mult)
                        else:
                            ins = v.scalar_tensor_tensor(out=a, in0=o, scalar=comb[:, tt, e:e + 1], in1=a,
                                                         op0=ALU.mult, op1=ALU.add)
                        ins.then_inc(dve_done, 1)
                        did(f"read y {name} {tt} {n}")
                eng.wait_ge(dve_done, did.count)

            for l in range(DEPTH):
                streams = layer_streams[l]
                modulation(l)
                filters(l)
                norm(l, 1, (0, 1))
                project_in(l, streams)
                hyena(l, streams)
                pooling(l, streams)
                latents(l, streams)
                attention(l, streams)
                project_out(l, streams)
                norm(l, 2, streams)
                if l == 0:
                    for s in (0, 1):
                        feed_forward(f"f{s}", gindex[("ffn", 0, 0, s)])
                        if s == 0:
                            diagonal(l, 1, 0)
                        for tt in range(2):
                            for n in range(2):
                                eng.wait_ge(pe_done, after(f"down f{s} {FC - 1}"))
                                dst = (acc if s == 0 else acc2)[:, tt, 512 * n:512 * n + 512]
                                v.tensor_copy(dst, PS[:, 4 + 2 * tt + n, :]).then_inc(dve_done, 1)
                                did(f"read y f{s} {tt} {n}")
                    for s in (0, 1):
                        if s == 1:
                            eng.wait_ge(pe_done, after(f"gate {l} 1 0 1"))
                            diagonal(l, 1, 1)
                        eng.wait_ge(act_done, after(f"gb {l} 1 {s}"))
                        eng.wait_ge(dve_done, did.count)
                        src = acc if s == 0 else acc2
                        for tt in range(2):
                            v.tensor_tensor(src[:, tt, :], src[:, tt, :], gbf, ALU.mult).then_inc(dve_done, 1)
                            eng.wait_ge(dve_done, did())
                            v.tensor_tensor(X[:, 2 * s + tt, :], X[:, 2 * s + tt, :], src[:, tt, :], ALU.add).then_inc(dve_done, 1)
                            eng.wait_ge(dve_done, did())
                        did.name(f"res {l} 1 {s}")
                    did.name("layer 0")
                else:
                    choose()
                    diagonal(l, 1, 1)
                    for e in range(NE):
                        feed_forward(f"m{e}", gindex[("moe", e, 0, 0)])
                        combine(f"m{e}", e)
                    eng.wait_ge(act_done, after(f"gb {l} 1 1"))
                    for tt in range(2):
                        v.tensor_tensor(acc[:, tt, :], acc[:, tt, :], gbf, ALU.mult).then_inc(dve_done, 1)
                        eng.wait_ge(dve_done, did())
                        v.tensor_tensor(X[:, 2 + tt, :], X[:, 2 + tt, :], acc[:, tt, :], ALU.add).then_inc(dve_done, 1)
                        eng.wait_ge(dve_done, did())
            for tt in range(2):
                v.tensor_tensor_reduce(acc[:, tt, :], X[:, 2 + tt, :], X[:, 2 + tt, :], 1.0, 0.0, ALU.mult,
                                            ALU.add, small[:, 34 + tt:35 + tt]).then_inc(dve_done, 1)
                eng.wait_ge(dve_done, did("ssf"))
            eng.wait_ge(act_done, after("stdf"))
            v.reciprocal(small[:, 36:38], small[:, 36:38]).then_inc(dve_done, 1)
            eng.wait_ge(dve_done, did())
            eng.wait_ge(*loaded["final"])
            for tt in range(2):
                v.tensor_scalar(acc[:, tt, :], X[:, 2 + tt, :], small[:, 36 + tt:37 + tt], None, ALU.mult).then_inc(dve_done, 1)
                eng.wait_ge(dve_done, did())
                v.tensor_tensor(acc[:, tt, :], acc[:, tt, :], fing, ALU.mult).then_inc(dve_done, 1)
                eng.wait_ge(dve_done, did(f"out {tt}"))

        @blk.sync
        def _(eng):
            for g, (kind, e, i) in enumerate(plan):
                w = width(kind)
                if g >= RING:
                    eng.wait_ge(dve_done, after(f"lo {g - RING}"))
                eng.dma_start(raw[:, g % RING, 0:w], source(kind, e, i)).then_inc(raw_full[g % RING], 16)
            stored = loaded["stored"][0]
            for tt in range(2):
                eng.wait_ge(dve_done, after(f"out {tt}"))
                eng.dma_start(io["y"][P * tt:P * tt + P, :], acc[:, tt, :]).then_inc(stored, 16)
            eng.wait_ge(stored, 32)

        @blk.gpsimd
        def _(eng):
            def load(name, *pairs):
                s = loaded[name][0]
                for dst, src in pairs:
                    eng.dma_start(dst, src).then_inc(s, 16)
                assert loaded[name][1] == 16 * len(pairs)

            load("start", *((X[:, t, :], io["x"][P * t:P * t + P, :]) for t in range(NT)),
                 (par[:, :, :], io["par"]), (ident[:, :], io["ident"]), (ones[:, :], io["ones"]), (sel[:, :], io["sel"]),
                 (cvec[:, :, :], io["cvec"]), (router[:, :, :], io["router"]), (iota8[:, :], io["iota8"]))
            for l in range(DEPTH):
                if l:
                    eng.wait_ge(dve_done, after("layer 0"))
                load(f"hy {l}", (hyc, io["hyc"]), (fw, io["fw"][l]))
                eng.wait_ge(dve_done, after(f"hyena {l}"))
                eng.wait_ge(pe_done, after(f"y {l} 1"))
                eng.wait_ge(pe_done, after(f"zT {l} 1"))
                eng.wait_ge(act_done, after(f"mixhi {l} 1"))
                load(f"pool {l}", (A(0, 2048), io["pm"]), (pwts[0:GROUP], io["pw"][l]))
                load(f"mla {l}", (A(7936, 3072), io["wuq"][l]), (A(11008, 2048), io["wukv"][l]), (A(19712, 512), io["ropeq"]),
                     (A(20224, 128), io["ropek"]))
            eng.wait_ge(pe_done, after("down m0 0"))
            load("final", (fing, io["fing"]))



def lay(inputs):
    f = lambda n: np.asarray(inputs[n])
    c = np.ascontiguousarray
    io = {}
    io["x"] = c(np.concatenate([f("ctx")[0], f("x")[0]], axis=0))
    io["cvec"] = c(np.stack([f("c_ctx"), f("c")[0]], axis=-1).reshape(KD, P, 2).transpose(1, 0, 2))
    io["ada"] = c(f("w_ada").reshape(DEPTH, 2, 4, P, 12, 512).transpose(0, 4, 1, 3, 2, 5).reshape(DEPTH, 24, P, GRAN))
    w_in = f("w_in")
    io["ina"] = c(w_in[:, :, :3 * HY].reshape(DEPTH, KD, P, 3, 256).transpose(0, 3, 2, 1, 4).reshape(DEPTH, 3, P, GRAN))
    a = w_in.shape[2] - ROPE
    inb = np.concatenate([w_in[:, :, 3 * HY:], w_in[:, :, a + ROPE // 2:], w_in[:, :, a:a + ROPE // 2]], axis=2)
    io["inb"] = c(inb.reshape(DEPTH, 2, 4, P, 2, HB).transpose(0, 4, 1, 3, 2, 5).reshape(DEPTH, 4, P, 4 * HB))
    io["out"] = c(f("w_out").reshape(DEPTH, 2, 4, P, 2, 512).transpose(0, 4, 1, 3, 2, 5).reshape(DEPTH, 4, P, GRAN))

    def swiglu(wg, wu, wd):
        n = wg.shape[0]
        out = np.empty((n, 3 * FC, P, GRAN), wg.dtype)
        gu = out.reshape(n, 3 * FC, P, 4, 2, 256)
        g6, u6 = (w.reshape(n, 2, 4, P, FC, 256) for w in (wg, wu))
        d5 = wd.reshape(n, FC, 2, P, D)
        for i, (kind, s, half) in enumerate(ffn_order()):
            if kind == "gu":
                gu[:, i, :, :, 0, :] = g6[:, half, :, :, s, :].transpose(0, 2, 1, 3)
                gu[:, i, :, :, 1, :] = u6[:, half, :, :, s, :].transpose(0, 2, 1, 3)
            else:
                out[:, i] = d5[:, s].transpose(0, 2, 1, 3).reshape(n, P, GRAN)
        return out

    io["ffn"] = swiglu(f("ffn_wg"), f("ffn_wu"), f("ffn_wd"))
    io["moe"] = swiglu(f("moe_wg")[0], f("moe_wu")[0], f("moe_wd")[0])
    io["router"] = c(f("moe_router")[0].reshape(KD, P, NE).transpose(1, 0, 2))
    par = np.zeros((P, DEPTH, NPAR), np.float32)

    def put(name, a):
        lo, hi = PAR[name]
        par[:a.shape[-1], :, lo:hi] = a.reshape(DEPTH, hi - lo, a.shape[-1]).transpose(2, 0, 1)

    for name, src in (("g1", "norm1_g"), ("g2", "norm2_g"), ("bada", "b_ada"), ("qg", "q_norm_g"), ("kvg", "kv_norm_g"),
                      ("sw", "hy_short_w"), ("sb", "hy_short_b"), ("hyb", "hy_bias"), ("psc", "pool_scale")):
        put(name, f(src).reshape(DEPTH, -1, P))
    for name, src in (("b1", "filt_b1"), ("f1", "filt_freq1"), ("b2", "filt_b2"), ("f2", "filt_freq2")):
        put(name, f(src).reshape(DEPTH, 1, FH))
    io["par"] = par
    uq = f("w_uq").reshape(DEPTH, KQ, P, HEADS, NOPE + ROPE)
    uq = np.concatenate([uq, uq[..., NOPE + ROPE // 2:], uq[..., NOPE:NOPE + ROPE // 2]], axis=-1)
    io["wuq"] = c(uq.transpose(0, 2, 1, 3, 4).reshape(DEPTH, P, KQ * HEADS * P))
    ukv = f("w_ukv").reshape(DEPTH, KKV, P, HEADS, 2, NOPE)
    io["wukv"] = c(ukv.transpose(0, 2, 1, 4, 3, 5).reshape(DEPTH, P, KKV * 1024))
    io["pw"] = c(f("pool_w").transpose(0, 2, 1, 3))
    fw = np.zeros((DEPTH, P, 640), np.float32)
    fw[:, :FE, 0:64] = f("filt_w1")
    fw[:, :FH, 64:128] = f("filt_w2")
    fw[:, :FH, 128:640] = f("filt_w3")
    io["fw"] = fw
    io["fing"] = c(np.broadcast_to(f("final_g"), (P, D)))

    t = np.arange(L)
    fr = np.arange(L)
    sign = (-1.0) ** t
    ang = 2 * np.pi * ((np.outer(t, fr)) % (2 * L)) / (2 * L)
    C, S = np.cos(ang), np.sin(ang)
    Sn, Cn = S.copy(), C.copy()
    Sn[:, 0], Cn[:, 0] = sign, sign
    wt = np.full(L, 2.0 / (2 * L))
    wt[0] = 1.0 / (2 * L)
    tiles = lambda m: m.reshape(2, P, -1).transpose(1, 0, 2).reshape(P, -1)
    tt = (t / (L - 1)).astype(np.float32)
    deltas = np.linspace(math.log(1e-2) / 1.5, math.log(1e-2) / 0.3, HY)
    dec = np.exp(-tt[:, None].astype(np.float64) * np.abs(deltas))
    dec2 = np.concatenate([dec, dec], axis=1)
    dec2[0, HY:] = 0.0
    bands = (FE - 1) // 2
    w = 2.0 * math.pi * t[:, None] / L
    fb = np.linspace(1e-4, bands - 1, bands)[None, :]
    feat = np.concatenate([tt[:, None], np.cos(fb * w), -np.sin(fb * w)], axis=1)
    featT = np.zeros((P, L))
    featT[:FE] = feat.T
    io["hyc"] = np.concatenate([tiles(C), tiles(Sn), tiles(S[:, :P]), tiles(Cn[:, :P]), tiles((C * wt).T),
                                tiles((Sn * wt).T), tiles(dec2), featT], axis=1).astype(np.float32)
    pm = np.zeros((4, L, L))
    for g, win in enumerate(WINDOWS):
        for i in range(L):
            lo, hi = max(i - win // 2, 0), min(i + win // 2, L)
            pm[g, lo:hi, i] = 1.0 / (hi - lo)
            pm[g, i, i] -= 1.0
    io["pm"] = np.stack([tiles(m) for m in pm], axis=1).reshape(P, 4 * 2 * L).astype(np.float32)
    nf = ROPE // 4
    inv = 1.0 / (10000.0 ** (np.arange(nf) / nf))
    an = np.concatenate([(t // 64)[:, None] * inv, (t % 64)[:, None] * inv], axis=1)
    co, si = np.cos(an), np.sin(an)
    COS, SIN = np.concatenate([co, co], 1), np.concatenate([-si, si], 1)
    rq = np.zeros((P, 512), np.float32)
    rq[64:96, 0:256] = COS.T
    rq[96:128, 256:512] = SIN.T
    io["ropeq"] = rq
    io["ropek"] = np.concatenate([COS, SIN], axis=1).reshape(2, P, 64).transpose(1, 0, 2).astype(np.float32)
    io["ident"] = np.eye(P, dtype=np.float32)
    io["ones"] = np.ones((P, P), np.float32)
    io["sel"] = np.array([[1, 0], [0, 1], [1, 0], [0, 1]], np.float32)
    io["iota8"] = c(np.broadcast_to(np.arange(NE, dtype=np.float32), (P, NE)))
    return {k: c(v) for k, v in io.items()}


def kernel(**inputs):
    import concourse.bacc as _bacc
    from concourse.bass_utils import run_bass_kernel_spmd as _run

    data = lay(inputs)
    table = {"count": {}, "bank": {}, "final": False}
    for final in (False, True):
        nc = _bacc.Bacc("TRN2", target_bir_lowering=False, num_devices=1)
        io = {k: nc.dram_tensor(f"in_{k}", v.shape, F32, kind="ExternalInput").ap() for k, v in data.items()}
        io["y"] = nc.dram_tensor("out_y", (L, D), F32, kind="ExternalOutput").ap()
        build(nc, io, table)
        table["final"] = True
    r = _run(nc, [{f"in_{k}": v for k, v in data.items()}], core_ids=[0])
    return r.results[0]["out_y"].reshape(1, L, D)
```

```python
import math
from contextlib import ExitStack

import concourse.bass as bass
import numpy as np
from concourse import mybir

F32 = mybir.dt.float32
F32R = mybir.dt.float32r
U32 = mybir.dt.uint32
I32 = mybir.dt.int32
ALU = mybir.AluOpType
ACT = mybir.ActivationFunctionType
AX = mybir.AxisListType

P = 128
D = 1024
L = 256
DEPTH = 2
KD = D // P
NT = 4
HY = 256
POOLW = 256
WINDOWS = (2, 4, 8, 16)
GROUP = 64
HEADS = 8
NOPE, ROPE, VD = 64, 32, 64
QL, KVL = 384, 256
KQ, KKV = QL // P, KVL // P
SM_SCALE = (NOPE + ROPE) ** -0.5
INB = POOLW + QL + KVL + 2 * ROPE
HB = INB // 2
EPS = 1e-6
FF = 2816
NE = 8
FC = FF // 256
FH = 64
FE = 33
GRAN = 2048
RING = 3
XRING = 2 * RING
SLOTS = NE + 3
COLS = SLOTS + 1
TWO_PI_A = 6.28125
TWO_PI_B = 2 * math.pi - TWO_PI_A
ROUND = 1.5 * 2 ** 23

PAR = {}
_at = 0
for _n, _w in (("g1", KD), ("g2", KD), ("bada", 48), ("qg", KQ), ("kvg", KKV), ("sw", 18), ("sb", 6), ("hyb", 2),
               ("psc", 2), ("b1", 1), ("f1", 1), ("b2", 1), ("f2", 1)):
    PAR[_n] = (_at, _at + _w)
    _at += _w
NPAR = _at


def stream_plan():
    plan = []
    for l in range(DEPTH):
        plan += [("ada", l, i) for i in range(24)]
        plan += [("ina", l, i) for i in range(3)]
        plan += [("inb", l, i) for i in range(4)]
        plan += [("out", l, i) for i in range(4)]
        if l == 0:
            plan += 2 * [("ffn", 0, i) for i in range(3 * FC)]
    return plan


def ffn_order():
    order = []
    for s in range(FC):
        order += [("gu", s, 0), ("gu", s, 1)]
        if s:
            order.append(("d", s - 1, 0))
    return order + [("d", FC - 1, 0)]


class Steps:

    def __init__(self, table, key):
        self.table, self.key, self.count = table, key, 0

    def __call__(self, *names):
        self.count += 1
        for n in names:
            self.name(n)
        return self.count

    def name(self, n):
        if not self.table["final"]:
            self.table["count"][n] = (self.key, self.count)


def build(nc, io, table):
    with ExitStack() as ctx:
        def sb(name, shape, dt=F32):
            return ctx.enter_context(nc.sbuf_tensor(name, shape, dt))

        X = sb("X", [P, NT, D])
        hT_hi = sb("hT_hi", [P, KD, 512], F32R)
        hT_lo = sb("hT_lo", [P, KD, 512], F32R)
        raw = sb("raw", [P, RING, GRAN])
        w_hi = sb("w_hi", [P, RING, GRAN], F32R)
        w_lo = sb("w_lo", [P, RING, GRAN], F32R)
        f_hi = sb("f_hi", [P, 512], F32R)
        f_lo = sb("f_lo", [P, 512], F32R)
        par = sb("par", [P, DEPTH, NPAR])
        ident = sb("ident", [P, P])
        ones = sb("ones", [P, P])
        sel = sb("sel", [4, 2])
        cvec = sb("cvec", [P, KD, 2])
        csil = sb("csil", [P, KD, 2])
        mod = sb("mod", [P, 48, 2])
        gsc = sb("gsc", [P, 2, KD, 2])
        small = sb("small", [P, 256])
        r_hi = sb("r_hi", [P, KD, NE], F32R)
        r_lo = sb("r_lo", [P, KD, NE], F32R)
        iota8 = sb("iota8", [P, NE])
        idx8 = sb("idx8", [P, NE], U32)
        comb = sb("comb", [P, 2, NE])
        pick = f_hi[:, 256:512].rearrange("p (t c) -> p t c", c=P)
        expert_i = sb("expert_i", [1, COLS], I32)
        second = sb("second", [1, 1], I32)
        NA = 20352
        arena = sb("arena", [P, NA])
        PS = ctx.enter_context(nc.psum_tensor("PS", [P, 8, 512], F32))

        def sem(name):
            return ctx.enter_context(nc.semaphore(name))

        pe_done, act_done, dve_done = sem("pe_done"), sem("act_done"), sem("dve_done")
        raw_full = [sem(f"raw_full{i}") for i in range(RING)]
        loaded = {"start": (sem("start_loaded"), 16 * 10), "route": (sem("route_tables_loaded"), 64),
                "stored": (sem("stored"), 32)}
        for l in range(DEPTH):
            loaded[f"hy {l}"] = (sem(f"hyena_tables_loaded{l}"), 32)
            loaded[f"pool {l}"] = (sem(f"pool_tables_loaded{l}"), 32)
            loaded[f"mla {l}"] = (sem(f"attention_weights_loaded{l}"), 64)

        x_hi, x_lo, x_used = sem("x_hi"), sem("x_lo"), sem("x_used")
        x_silu, x_h = sem("x_silu"), sem("x_h")
        x_turned, x_thi, x_tlo = sem("x_turned"), sem("x_turned_hi"), sem("x_turned_lo")
        x_pick, x_gather = sem("x_pick"), sem("x_gather")
        x_gt = sem("x_gathered_modulated")
        x_ghi, x_glo = sem("x_gathered_hi"), sem("x_gathered_lo")
        x_pickT, x_pickTs = sem("x_pickT"), sem("x_pickT_saved")
        x_y, x_z, x_add = sem("x_y_saved"), sem("x_spread"), sem("x_added")
        NGR = 3 * FC
        x_full = [sem(f"x_full{i}") for i in range(XRING)]

        def after(name):
            return table["count"].get(name, (None, 1))[1]

        def reader_of(job):
            return act_done if table["count"].get("read " + job, ("act", 1))[0] == "act" else dve_done

        def bank_of(job):
            return PS[:, table["bank"][job], :]

        def A(off, *shape):
            n = int(np.prod(shape))
            assert off + n <= NA
            v = arena[:, off:off + n]
            if len(shape) == 1:
                return v
            letters = "abcd"[:len(shape)]
            kw = {c: s for c, s in zip(letters[1:], shape[1:])}
            return v.rearrange(f"p ({' '.join(letters)}) -> p {' '.join(letters)}", **kw)

        xn = A(0, NT, D)
        tn = A(4096, 2, 512)
        Bm = A(4096, NT, INB)
        uc = A(7936, 6, 512)
        upad = A(11008, 2, 2, 258)
        hyc = A(12040, 3840)
        Cf = A(12040, 2, 256)
        Sf = A(12552, 2, 256)
        Sz0 = A(13064, 2, 128)
        Cn0 = A(13320, 2, 128)
        IC = A(13576, 2, 256)
        IS = A(14088, 2, 256)
        decay = A(14600, 2, 512)
        featT = A(15624, 256)
        fw = A(15880, 640)
        fw1, fw2, fw3 = A(15880, 64), A(15944, 64), A(16008, 512)
        hfil = A(16520, 2, 512)
        hp, hm = A(17544, 2, 256), A(18056, 2, 256)
        HA, HBs = A(18568, 2, 256), A(19080, 2, 256)
        HD0 = A(19592, 256)
        farg = A(0, 2, 256)
        fsc = A(512, 2, 256)
        zT = A(0, 2, 512)
        Yc, Ys = A(1024, 2, 512), A(2048, 2, 512)
        ytmp = A(3072, 2, 512)
        pm = A(0, 4, 2, 256)
        dT = A(2048, 2, 512)
        junk = A(3072, QL)
        pwts = A(3456, 4, GROUP)
        row4 = arena[0:4, 11008:12032].rearrange("p (a b) -> p a b", b=512)
        wuq = A(7936, KQ, HEADS, P)
        wukv = A(11008, KKV, 1024)
        cqT = A(13056, KQ, 512)
        ckvT = A(14592, KKV, 512)
        qT = A(15616, HEADS, 512)
        ropeq = A(19712, 512)
        ropek = A(20224, 2, 64)
        KT = A(0, HEADS, 512)
        V = A(4096, NT, 512)
        qtmp = A(6144, 256)
        att = A(7936, NT, 512)
        prob = A(9984, 2, 512)
        probT = A(11008, 2, 512)
        gbc = A(12032, 2, D)
        diag = A(14080, 8, P)
        rtmp = A(15104, 2, 512)
        sg = A(4096, 2, 256)
        hh = A(4608, 2, 256)
        acc = A(5120, 2, D)
        gbf = A(7168, D)
        fdiag = A(8192, 8, P)
        ftmp = A(9216, 2, 512)
        ysb = A(9216, D)
        pickT = A(10240, 2, 256)
        rt = A(11264, 64)
        comb_s, place_s, expert_f = A(11328, 2, COLS), A(11352, 2, COLS), A(11376, COLS)
        gt = A(11520, 4, P)
        iota = A(16384, P)
        before = A(16512, P)
        fing = A(16640, D)
        router = A(17664, KD, NE)
        more_raw = [A(12032, GRAN), A(14080, GRAN), A(17728, GRAN)]

        def x_raw(n):
            n = n % XRING
            return raw[:, n, :] if n < RING else more_raw[n - RING]

        acc2 = A(10240, 2, D)

        plan = stream_plan()
        gindex = {}
        counts = {}
        for g, (kind, e, i) in enumerate(plan):
            n = counts.get((kind, e, i), 0)
            counts[(kind, e, i)] = n + 1
            gindex[(kind, e, i, n)] = g
        NG = len(plan)
        order = ffn_order()
        fpos = {x: i for i, x in enumerate(order)}

        def width(kind):
            return 4 * HB if kind == "inb" else GRAN

        def source(kind, e, i):
            return io[kind][e, i]

        blk = ctx.enter_context(nc.Block())
        layer_streams = {0: (0, 1), 1: (1,)}

        def tiles_of(streams):
            return [2 * s + j for s in streams for j in range(2)]

        def span(streams):
            return slice(256 * streams[0], 512)

        @blk.tensor
        def _(eng):
            did = Steps(table, "pe")
            state = {"next": 0, "last": [None] * 8}

            def bank(job, b=None):
                if b is None:
                    b = state["next"]
                    state["next"] = (b + 1) % 8
                if state["last"][b]:
                    eng.wait_ge(reader_of(state["last"][b]), after("read " + state["last"][b]))
                state["last"][b] = job
                table["bank"][job] = b
                return PS[:, b, :]

            mm = nc.tensor.matmul

            def granule(g):
                eng.wait_ge(dve_done, after(f"lo {g}"))
                return w_hi[:, g % RING, :], w_lo[:, g % RING, :]

            def split3(out, s_hi, s_lo, m_hi, m_lo, start, stop):
                mm(out, s_hi, m_hi, start=start, stop=False)
                mm(out, s_hi, m_lo, start=False, stop=False)
                return mm(out, s_lo, m_hi, start=False, stop=stop)

            def modulation(l):
                eng.wait_ge(dve_done, after(f"cs {l}"))
                for n in range(12):
                    o = bank(f"ada {l} {n}")
                    for half in range(2):
                        g = gindex[("ada", l, 2 * n + half, 0)]
                        hi, lo = granule(g)
                        for k in range(4):
                            kk = 4 * half + k
                            mm(o, hT_hi[:, kk, 0:P], hi[:, 512 * k:512 * k + 512], start=kk == 0, stop=False)
                            i = mm(o, hT_hi[:, kk, 0:P], lo[:, 512 * k:512 * k + 512], start=False, stop=kk == 7)
                        i.then_inc(pe_done, 1)
                        did(f"used {g}", f"ada {l} {n}")
                    if n:
                        turn(l, n - 1)
                turn(l, 11)

            def turn(l, n):
                eng.wait_ge(act_done, after(f"row {l} {n}"))
                o = bank(f"modT {l} {n}")
                for j in range(4):
                    i = mm(o[:, 2 * j:2 * j + 2], row4[:, n % 2, P * j:P * j + P], sel[:, :], start=True, stop=True)
                i.then_inc(pe_done, 1)
                did(f"modT {l} {n}")

            def filters(l):
                eng.wait_ge(*loaded[f"hy {l}"])
                mm(bank(f"f1 {l}")[0:FH, 0:L], fw1[0:FE, :], featT[0:FE, :], start=True, stop=True).then_inc(pe_done, 1)
                did(f"f1 {l}")
                eng.wait_ge(act_done, after(f"sin1 {l}"))
                mm(bank(f"f2 {l}")[0:FH, 0:L], fw2[0:FH, :], farg[0:FH, 0, :], start=True, stop=True).then_inc(pe_done, 1)
                did(f"f2 {l}")
                eng.wait_ge(act_done, after(f"sin2 {l}"))
                for t in range(2):
                    mm(bank(f"f3 {l} {t}"), farg[0:FH, 1, P * t:P * t + P], fw3[0:FH, :], start=True, stop=True).then_inc(pe_done, 1)
                    did(f"f3 {l} {t}")
                eng.wait_ge(dve_done, after(f"habs {l}"))
                o = bank(f"fn {l}")
                for ct in range(2):
                    for t in range(2):
                        i = mm(o[:, ct:ct + 1], fsc[:, t, P * ct:P * ct + P], ones[:, 0:1], start=t == 0, stop=t == 1)
                i.then_inc(pe_done, 1)
                did(f"fn {l}")
                for ft in range(2):
                    s = slice(P * ft, P * ft + P)
                    o = bank(f"fA {l} {ft}")
                    for t in range(2):
                        mm(o[:, 0:L], Cf[:, t, s], hp[:, t, :], start=t == 0, stop=t == 1)
                    for t in range(2):
                        basis = Sz0[:, t, :] if ft == 0 else Sf[:, t, s]
                        i = mm(o[:, L:2 * L], basis, hm[:, t, :], start=t == 0, stop=t == 1)
                    i.then_inc(pe_done, 1)
                    did(f"fA {l} {ft}")
                o = bank(f"fD {l}")
                for t in range(2):
                    i = mm(o[:, 0:L], Cn0[:, t, :], hp[:, t, :], start=t == 0, stop=t == 1)
                i.then_inc(pe_done, 1)
                did(f"fD {l}")

            def norm_turn(l, w, streams):
                for k in range(KD):
                    for t in tiles_of(streams):
                        eng.wait_ge(dve_done, after(f"xn {l} {w} {t}"))
                    o = bank(f"nT {l} {w} {k}")
                    for t in tiles_of(streams):
                        i = nc.tensor.transpose(o[:, P * t:P * t + P], xn[:, t, P * k:P * k + P], ident[:, :])
                    i.then_inc(pe_done, 1)
                    did(f"nT {l} {w} {k}")

            def project_in(l, streams):
                sp = span(streams)
                for ct in range(6):
                    g = gindex[("ina", l, ct // 2, 0)]
                    hi, lo = granule(g)
                    o = bank(f"u {l} {ct}")
                    for k in range(KD):
                        if ct == 0:
                            eng.wait_ge(dve_done, after(f"hT {l} 1 {k}"))
                        s = slice(256 * k + P * (ct % 2), 256 * k + P * (ct % 2) + P)
                        i = split3(o[:, sp], hi[:, s], lo[:, s], hT_hi[:, k, sp], hT_lo[:, k, sp], k == 0, k == 7)
                    i.then_inc(pe_done, 1)
                    did(f"u {l} {ct}", f"used {g}")
                for b in range(2):
                    ts = tiles_of(streams) if b == 0 else range(NT)
                    os = {t: bank(f"B {l} {b} {t}") for t in ts}
                    for half in range(2):
                        g = gindex[("inb", l, 2 * b + half, 0)]
                        hi, lo = granule(g)
                        for t in ts:
                            for k in range(4):
                                kk, s = 4 * half + k, slice(HB * k, HB * k + HB)
                                i = split3(os[t][:, 0:HB], hT_hi[:, kk, P * t:P * t + P], hT_lo[:, kk, P * t:P * t + P],
                                           hi[:, s], lo[:, s], kk == 0, kk == 7)
                            if half:
                                i.then_inc(pe_done, 1)
                                did(f"B {l} {b} {t}")
                        if half:
                            did.name(f"used {g}")
                        else:
                            i.then_inc(pe_done, 1)
                            did(f"used {g}")

            def hyena(l, streams):
                sp = span(streams)
                n = 256 * len(streams)
                for ct in range(2):
                    eng.wait_ge(dve_done, after(f"z {l} {ct}"))
                    o = bank(f"zT {l} {ct}")
                    for j, s in enumerate(streams):
                        for t in range(2):
                            i = nc.tensor.transpose(o[:, 256 * s + P * t:256 * s + P * t + P],
                                                    uc[:, 2 + ct, 256 * s + P * t:256 * s + P * t + P], ident[:, :])
                    i.then_inc(pe_done, 1)
                    did(f"zT {l} {ct}")
                for ft in range(2):
                    for nm, basis in (("c", Cf), ("s", Sf)):
                        eng.wait_ge(act_done, after(f"zTs {l} 0"))
                        eng.wait_ge(act_done, after(f"zTs {l} 1"))
                        o = bank(f"Z{nm} {l} {ft}")
                        for t in range(2):
                            i = mm(o[:, sp], basis[:, t, P * ft:P * ft + P], zT[:, t, sp], start=t == 0, stop=t == 1)
                        i.then_inc(pe_done, 1)
                        did(f"Z{nm} {l} {ft}")
                eng.wait_ge(dve_done, after(f"Y {l}"))
                for ct in range(2):
                    o = bank(f"y {l} {ct}")
                    for s in streams:
                        for ft in range(2):
                            a = slice(256 * s + P * ct, 256 * s + P * ct + P)
                            mm(o[:, 256 * s:256 * s + 256], Yc[:, ft, a], IC[:, ft, :], start=ft == 0, stop=False)
                            i = mm(o[:, 256 * s:256 * s + 256], Ys[:, ft, a], IS[:, ft, :], start=False, stop=ft == 1)
                    i.then_inc(pe_done, 1)
                    did(f"y {l} {ct}")

            def pooling(l, streams):
                eng.wait_ge(*loaded[f"pool {l}"])
                sp = span(streams)
                for t in tiles_of(streams):
                    eng.wait_ge(act_done, after(f"Bs {l} 0 {t}"))
                for g in range(4):
                    o = bank(f"d {l} {g}")
                    for s in streams:
                        for t in range(2):
                            i = mm(o[0:GROUP, 256 * s:256 * s + 256], Bm[:, 2 * s + t, GROUP * g:GROUP * g + GROUP],
                                   pm[:, g, t, :], start=t == 0, stop=t == 1)
                    i.then_inc(pe_done, 1)
                    did(f"d {l} {g}")
                for pair in range(2):
                    o = bank(f"yp {l} {pair}")
                    for j in range(2):
                        g = 2 * pair + j
                        eng.wait_ge(act_done, after(f"dT {l} {g}"))
                        i = mm(o[GROUP * j:GROUP * j + GROUP, sp], pwts[0:GROUP, g, :], dT[0:GROUP, g % 2, sp],
                               start=True, stop=True)
                        i.then_inc(pe_done, 1)
                        did(f"yp {l} {pair}", f"yp {l} {pair} {j}")

            def latents(l, streams):
                sp = span(streams)
                eng.wait_ge(*loaded[f"mla {l}"])
                for k in range(KQ):
                    o = bank(f"cqT {l} {k}")
                    for t in tiles_of(streams):
                        eng.wait_ge(dve_done, after(f"cqn {l} {t}"))
                        i = nc.tensor.transpose(o[:, P * t:P * t + P], Bm[:, t, 256 + P * k:256 + P * k + P], ident[:, :])
                    i.then_inc(pe_done, 1)
                    did(f"cqT {l} {k}")
                for k in range(KKV):
                    o = bank(f"ckvT {l} {k}")
                    for t in range(NT):
                        eng.wait_ge(dve_done, after(f"ckvn {l} {t}"))
                        i = nc.tensor.transpose(o[:, P * t:P * t + P], Bm[:, t, 640 + P * k:640 + P * k + P], ident[:, :])
                    i.then_inc(pe_done, 1)
                    did(f"ckvT {l} {k}")
                o = bank(f"kpT {l}")
                for t in range(NT):
                    eng.wait_ge(dve_done, after(f"kpe {l}"))
                    i = nc.tensor.transpose(o[0:ROPE, P * t:P * t + P], Bm[:, t, 896:896 + ROPE], ident[:, :])
                i.then_inc(pe_done, 1)
                did(f"kpT {l}")
                for k in range(KQ):
                    eng.wait_ge(act_done, after(f"cqTs {l} {k}"))
                for h in range(HEADS):
                    o = bank(f"q {l} {h}")
                    for k in range(KQ):
                        i = mm(o[:, sp], wuq[:, k, h, :], cqT[:, k, sp], start=k == 0, stop=k == KQ - 1)
                    i.then_inc(pe_done, 1)
                    did(f"q {l} {h}")
                for k in range(KKV):
                    eng.wait_ge(act_done, after(f"ckvTs {l} {k}"))
                for pr in range(4):
                    o = bank(f"k {l} {pr}")
                    for k in range(KKV):
                        i = mm(o, wukv[:, k, P * pr:P * pr + P], ckvT[:, k, :], start=k == 0, stop=k == KKV - 1)
                    i.then_inc(pe_done, 1)
                    did(f"k {l} {pr}")
                for t in range(NT):
                    o = bank(f"v {l} {t}")
                    for k in range(KKV):
                        i = mm(o, ckvT[:, k, P * t:P * t + P], wukv[:, k, 512:1024], start=k == 0, stop=k == KKV - 1)
                    i.then_inc(pe_done, 1)
                    did(f"v {l} {t}")

            def attention(l, streams):
                units = [(t, h) for t in tiles_of(streams) for h in range(HEADS)]

                def score(n):
                    t, h = units[n]
                    eng.wait_ge(dve_done, after(f"qTs {l} {h}"))
                    eng.wait_ge(act_done, after(f"KTs {l}"))
                    nk = 256 if t < 2 else 512
                    o = bank(f"s {l} {n}", n % 3)
                    mm(o[:, 0:nk], qT[0:96, h, P * t:P * t + P], KT[0:96, h, 0:nk], start=True, stop=True).then_inc(pe_done, 1)
                    did(f"s {l} {n}")

                def turn_p(n):
                    t, h = units[n]
                    eng.wait_ge(act_done, after(f"p {l} {n}"))
                    o = bank(f"pT {l} {n}", 3 + n % 3)
                    for b in range(2 if t < 2 else 4):
                        i = nc.tensor.transpose(o[:, P * b:P * b + P], prob[:, n % 2, P * b:P * b + P], ident[:, :])
                    i.then_inc(pe_done, 1)
                    did(f"pT {l} {n}")

                def pv(n):
                    t, h = units[n]
                    eng.wait_ge(dve_done, after(f"pTs {l} {n}"))
                    eng.wait_ge(act_done, after(f"Vs {l}"))
                    if h == 0:
                        state["pv"] = bank(f"pv {l} {t}", 6 + t % 2)
                    o = state["pv"]
                    nb = 2 if t < 2 else 4
                    for b in range(nb):
                        i = mm(o[:, VD * h:VD * h + VD], probT[:, n % 2, P * b:P * b + P], V[:, b, VD * h:VD * h + VD],
                               start=b == 0, stop=b == nb - 1)
                    i.then_inc(pe_done, 1)
                    did(f"pvn {l} {n}", *([f"pv {l} {t}"] if h == HEADS - 1 else []))

                score(0)
                for n in range(len(units)):
                    if n + 1 < len(units):
                        score(n + 1)
                    turn_p(n)
                    if n:
                        pv(n - 1)
                pv(len(units) - 1)
                for k in range(4):
                    o = bank(f"aT {l} {k}")
                    for t in tiles_of(streams):
                        eng.wait_ge(dve_done, after(f"att {l} {t}"))
                        i = nc.tensor.transpose(o[:, P * t:P * t + P], att[:, t, P * k:P * k + P], ident[:, :])
                    i.then_inc(pe_done, 1)
                    did(f"aT {l} {k}")

            def gates(l, w, s):
                for half in range(2):
                    eng.wait_ge(dve_done, after(f"diag {l} {w} {s}"))
                    o = bank(f"gate {l} {w} {s} {half}")
                    for j in range(4):
                        k = 4 * half + j
                        dg = diag if w == 0 else fdiag
                        i = mm(o[:, P * j:P * j + P], ones[:, :], dg[:, k, :], start=True, stop=True)
                    i.then_inc(pe_done, 1)
                    did(f"gate {l} {w} {s} {half}")

            def project_out(l, streams):
                for s in streams:
                    gates(l, 0, s)
                for k in range(KD):
                    eng.wait_ge(dve_done, after(f"mix {l} {k}"))
                ts = tiles_of(streams)
                for n in range(2):
                    os = {t: bank(f"o {l} {n} {t}") for t in ts}
                    for half in range(2):
                        g = gindex[("out", l, 2 * n + half, 0)]
                        hi, lo = granule(g)
                        for t in ts:
                            for k in range(4):
                                kk, s = 4 * half + k, slice(512 * k, 512 * k + 512)
                                i = split3(os[t], hT_hi[:, kk, P * t:P * t + P], hT_lo[:, kk, P * t:P * t + P],
                                           hi[:, s], lo[:, s], kk == 0, kk == 7)
                            if half:
                                i.then_inc(pe_done, 1)
                                did(f"o {l} {n} {t}")
                        if half:
                            did.name(f"used {g}")
                        else:
                            i.then_inc(pe_done, 1)
                            did(f"used {g}")

            def feed_forward(name, g0, stream):
                y = {(tt, n): bank(f"y {name} {tt} {n}", 4 + 2 * tt + n) for tt in range(2) for n in range(2)}

                def gate_up(s, half, os):
                    g = g0 + fpos[("gu", s, half)]
                    hi, lo = granule(g)
                    for tt in range(2):
                        t = 2 * stream + tt
                        for k in range(4):
                            kk, cs = 4 * half + k, slice(512 * k, 512 * k + 512)
                            i = split3(os[tt], hT_hi[:, kk, P * t:P * t + P], hT_lo[:, kk, P * t:P * t + P],
                                       hi[:, cs], lo[:, cs], kk == 0, kk == 7)
                        if half:
                            i.then_inc(pe_done, 1)
                            did(f"gu {name} {s} {tt}")
                    if half:
                        did.name(f"used {g}")
                    else:
                        i.then_inc(pe_done, 1)
                        did(f"used {g}")

                def turn_h(s):
                    o = bank(f"hh {name} {s}", 2)
                    for tt in range(2):
                        eng.wait_ge(dve_done, after(f"h {name} {s} {tt}"))
                        for f in range(2):
                            i = nc.tensor.transpose(o[:, 256 * f + P * tt:256 * f + P * tt + P],
                                                    hh[:, tt, P * f:P * f + P], ident[:, :])
                    i.then_inc(pe_done, 1)
                    did(f"hh {name} {s}")

                def down(s):
                    g = g0 + fpos[("d", s, 0)]
                    hi, lo = granule(g)
                    eng.wait_ge(dve_done, after(f"fs {name} {s}"))
                    for f in range(2):
                        for tt in range(2):
                            a = slice(256 * f + P * tt, 256 * f + P * tt + P)
                            for n in range(2):
                                cs = slice(1024 * f + 512 * n, 1024 * f + 512 * n + 512)
                                i = split3(y[(tt, n)], f_hi[:, a], f_lo[:, a], hi[:, cs], lo[:, cs],
                                           s == 0 and f == 0, s == FC - 1 and f == 1)
                    i.then_inc(pe_done, 1)
                    did(f"used {g}", f"down {name} {s}")

                for s in range(FC):
                    os = [bank(f"gu {name} {s} {tt}", tt) for tt in range(2)]
                    gate_up(s, 0, os)
                    if s:
                        turn_h(s - 1)
                    gate_up(s, 1, os)
                    if s:
                        down(s - 1)
                turn_h(FC - 1)
                down(FC - 1)

            def route():
                eng.wait_ge(dve_done, after("router split"))
                for k in range(KD):
                    eng.wait_ge(dve_done, after(f"hT 1 2 {k}"))
                o = bank("logits")
                for tt in range(2):
                    t = 2 + tt
                    for k in range(KD):
                        a = slice(P * t, P * t + P)
                        q = o[:, NE * tt:NE * tt + NE]
                        split3(q, hT_hi[:, k, a], hT_lo[:, k, a], r_hi[:, k, :], r_lo[:, k, :], k == 0, False)
                        i = mm(q, hT_lo[:, k, a], r_lo[:, k, :], start=False, stop=k == 7)
                i.then_inc(pe_done, 1)
                did("logits")

            def rank():
                eng.wait_ge(*loaded["route"])
                eng.wait_ge(dve_done, after("mask"))
                o = bank("rank")
                mask = rt[:, 0:2 * NE].rearrange("p (t e) -> p t e", e=NE)
                mm(o[:, 0:NE], before, mask[:, 0, :], start=True, stop=True)
                mm(o[:, NE:2 * NE], ones[:, :], mask[:, 0, :], start=True, stop=False)
                mm(o[:, NE:2 * NE], before, mask[:, 1, :], start=False, stop=True)
                mm(o[:, 2 * NE:3 * NE], ones[:, :], mask[:, 0, :], start=True, stop=False)
                mm(o[:, 2 * NE:3 * NE], ones[:, :], mask[:, 1, :], start=False, stop=True).then_inc(pe_done, 1)
                did("rank")

            def gather(i, par, q):
                if q == 0:
                    eng.wait_ge(x_pick, i + 1)
                    for part in ("hi", "lo"):
                        eng.wait_ge(act_done if part == "hi" else dve_done, after(f"x{part}"))
                if isinstance(i, int) and i == 0 and q == 0:
                    pass
                else:
                    eng.wait_ge(x_glo, 2 * i + q)
                    if q == 0:
                        eng.wait_ge(x_pickTs, i)
                o = PS[:, 3, :]
                for kk in range(4):
                    k = 4 * q + kk
                    for tt in range(2):
                        mm(o[:, P * kk:P * kk + P], hT_hi[:, k, P * tt:P * tt + P], pick[:, tt, :],
                           start=tt == 0, stop=False)
                        last = mm(o[:, P * kk:P * kk + P], hT_lo[:, k, P * tt:P * tt + P], pick[:, tt, :],
                                  start=False, stop=tt == 1)
                last.then_inc(x_gather, 1)

            def turn_pick(i, par):
                eng.wait_ge(x_glo, 2 * i + 2)
                for tt in range(2):
                    last = nc.tensor.transpose(PS[:, 3, P * tt:P * tt + P], pick[:, tt, :].bitcast(F32), ident[:, :])
                last.then_inc(x_pickT, 1)

            def spread(i, par, tt):
                eng.wait_ge(x_y, 2 * i)
                eng.wait_ge(x_pickTs, i)
                if tt == 0:
                    if not (isinstance(i, int) and i == 1):
                        eng.wait_ge(x_add, 2 * i - 2)
                else:
                    eng.wait_ge(x_add, 2 * i - 1)
                for n in range(2):
                    if par is None:
                        break
                    last = mm(PS[:, 6 + n, :], pickT[:, 1 - par, P * tt:P * tt + P], ysb[:, 512 * n:512 * n + 512],
                              start=True, stop=True)
                if par is None:
                    for odd in range(2):
                        with eng.If((i & 1) == odd):
                            for n in range(2):
                                last = mm(PS[:, 6 + n, :], pickT[:, 1 - odd, P * tt:P * tt + P],
                                          ysb[:, 512 * n:512 * n + 512], start=True, stop=True)
                            last.then_inc(x_z, 1)
                else:
                    last.then_inc(x_z, 1)

            def expert_pass(i, par, follows):
                xa = slice(256 + P * par, 384 + P * par)

                def granule_of(j):
                    eng.wait_ge(x_lo, NGR * i + j + 1)
                    return w_hi[:, j % RING, :], w_lo[:, j % RING, :]

                def gate_up(s, half):
                    j = fpos[("gu", s, half)]
                    hi, lo = granule_of(j)
                    if half == 0 and (follows or s >= 2):
                        eng.wait_ge(x_h, FC * i + (s - 1 if s >= 2 else (0 if s == 0 else -1 + 1)))
                    for k in range(4):
                        kk, cs = 4 * half + k, slice(512 * k, 512 * k + 512)
                        last = split3(PS[:, s % 2, :], hT_hi[:, kk, xa], hT_lo[:, kk, xa], hi[:, cs], lo[:, cs],
                                      kk == 0, kk == 7)
                    last.then_inc(x_used, 1)

                def turn_h(s):
                    eng.wait_ge(x_h, FC * i + s + 1)
                    if follows or s:
                        eng.wait_ge(x_tlo, FC * i + s)
                    for f in range(2):
                        last = nc.tensor.transpose(PS[:, 2, P * f:P * f + P], hh[:, s % 2, P * f:P * f + P],
                                                   ident[:, :])
                    last.then_inc(x_turned, 1)

                def down(s):
                    j = fpos[("d", s, 0)]
                    hi, lo = granule_of(j)
                    eng.wait_ge(x_tlo, FC * i + s + 1)
                    if s == 0 and follows:
                        eng.wait_ge(x_y, 2 * i)
                    for f in range(2):
                        a = slice(P * f, P * f + P)
                        for n in range(2):
                            cs = slice(1024 * f + 512 * n, 1024 * f + 512 * n + 512)
                            last = split3(PS[:, 4 + n, :], f_hi[:, a], f_lo[:, a], hi[:, cs], lo[:, cs],
                                          s == 0 and f == 0, s == FC - 1 and f == 1)
                    last.then_inc(x_used, 1)

                eng.wait_ge(x_glo, 2 * i + 2)
                for s in range(FC):
                    gate_up(s, 0)
                    if s:
                        turn_h(s - 1)
                    gate_up(s, 1)
                    if s:
                        down(s - 1)
                    if follows and s in (2, 4):
                        spread(i, par, s // 4)
                    if s in (6, 8):
                        gather(i + 1, 1 - par, s // 8)
                    if s == 10:
                        turn_pick(i + 1, 1 - par)
                turn_h(FC - 1)
                down(FC - 1)

            eng.wait_ge(*loaded["start"])
            g = 0
            for l in range(DEPTH):
                streams = layer_streams[l]
                modulation(l)
                filters(l)
                norm_turn(l, 1, (0, 1))
                project_in(l, streams)
                hyena(l, streams)
                pooling(l, streams)
                latents(l, streams)
                attention(l, streams)
                project_out(l, streams)
                norm_turn(l, 2, streams)
                for k in range(KD):
                    eng.wait_ge(dve_done, after(f"hT {l} 2 {k}"))
                if l == 0:
                    for s in (0, 1):
                        feed_forward(f"f{s}", gindex[("ffn", 0, 0, s)], s)
                    for s in (0, 1):
                        gates(l, 1, s)
                else:
                    route()
                    rank()
                    gates(l, 1, 1)
                    for b in range(8):
                        eng.wait_ge(reader_of(state["last"][b]), after("read " + state["last"][b]))
                    eng.wait_ge(dve_done, after("plan"))
                    passes = NE + eng.value_load(second[0:1, 0:1], min_val=0, max_val=SLOTS - NE)
                    gather(0, 0, 0)
                    gather(0, 0, 1)
                    turn_pick(0, 0)
                    expert_pass(0, 0, False)
                    with eng.Fori(0, (SLOTS - 1) // 2) as j:
                        for odd in (1, 0):
                            i = 2 * j + (1 if odd else 2)
                            with eng.If(i < passes):
                                expert_pass(i, odd, True)
                    spread(passes, None, 0)
                    spread(passes, None, 1)

        @blk.scalar
        def _(eng):
            did = Steps(table, "act")
            act = nc.scalar.activation
            split = {"next": 0}

            def upto(g):
                while split["next"] <= min(g, NG - 1):
                    n = split["next"]
                    w = width(plan[n][0])
                    if n >= RING:
                        eng.wait_ge(pe_done, after(f"used {n - RING}"))
                    eng.wait_ge(raw_full[n % RING], 16 * (n // RING + 1))
                    nc.scalar.copy(w_hi[:, n % RING, 0:w], raw[:, n % RING, 0:w]).then_inc(act_done, 1)
                    did(f"hi {n}")
                    split["next"] += 1


            def modulation(l):
                if l == 0:
                    eng.wait_ge(*loaded["start"])
                    act(csil[:, :, :], cvec[:, :, :], ACT.Silu).then_inc(act_done, 1)
                    did("csil")
                    eng.wait_ge(act_done, did.count)
                if l:
                    eng.wait_ge(dve_done, after("layer 0"))
                eng.wait_ge(dve_done, after(f"cs0 {l}"))
                nc.scalar.copy(hT_hi[:, :, 0:2], csil[:, :, :]).then_inc(act_done, 1)
                did(f"cshi {l}")
                for n in range(12):
                    upto(gindex[("ada", l, 2 * n + 1, 0)])
                    eng.wait_ge(pe_done, after(f"ada {l} {n}"))
                    o = bank_of(f"ada {l} {n}")
                    if n >= 2:
                        eng.wait_ge(pe_done, after(f"modT {l} {n - 2}"))
                    nc.scalar.copy(row4[:, n % 2, :], o[0:4, :]).then_inc(act_done, 1)
                    did(f"row {l} {n}", f"read ada {l} {n}")

            def filters(l):
                for i in (1, 2):
                    eng.wait_ge(dve_done, after(f"arg{i} {l}"))
                    act(farg[0:FH, i - 1, :], fsc[0:FH, 0, :], ACT.Sin).then_inc(act_done, 1)
                    did(f"sin{i} {l}")
                eng.wait_ge(dve_done, after(f"hfil {l}"))
                for t in range(2):
                    act(fsc[:, t, :], hfil[:, t, 0:L], ACT.Abs).then_inc(act_done, 1)
                    did(f"abs {l} {t}")
                    act(farg[:, t, :], hfil[:, t, L:2 * L], ACT.Abs).then_inc(act_done, 1)
                    did(f"abs {l} {t}")
                for ft in range(2):
                    eng.wait_ge(pe_done, after(f"fA {l} {ft}"))
                    o = bank_of(f"fA {l} {ft}")
                    nc.scalar.copy(HA[:, ft, :], o[:, 0:L]).then_inc(act_done, 1)
                    did()
                    nc.scalar.copy(HBs[:, ft, :], o[:, L:2 * L]).then_inc(act_done, 1)
                    did(f"read fA {l} {ft}")
                eng.wait_ge(pe_done, after(f"fD {l}"))
                o = bank_of(f"fD {l}")
                nc.scalar.copy(HD0, o[:, 0:L]).then_inc(act_done, 1)
                did(f"read fD {l}", f"H {l}")

            def norm(l, w, streams):
                eng.wait_ge(dve_done, after(f"ss {l} {w}"))
                ts = tiles_of(streams)
                a, b = ts[0], ts[-1] + 1
                act(small[:, 8 + a:8 + b], small[:, a:b], ACT.Sqrt, bias=epsb[:, 0:1], scale=1.0 / D).then_inc(act_done, 1)
                did(f"std {l} {w}")
                for k in range(KD):
                    eng.wait_ge(pe_done, after(f"nT {l} {w} {k}"))
                    o = bank_of(f"nT {l} {w} {k}")
                    if k == 0:
                        eng.wait_ge(dve_done, after(f"gs {l}"))
                    for s in streams:
                        q = slice(256 * s, 256 * s + 256)
                        j = 3 * (w - 1)
                        act(hT_hi[:, k, q], o[:, q], ACT.Identity, bias=mod[:, 8 * j + k, s:s + 1],
                                 scale=gsc[:, w - 1, k, s:s + 1]).then_inc(act_done, 1)
                        did(f"hThi {l} {w} {k}")

            def project_in(l, streams):
                sp = span(streams)
                for ct in range(6):
                    upto(gindex[("ina", l, ct // 2, 0)])
                    eng.wait_ge(pe_done, after(f"u {l} {ct}"))
                    o = bank_of(f"u {l} {ct}")
                    if ct == 0:
                        eng.wait_ge(dve_done, after(f"upad {l}"))
                    if ct >= 2:
                        eng.wait_ge(dve_done, after(f"conv {l} {ct - 2}"))
                    for s in streams:
                        nc.scalar.copy(upad[:, ct % 2, s, 1:257], o[:, 256 * s:256 * s + 256]).then_inc(act_done, 1)
                        did(f"us {l} {ct}", f"read u {l} {ct}")
                for b in range(2):
                    upto(gindex[("inb", l, 2 * b + 1, 0)])
                    for t in (tiles_of(streams) if b == 0 else range(NT)):
                        eng.wait_ge(pe_done, after(f"B {l} {b} {t}"))
                        o = bank_of(f"B {l} {b} {t}")
                        nc.scalar.copy(Bm[:, t, HB * b:HB * b + HB], o[:, 0:HB]).then_inc(act_done, 1)
                        did(f"Bs {l} {b} {t}", f"read B {l} {b} {t}")

            def hyena(l, streams):
                sp = span(streams)
                for ct in range(2):
                    eng.wait_ge(pe_done, after(f"zT {l} {ct}"))
                    o = bank_of(f"zT {l} {ct}")
                    for s in streams:
                        for t in range(2):
                            nc.scalar.copy(zT[:, t, 256 * s + P * ct:256 * s + P * ct + P],
                                                o[:, 256 * s + P * t:256 * s + P * t + P]).then_inc(act_done, 1)
                            did(f"zTs {l} {ct}", f"read zT {l} {ct}")
                for ct in range(2):
                    eng.wait_ge(dve_done, after(f"yh {l} {ct}"))
                    nc.scalar.copy(hT_hi[:, ct, sp], ytmp[:, ct, sp]).then_inc(act_done, 1)
                    did(f"mixhi {l} {ct}")

            def pooling(l, streams):
                sp = span(streams)
                for g in range(4):
                    eng.wait_ge(pe_done, after(f"d {l} {g}"))
                    o = bank_of(f"d {l} {g}")
                    if g >= 2:
                        eng.wait_ge(pe_done, after(f"yp {l} {(g - 2) // 2} {g % 2}"))
                    nc.scalar.copy(dT[0:GROUP, g % 2, sp], o[0:GROUP, sp]).then_inc(act_done, 1)
                    did(f"dT {l} {g}", f"read d {l} {g}")
                for pair in range(2):
                    eng.wait_ge(pe_done, after(f"yp {l} {pair}"))
                    o = bank_of(f"yp {l} {pair}")
                    a = PAR["psc"][0] + pair
                    act(hT_hi[:, 2 + pair, sp], o[:, sp], ACT.Copy, scale=par[:, l, a:a + 1]).then_inc(act_done, 1)
                    did(f"mixhi {l} {2 + pair}")

            def latents(l, streams):
                sp = span(streams)
                eng.wait_ge(dve_done, after(f"ssq {l}"))
                act(small[:, 24:28], small[:, 16:20], ACT.Sqrt, bias=epsb[:, 0:1], scale=1.0 / QL).then_inc(act_done, 1)
                did()
                act(small[:, 28:32], small[:, 20:24], ACT.Sqrt, bias=epsb[:, 0:1], scale=1.0 / KVL).then_inc(act_done, 1)
                did(f"stdq {l}")
                for k in range(KQ):
                    eng.wait_ge(pe_done, after(f"cqT {l} {k}"))
                    o = bank_of(f"cqT {l} {k}")
                    a = PAR["qg"][0] + k
                    act(cqT[:, k, sp], o[:, sp], ACT.Copy, scale=par[:, l, a:a + 1]).then_inc(act_done, 1)
                    did(f"cqTs {l} {k}", f"read cqT {l} {k}")
                for k in range(KKV):
                    eng.wait_ge(pe_done, after(f"ckvT {l} {k}"))
                    o = bank_of(f"ckvT {l} {k}")
                    a = PAR["kvg"][0] + k
                    act(ckvT[:, k, :], o, ACT.Copy, scale=par[:, l, a:a + 1]).then_inc(act_done, 1)
                    did(f"ckvTs {l} {k}", f"read ckvT {l} {k}")
                eng.wait_ge(pe_done, after(f"kpT {l}"))
                o = bank_of(f"kpT {l}")
                for h in range(HEADS):
                    nc.scalar.copy(KT[64:96, h, :], o[0:ROPE, :]).then_inc(act_done, 1)
                    did(f"KTpe {l}", f"read kpT {l}")
                for pr in range(4):
                    eng.wait_ge(pe_done, after(f"k {l} {pr}"))
                    o = bank_of(f"k {l} {pr}")
                    for j in range(2):
                        nc.scalar.copy(KT[0:64, 2 * pr + j, :], o[64 * j:64 * j + 64, :]).then_inc(act_done, 1)
                        did(f"KTs {l}", f"read k {l} {pr}")
                for t in range(NT):
                    eng.wait_ge(pe_done, after(f"v {l} {t}"))
                    o = bank_of(f"v {l} {t}")
                    nc.scalar.copy(V[:, t, :], o).then_inc(act_done, 1)
                    did(f"Vs {l}", f"read v {l} {t}")

            def attention(l, streams):
                units = [(t, h) for t in tiles_of(streams) for h in range(HEADS)]
                for n, (t, h) in enumerate(units):
                    nk = 256 if t < 2 else 512
                    eng.wait_ge(pe_done, after(f"s {l} {n}"))
                    o = bank_of(f"s {l} {n}")
                    eng.wait_ge(dve_done, after(f"nmax {l} {n}"))
                    if n >= 2:
                        eng.wait_ge(pe_done, after(f"pT {l} {n - 2}"))
                    if n == 0:
                        eng.wait_ge(pe_done, after(f"q {l} {HEADS - 1}"))
                    act(prob[:, n % 2, 0:nk], o[:, 0:nk], ACT.Exp, bias=small[:, 64 + n:65 + n], scale=SM_SCALE,
                             accum_out=small[:, 128 + n:129 + n]).then_inc(act_done, 1)
                    did(f"p {l} {n}", f"read s {l} {n}")
                for k in range(4):
                    eng.wait_ge(pe_done, after(f"aT {l} {k}"))
                    o = bank_of(f"aT {l} {k}")
                    sp = span(streams)
                    nc.scalar.copy(hT_hi[:, 4 + k, sp], o[:, sp]).then_inc(act_done, 1)
                    did(f"mixhi {l} {4 + k}")

            def gates(l, w, s):
                for half in range(2):
                    eng.wait_ge(pe_done, after(f"gate {l} {w} {s} {half}"))
                    o = bank_of(f"gate {l} {w} {s} {half}")
                    dst = gbc[:, s, 512 * half:512 * half + 512] if w == 0 else gbf[:, 512 * half:512 * half + 512]
                    if w == 1 and s == 1 and l == 0:
                        eng.wait_ge(dve_done, after(f"res {l} 1 0"))
                    nc.scalar.copy(dst, o).then_inc(act_done, 1)
                    did(f"gb {l} {w} {s}", f"read gate {l} {w} {s} {half}")

            def project_out(l, streams):
                for s in streams:
                    gates(l, 0, s)
                upto(gindex[("out", l, 3, 0)])

            def feed_forward(name, g0):
                upto(g0 + 2)
                for s in range(FC):
                    if s:
                        eng.wait_ge(pe_done, after(f"hh {name} {s - 1}"))
                        o = bank_of(f"hh {name} {s - 1}")
                        if s > 1:
                            eng.wait_ge(pe_done, after(f"down {name} {s - 2}"))
                        nc.scalar.copy(f_hi[:, :], o).then_inc(act_done, 1)
                        did(f"fhi {name} {s - 1}")
                    if s + 1 < FC:
                        upto(g0 + fpos[("gu", s + 1, 1)])
                    for tt in range(2):
                        eng.wait_ge(pe_done, after(f"gu {name} {s} {tt}"))
                        o = bank_of(f"gu {name} {s} {tt}")
                        act(sg[:, tt, :], o[:, 0:256], ACT.Silu).then_inc(act_done, 1)
                        did(f"sg {name} {s} {tt}")
                    upto(g0 + fpos[("d", s, 0)])
                eng.wait_ge(pe_done, after(f"hh {name} {FC - 1}"))
                o = bank_of(f"hh {name} {FC - 1}")
                eng.wait_ge(pe_done, after(f"down {name} {FC - 2}"))
                nc.scalar.copy(f_hi[:, :], o).then_inc(act_done, 1)
                did(f"fhi {name} {FC - 1}")

            def gathered(i, par, q):
                eng.wait_ge(x_gather, 2 * i + q + 1)
                for kk in range(4):
                    k = 4 * q + kk
                    last = act(hT_hi[:, k, 256 + P * par:384 + P * par], PS[:, 3, P * kk:P * kk + P], ACT.Identity,
                               bias=mod[:, 24 + k, 1:2], scale=gsc[:, 1, k, 1:2])
                last.then_inc(x_ghi, 1)

            def save_pick(i, par):
                eng.wait_ge(x_pickT, i + 1)
                nc.scalar.copy(pickT[:, par, :], PS[:, 3, 0:256]).then_inc(x_pickTs, 1)

            def save_y(i):
                eng.wait_ge(x_used, NGR * i)
                if not (isinstance(i, int) and i == 1):
                    eng.wait_ge(x_z, 2 * i - 2)
                for n in range(2):
                    nc.scalar.copy(ysb[:, 512 * n:512 * n + 512], PS[:, 4 + n, :]).then_inc(x_y, 1)

            def expert_pass(i, par, follows, pair):
                def high(j):
                    if follows or j >= RING:
                        eng.wait_ge(x_used, NGR * i + j + 1 - RING)
                    else:
                        eng.wait_ge(pe_done, after(f"used {NG - RING + j}"))
                    n = NGR * par + j
                    eng.wait_ge(x_full[n % XRING], 16 * (FC * pair + n // XRING + 1))
                    nc.scalar.copy(w_hi[:, j % RING, :], x_raw(n)).then_inc(x_hi, 1)

                def high_turned(s):
                    eng.wait_ge(x_turned, FC * i + s + 1)
                    if follows or s:
                        j = fpos[("d", s - 1, 0)] + 1 if s else 0
                        eng.wait_ge(x_used, NGR * i + j)
                    nc.scalar.copy(f_hi[:, 0:256], PS[:, 2, 0:256]).then_inc(x_thi, 1)

                for j in range(RING):
                    high(j)
                if follows:
                    save_y(i)
                for s in range(FC):
                    if s:
                        high_turned(s - 1)
                    if s + 1 < FC:
                        for j in range(fpos[("gu", s + 1, 0)] if s else RING, fpos[("gu", s + 1, 1)] + 1):
                            high(j)
                    eng.wait_ge(x_used, NGR * i + fpos[("gu", s, 1)] + 1)
                    act(sg[:, s % 2, :], PS[:, s % 2, 0:256], ACT.Silu).then_inc(x_silu, 1)
                    high(fpos[("d", s, 0)])
                    if s in (6, 8):
                        gathered(i + 1, 1 - par, s // 8)
                    if s == 10:
                        save_pick(i + 1, 1 - par)
                high_turned(FC - 1)

            epsb = small[:, 250:251]
            for l in range(DEPTH):
                streams = layer_streams[l]
                if l == 0:
                    eng.wait_ge(dve_done, after("eps"))
                modulation(l)
                filters(l)
                norm(l, 1, (0, 1))
                project_in(l, streams)
                hyena(l, streams)
                pooling(l, streams)
                latents(l, streams)
                attention(l, streams)
                project_out(l, streams)
                norm(l, 2, streams)
                if l == 0:
                    for s in (0, 1):
                        feed_forward(f"f{s}", gindex[("ffn", 0, 0, s)])
                    for s in (0, 1):
                        gates(l, 1, s)
                else:
                    eng.wait_ge(*loaded["route"])
                    nc.scalar.copy(r_hi[:, :, :], router).then_inc(act_done, 1)
                    did("rhi")
                    eng.wait_ge(dve_done, after("dlogit"))
                    act(small[:, 40:42], small[:, 38:40], ACT.Exp).then_inc(act_done, 1)
                    did("elogit")
                    for tt in range(2):
                        eng.wait_ge(pe_done, after("logits"))
                        nc.scalar.copy(hT_hi[:, :, P * tt:P * tt + P],
                                       xn[:, 2 + tt, :].rearrange("p (k c) -> p k c", c=P)).then_inc(act_done, 1)
                        did("xhi")
                    gates(l, 1, 1)
                    eng.wait_ge(dve_done, after("plan"))
                    passes = NE + eng.value_load(second[0:1, 0:1], min_val=0, max_val=SLOTS - NE)
                    gathered(0, 0, 0)
                    gathered(0, 0, 1)
                    save_pick(0, 0)
                    expert_pass(0, 0, False, 0)
                    with eng.Fori(0, (SLOTS - 1) // 2) as j:
                        for odd in (1, 0):
                            i = 2 * j + (1 if odd else 2)
                            with eng.If(i < passes):
                                expert_pass(i, odd, True, j if odd else j + 1)
                    save_y(passes)
            eng.wait_ge(dve_done, after("ssf"))
            act(small[:, 36:38], small[:, 34:36], ACT.Sqrt, bias=epsb[:, 0:1], scale=1.0 / D).then_inc(act_done, 1)
            did("stdf")

        @blk.vector
        def _(eng):
            did = Steps(table, "dve")
            v = nc.vector
            split = {"next": 0}

            def upto(g):
                while split["next"] <= min(g, NG - 1):
                    n = split["next"]
                    w = width(plan[n][0])
                    eng.wait_ge(act_done, after(f"hi {n}"))
                    v.tensor_tensor(w_lo[:, n % RING, 0:w], raw[:, n % RING, 0:w],
                                         w_hi[:, n % RING, 0:w].bitcast(F32), ALU.subtract).then_inc(dve_done, 1)
                    did(f"lo {n}")
                    split["next"] += 1



            def modulation(l):
                if l == 0:
                    v.memset(small[:, :], 0.0).then_inc(dve_done, 1)
                    eng.wait_ge(dve_done, did())
                    v.memset(small[:, 250:251], EPS).then_inc(dve_done, 1)
                    did("eps")
                if l:
                    eng.wait_ge(pe_done, after("used %d" % (gindex[("ffn", 0, 0, 1)] + 3 * FC - 1)))
                v.memset(hT_hi[:, :, 0:P].bitcast(F32), 0.0).then_inc(dve_done, 1)
                did(f"cs0 {l}")
                eng.wait_ge(act_done, after(f"cshi {l}"))
                eng.wait_ge(*loaded["start"])
                eng.wait_ge(act_done, after("csil"))
                v.tensor_tensor(hT_hi[:, :, 2:4], csil[:, :, :], hT_hi[:, :, 0:2].bitcast(F32), ALU.subtract).then_inc(dve_done, 1)
                did(f"cs {l}")
                b = PAR["bada"][0]
                for n in range(12):
                    upto(gindex[("ada", l, 2 * n + 1, 0)])
                    if n:
                        bias_mod(l, n - 1)
                bias_mod(l, 11)
                eng.wait_ge(dve_done, did.count)
                for w in range(2):
                    g0 = PAR["g1"][0] + KD * w
                    j = 3 * w + 1
                    for s in range(2):
                        v.scalar_tensor_tensor(out=gsc[:, w, :, s], in0=mod[:, 8 * j:8 * j + 8, s], scalar=1.0,
                                                    in1=par[:, l, g0:g0 + KD], op0=ALU.add, op1=ALU.mult).then_inc(dve_done, 1)
                        did(f"gs {l}")

            def bias_mod(l, n):
                eng.wait_ge(pe_done, after(f"modT {l} {n}"))
                o = bank_of(f"modT {l} {n}")
                b = PAR["bada"][0] + 4 * n
                for s in range(2):
                    q = o[:, 0:8].rearrange("p (j s) -> p j s", s=2)
                    v.tensor_tensor(mod[:, 4 * n:4 * n + 4, s], q[:, :, s], par[:, l, b:b + 4], ALU.add).then_inc(dve_done, 1)
                    did(f"read modT {l} {n}")

            def filters(l):
                for i, nm in ((1, "f1"), (2, "f2")):
                    eng.wait_ge(pe_done, after(f"{nm} {l}"))
                    o = bank_of(f"{nm} {l}")[0:FH, 0:L]
                    b, f = PAR[f"b{i}"][0], PAR[f"f{i}"][0]
                    ar, rt = fsc[0:FH, 0, :], fsc[0:FH, 1, :]
                    v.tensor_scalar(ar, o, par[0:FH, l, b:b + 1], par[0:FH, l, f:f + 1], ALU.add, ALU.mult).then_inc(dve_done, 1)
                    eng.wait_ge(dve_done, did(f"read {nm} {l}"))
                    v.tensor_scalar(rt, ar, 1 / (2 * math.pi), ROUND, ALU.mult, ALU.add).then_inc(dve_done, 1)
                    eng.wait_ge(dve_done, did())
                    v.tensor_scalar(rt, rt, ROUND, None, ALU.subtract).then_inc(dve_done, 1)
                    eng.wait_ge(dve_done, did())
                    v.scalar_tensor_tensor(out=ar, in0=rt, scalar=-TWO_PI_A, in1=ar, op0=ALU.mult, op1=ALU.add).then_inc(dve_done, 1)
                    eng.wait_ge(dve_done, did())
                    v.scalar_tensor_tensor(out=ar, in0=rt, scalar=-TWO_PI_B, in1=ar, op0=ALU.mult, op1=ALU.add).then_inc(dve_done, 1)
                    eng.wait_ge(dve_done, did())
                    v.tensor_scalar(ar, ar, 3.1415925, -3.1415925, ALU.min, ALU.max).then_inc(dve_done, 1)
                    eng.wait_ge(dve_done, did(f"arg{i} {l}"))
                eng.wait_ge(act_done, after(f"sin2 {l}"))
                for t in range(2):
                    eng.wait_ge(pe_done, after(f"f3 {l} {t}"))
                    o = bank_of(f"f3 {l} {t}")
                    v.tensor_tensor(hfil[:, t, :], o, decay[:, t, :], ALU.mult).then_inc(dve_done, 1)
                    eng.wait_ge(dve_done, did(f"read f3 {l} {t}", f"hfil {l}"))
                    v.tensor_tensor(hp[:, t, :], hfil[:, t, 0:L], hfil[:, t, L:2 * L], ALU.add).then_inc(dve_done, 1)
                    did()
                    v.tensor_tensor(hm[:, t, :], hfil[:, t, 0:L], hfil[:, t, L:2 * L], ALU.subtract).then_inc(dve_done, 1)
                    did()
                eng.wait_ge(act_done, after(f"abs {l} 1"))
                for t in range(2):
                    v.tensor_tensor(fsc[:, t, :], fsc[:, t, :], farg[:, t, :], ALU.add).then_inc(dve_done, 1)
                    did(f"habs {l}")
                eng.wait_ge(pe_done, after(f"fn {l}"))
                o = bank_of(f"fn {l}")
                v.reciprocal(small[:, 32:34], o[:, 0:2]).then_inc(dve_done, 1)
                eng.wait_ge(dve_done, did(f"read fn {l}", f"rn {l}"))

            def norm(l, w, streams):
                ts = tiles_of(streams)
                if w == 1:
                    eng.wait_ge(pe_done, after(f"fn {l}"))
                for t in ts:
                    v.tensor_tensor_reduce(xn[:, t, :], X[:, t, :], X[:, t, :], 1.0, 0.0, ALU.mult, ALU.add,
                                                small[:, t:t + 1]).then_inc(dve_done, 1)
                    did(f"ss {l} {w}")
                a, b = ts[0], ts[-1] + 1
                eng.wait_ge(act_done, after(f"std {l} {w}"))
                v.reciprocal(small[:, 12:12 + b - a], small[:, 8 + a:8 + b]).then_inc(dve_done, 1)
                eng.wait_ge(dve_done, did())
                for t in ts:
                    v.tensor_scalar(xn[:, t, :], X[:, t, :], small[:, 12 + t - a:13 + t - a], None, ALU.mult).then_inc(dve_done, 1)
                    did(f"xn {l} {w} {t}")
                for k in range(KD):
                    eng.wait_ge(act_done, after(f"hThi {l} {w} {k}"))
                    eng.wait_ge(pe_done, after(f"nT {l} {w} {k}"))
                    o = bank_of(f"nT {l} {w} {k}")
                    j = 3 * (w - 1)
                    for s in streams:
                        q = slice(256 * s, 256 * s + 256)
                        v.tensor_scalar(tn[:, k % 2, q], o[:, q], gsc[:, w - 1, k, s:s + 1],
                                             mod[:, 8 * j + k, s:s + 1], ALU.mult, ALU.add).then_inc(dve_done, 1)
                        did(f"read nT {l} {w} {k}")
                    eng.wait_ge(dve_done, did.count)
                    q = span(streams)
                    v.tensor_tensor(hT_lo[:, k, q], tn[:, k % 2, q], hT_hi[:, k, q].bitcast(F32), ALU.subtract).then_inc(dve_done, 1)
                    did(f"hT {l} {w} {k}")

            def project_in(l, streams):
                for b in range(2):
                    for s in streams:
                        v.memset(upad[:, b, s, 0:1], 0.0).then_inc(dve_done, 1)
                        did()
                        v.memset(upad[:, b, s, 257:258], 0.0).then_inc(dve_done, 1)
                        did(f"upad {l}")
                a0, b0 = PAR["sw"][0], PAR["sb"][0]
                for ct in range(6):
                    upto(gindex[("ina", l, ct // 2, 0)])
                    eng.wait_ge(act_done, after(f"us {l} {ct}"))
                    for s in streams:
                        q = uc[:, ct, 256 * s:256 * s + 256]
                        u = lambda j: upad[:, ct % 2, s, j:j + 256]
                        w = lambda j: par[:, l, a0 + 6 * j + ct:a0 + 6 * j + ct + 1]
                        v.tensor_scalar(q, u(0), w(0), None, ALU.mult).then_inc(dve_done, 1)
                        eng.wait_ge(dve_done, did())
                        v.scalar_tensor_tensor(out=q, in0=u(1), scalar=w(1), in1=q, op0=ALU.mult, op1=ALU.add).then_inc(dve_done, 1)
                        eng.wait_ge(dve_done, did())
                        v.scalar_tensor_tensor(out=q, in0=u(2), scalar=w(2), in1=q, op0=ALU.mult, op1=ALU.add).then_inc(dve_done, 1)
                        eng.wait_ge(dve_done, did())
                        v.tensor_scalar(q, q, par[:, l, b0 + ct:b0 + ct + 1], None, ALU.add).then_inc(dve_done, 1)
                        eng.wait_ge(dve_done, did(f"conv {l} {ct}"))
                        if ct >= 4:
                            z = uc[:, ct - 2, 256 * s:256 * s + 256]
                            v.tensor_tensor(z, z, q, ALU.mult).then_inc(dve_done, 1)
                            did(f"z {l} {ct - 4}")
                upto(gindex[("inb", l, 3, 0)])

            def hyena(l, streams):
                sp = span(streams)
                eng.wait_ge(act_done, after(f"H {l}"))
                t1, t2 = ytmp[:, 0, :], ytmp[:, 1, :]
                for ft in range(2):
                    eng.wait_ge(pe_done, after(f"Zs {l} {ft}"))
                    zc, zs = bank_of(f"Zc {l} {ft}"), bank_of(f"Zs {l} {ft}")
                    dd = HD0 if ft == 0 else HA[:, 1, :]
                    for s in streams:
                        q = slice(256 * s, 256 * s + 256)
                        v.tensor_tensor(Yc[:, ft, q], zc[:, q], HA[:, ft, :], ALU.mult).then_inc(dve_done, 1)
                        did()
                        v.tensor_tensor(t1[:, q], zs[:, q], HBs[:, ft, :], ALU.mult).then_inc(dve_done, 1)
                        did()
                        v.tensor_tensor(Ys[:, ft, q], zc[:, q], HBs[:, ft, :], ALU.mult).then_inc(dve_done, 1)
                        did(f"read Zc {l} {ft}")
                        v.tensor_tensor(t2[:, q], zs[:, q], dd, ALU.mult).then_inc(dve_done, 1)
                        eng.wait_ge(dve_done, did(f"read Zs {l} {ft}"))
                    v.tensor_tensor(Yc[:, ft, sp], Yc[:, ft, sp], t1[:, sp], ALU.subtract).then_inc(dve_done, 1)
                    did()
                    v.tensor_tensor(Ys[:, ft, sp], Ys[:, ft, sp], t2[:, sp], ALU.add).then_inc(dve_done, 1)
                    eng.wait_ge(dve_done, did(f"Y {l}"))
                b0 = PAR["hyb"][0]
                for ct in range(2):
                    eng.wait_ge(pe_done, after(f"y {l} {ct}"))
                    o = bank_of(f"y {l} {ct}")
                    y = ytmp[:, ct, sp]
                    z = uc[:, 2 + ct, sp]
                    v.tensor_scalar(z, z, par[:, l, b0 + ct:b0 + ct + 1], None, ALU.mult).then_inc(dve_done, 1)
                    eng.wait_ge(dve_done, did())
                    v.scalar_tensor_tensor(out=y, in0=o[:, sp], scalar=small[:, 32 + ct:33 + ct], in1=z,
                                                op0=ALU.mult, op1=ALU.add).then_inc(dve_done, 1)
                    eng.wait_ge(dve_done, did(f"read y {l} {ct}"))
                    v.tensor_tensor(y, y, uc[:, ct, sp], ALU.mult).then_inc(dve_done, 1)
                    eng.wait_ge(dve_done, did(f"yh {l} {ct}"))
                    eng.wait_ge(act_done, after(f"mixhi {l} {ct}"))
                    v.tensor_tensor(hT_lo[:, ct, sp], y, hT_hi[:, ct, sp].bitcast(F32), ALU.subtract).then_inc(dve_done, 1)
                    did(f"mix {l} {ct}")
                did.name(f"hyena {l}")

            def pooling(l, streams):
                sp = span(streams)
                for pair in range(2):
                    eng.wait_ge(act_done, after(f"mixhi {l} {2 + pair}"))
                    eng.wait_ge(pe_done, after(f"yp {l} {pair}"))
                    o = bank_of(f"yp {l} {pair}")
                    a = PAR["psc"][0] + pair
                    v.scalar_tensor_tensor(out=hT_lo[:, 2 + pair, sp], in0=o[:, sp], scalar=par[:, l, a:a + 1],
                                                in1=hT_hi[:, 2 + pair, sp].bitcast(F32), op0=ALU.mult,
                                                op1=ALU.subtract).then_inc(dve_done, 1)
                    did(f"mix {l} {2 + pair}", f"read yp {l} {pair}")

            def latents(l, streams):
                sp = span(streams)
                eng.wait_ge(*loaded[f"mla {l}"])
                for t in range(NT):
                    eng.wait_ge(act_done, after(f"Bs {l} 1 {t}"))
                    if t in tiles_of(streams):
                        v.tensor_tensor_reduce(junk, Bm[:, t, 256:640], Bm[:, t, 256:640], 1.0, 0.0, ALU.mult,
                                                    ALU.add, small[:, 16 + t:17 + t]).then_inc(dve_done, 1)
                        eng.wait_ge(dve_done, did())
                    v.tensor_tensor_reduce(junk[:, 0:KVL], Bm[:, t, 640:896], Bm[:, t, 640:896], 1.0, 0.0,
                                                ALU.mult, ALU.add, small[:, 20 + t:21 + t]).then_inc(dve_done, 1)
                    eng.wait_ge(dve_done, did(f"ssq {l}"))
                eng.wait_ge(act_done, after(f"stdq {l}"))
                v.reciprocal(small[:, 24:32], small[:, 24:32]).then_inc(dve_done, 1)
                eng.wait_ge(dve_done, did())
                for t in range(NT):
                    if t in tiles_of(streams):
                        v.tensor_scalar(Bm[:, t, 256:640], Bm[:, t, 256:640], small[:, 24 + t:25 + t], None,
                                             ALU.mult).then_inc(dve_done, 1)
                        did(f"cqn {l} {t}")
                    v.tensor_scalar(Bm[:, t, 640:896], Bm[:, t, 640:896], small[:, 28 + t:29 + t], None,
                                         ALU.mult).then_inc(dve_done, 1)
                    did(f"ckvn {l} {t}")
                for j in range(2):
                    k1, k2 = Bm[:, 2 + j, 896:928], Bm[:, 2 + j, 928:960]
                    v.tensor_tensor(k1, k1, ropek[:, j, 0:32], ALU.mult).then_inc(dve_done, 1)
                    did()
                    v.tensor_tensor(k2, k2, ropek[:, j, 32:64], ALU.mult).then_inc(dve_done, 1)
                    eng.wait_ge(dve_done, did())
                    v.tensor_tensor(k1, k1, k2, ALU.add).then_inc(dve_done, 1)
                    did(f"kpe {l}")
                for h in range(HEADS):
                    eng.wait_ge(pe_done, after(f"q {l} {h}"))
                    o = bank_of(f"q {l} {h}")
                    if 0 in streams:
                        v.tensor_copy(qT[0:96, h, 0:256], o[0:96, 0:256]).then_inc(dve_done, 1)
                        did()
                    q = slice(256, 512)
                    v.tensor_copy(qT[0:64, h, q], o[0:64, q]).then_inc(dve_done, 1)
                    did()
                    v.tensor_tensor(qT[64:96, h, q], o[64:96, q], ropeq[64:96, 0:256], ALU.mult).then_inc(dve_done, 1)
                    did()
                    v.tensor_tensor(qtmp[64:96, :], o[96:128, q], ropeq[96:128, 256:512], ALU.mult).then_inc(dve_done, 1)
                    eng.wait_ge(dve_done, did(f"read q {l} {h}"))
                    v.tensor_tensor(qT[64:96, h, q], qT[64:96, h, q], qtmp[64:96, :], ALU.add).then_inc(dve_done, 1)
                    eng.wait_ge(dve_done, did(f"qTs {l} {h}"))

            def attention(l, streams):
                units = [(t, h) for t in tiles_of(streams) for h in range(HEADS)]
                N = len(units)

                def copy_p(n):
                    eng.wait_ge(pe_done, after(f"pT {l} {n}"))
                    o = bank_of(f"pT {l} {n}")
                    nk = 256 if units[n][0] < 2 else 512
                    if n >= 2:
                        eng.wait_ge(pe_done, after(f"pvn {l} {n - 2}"))
                    v.tensor_copy(probT[:, n % 2, 0:nk], o[:, 0:nk]).then_inc(dve_done, 1)
                    did(f"pTs {l} {n}", f"read pT {l} {n}")

                def finish(t):
                    eng.wait_ge(pe_done, after(f"pv {l} {t}"))
                    o = bank_of(f"pv {l} {t}")
                    n0 = units.index((t, 0))
                    v.reciprocal(small[:, 192:200], small[:, 128 + n0:136 + n0]).then_inc(dve_done, 1)
                    eng.wait_ge(dve_done, did())
                    for h in range(HEADS):
                        v.tensor_scalar(att[:, t, VD * h:VD * h + VD], o[:, VD * h:VD * h + VD],
                                             small[:, 192 + h:193 + h], None, ALU.mult).then_inc(dve_done, 1)
                        did(f"att {l} {t}", f"read pv {l} {t}")

                for n in range(N + 2):
                    if n < N:
                        t, h = units[n]
                        nk = 256 if t < 2 else 512
                        eng.wait_ge(pe_done, after(f"s {l} {n}"))
                        o = bank_of(f"s {l} {n}")
                        v.reduce_max(small[:, 64 + n:65 + n], o[:, 0:nk], AX.X).then_inc(dve_done, 1)
                        eng.wait_ge(dve_done, did())
                        v.tensor_scalar(small[:, 64 + n:65 + n], small[:, 64 + n:65 + n], -SM_SCALE, None, ALU.mult).then_inc(dve_done, 1)
                        did(f"nmax {l} {n}")
                    if 1 <= n <= N:
                        copy_p(n - 1)
                    if n >= 2 and units[n - 2][1] == HEADS - 1:
                        finish(units[n - 2][0])
                sp = span(streams)
                for k in range(4):
                    eng.wait_ge(act_done, after(f"mixhi {l} {4 + k}"))
                    eng.wait_ge(pe_done, after(f"aT {l} {k}"))
                    o = bank_of(f"aT {l} {k}")
                    v.tensor_tensor(hT_lo[:, 4 + k, sp], o[:, sp], hT_hi[:, 4 + k, sp].bitcast(F32),
                                         ALU.subtract).then_inc(dve_done, 1)
                    did(f"mix {l} {4 + k}", f"read aT {l} {k}")

            def diagonal(l, w, s):
                dg = diag if w == 0 else fdiag
                j = 16 if w == 0 else 40
                for k in range(KD):
                    v.tensor_scalar(dg[:, k, :], ident[:, :], mod[:, j + k, s:s + 1], None, ALU.mult).then_inc(dve_done, 1)
                    did(f"diag {l} {w} {s}")

            def project_out(l, streams):
                for s in streams:
                    if s == 1 and 0 in streams:
                        eng.wait_ge(pe_done, after(f"gate {l} 0 0 1"))
                    diagonal(l, 0, s)
                upto(gindex[("out", l, 3, 0)])
                eng.wait_ge(act_done, after(f"gb {l} 0 {streams[-1]}"))
                for n in range(2):
                    for j, t in enumerate(tiles_of(streams)):
                        eng.wait_ge(pe_done, after(f"o {l} {n} {t}"))
                        o = bank_of(f"o {l} {n} {t}")
                        q = slice(512 * n, 512 * n + 512)
                        v.tensor_tensor(rtmp[:, j % 2, :], o, gbc[:, t // 2, q], ALU.mult).then_inc(dve_done, 1)
                        eng.wait_ge(dve_done, did(f"read o {l} {n} {t}"))
                        v.tensor_tensor(X[:, t, q], X[:, t, q], rtmp[:, j % 2, :], ALU.add).then_inc(dve_done, 1)
                        did(f"projected {l}")
                eng.wait_ge(dve_done, did.count)

            def feed_forward(name, g0):
                def turned(s):
                    eng.wait_ge(act_done, after(f"fhi {name} {s}"))
                    eng.wait_ge(pe_done, after(f"hh {name} {s}"))
                    o = bank_of(f"hh {name} {s}")
                    v.tensor_tensor(f_lo[:, :], o, f_hi[:, :].bitcast(F32), ALU.subtract).then_inc(dve_done, 1)
                    did(f"fs {name} {s}", f"read hh {name} {s}")

                upto(g0 + 2)
                for s in range(FC):
                    if s:
                        turned(s - 1)
                    if s + 1 < FC:
                        upto(g0 + fpos[("gu", s + 1, 1)])
                    for tt in range(2):
                        eng.wait_ge(act_done, after(f"sg {name} {s} {tt}"))
                        eng.wait_ge(pe_done, after(f"gu {name} {s} {tt}"))
                        o = bank_of(f"gu {name} {s} {tt}")
                        v.tensor_tensor(hh[:, tt, :], o[:, 256:512], sg[:, tt, :], ALU.mult).then_inc(dve_done, 1)
                        did(f"h {name} {s} {tt}", f"read gu {name} {s} {tt}")
                    upto(g0 + fpos[("d", s, 0)])
                turned(FC - 1)

            def choose():
                eng.wait_ge(act_done, after("rhi"))
                v.tensor_tensor(r_lo[:, :, :], router, r_hi[:, :, :].bitcast(F32), ALU.subtract).then_inc(dve_done, 1)
                did("router split")
                eng.wait_ge(pe_done, after("logits"))
                o = bank_of("logits")
                lg = small[:, 204:220]
                v.tensor_copy(lg, o[:, 0:16]).then_inc(dve_done, 1)
                eng.wait_ge(dve_done, did("read logits"))
                for tt in range(2):
                    v.max(small[:, 220:228], lg[:, 8 * tt:8 * tt + 8]).then_inc(dve_done, 1)
                    eng.wait_ge(dve_done, did())
                    v.max_index(idx8[:, :], small[:, 220:228], lg[:, 8 * tt:8 * tt + 8]).then_inc(dve_done, 1)
                    eng.wait_ge(dve_done, did())
                    v.tensor_copy(small[:, 42 + 2 * tt:44 + 2 * tt], idx8[:, 0:2]).then_inc(dve_done, 1)
                    eng.wait_ge(dve_done, did())
                    v.tensor_tensor(small[:, 38 + tt:39 + tt], small[:, 221:222], small[:, 220:221],
                                         ALU.subtract).then_inc(dve_done, 1)
                    eng.wait_ge(dve_done, did("dlogit"))
                eng.wait_ge(act_done, after("elogit"))
                v.tensor_scalar(small[:, 46:48], small[:, 40:42], 1.0, None, ALU.add).then_inc(dve_done, 1)
                eng.wait_ge(dve_done, did())
                v.reciprocal(small[:, 46:48], small[:, 46:48]).then_inc(dve_done, 1)
                eng.wait_ge(dve_done, did())
                v.tensor_tensor(small[:, 48:50], small[:, 40:42], small[:, 46:48], ALU.mult).then_inc(dve_done, 1)
                eng.wait_ge(dve_done, did())
                mask = rt[:, 0:2 * NE].rearrange("p (t e) -> p t e", e=NE)
                for tt in range(2):
                    for n in range(2):
                        v.tensor_scalar(rt[:, 48 + 8 * n:56 + 8 * n], iota8[:, :],
                                        small[:, 42 + 2 * tt + n:43 + 2 * tt + n], None,
                                        ALU.is_equal).then_inc(dve_done, 1)
                        eng.wait_ge(dve_done, did())
                    v.tensor_tensor(mask[:, tt, :], rt[:, 48:56], rt[:, 56:64], ALU.add).then_inc(dve_done, 1)
                    eng.wait_ge(dve_done, did("mask"))
                for tt in range(2):
                    v.tensor_scalar(comb[:, tt, :], iota8[:, :], small[:, 42 + 2 * tt:43 + 2 * tt],
                                         small[:, 46 + tt:47 + tt], ALU.is_equal, ALU.mult).then_inc(dve_done, 1)
                    eng.wait_ge(dve_done, did())
                    v.tensor_scalar(small[:, 228:236], iota8[:, :], small[:, 43 + 2 * tt:44 + 2 * tt],
                                         small[:, 48 + tt:49 + tt], ALU.is_equal, ALU.mult).then_inc(dve_done, 1)
                    eng.wait_ge(dve_done, did())
                    v.tensor_tensor(comb[:, tt, :], comb[:, tt, :], small[:, 228:236], ALU.add).then_inc(dve_done, 1)
                    eng.wait_ge(dve_done, did())

            def plan_passes():
                mask = rt[:, 0:2 * NE].rearrange("p (t e) -> p t e", e=NE)
                eng.wait_ge(pe_done, after("rank"))
                o = bank_of("rank")
                over, cum, one = rt[:, 16:24], rt[:, 24:32], rt[:, 32:40]
                v.memset(acc[:, :, :], 0.0).then_inc(dve_done, 1)
                did()
                v.tensor_scalar(over, o[:, 16:24], float(P), None, ALU.is_gt).then_inc(dve_done, 1)
                did()
                for tt in range(2):
                    v.scalar_tensor_tensor(out=place_s[:, tt, 0:NE], in0=o[:, NE * tt:NE * tt + NE], scalar=1.0,
                                           in1=mask[:, tt, :], op0=ALU.add, op1=ALU.mult).then_inc(dve_done, 1)
                    did("read rank")
                    v.tensor_copy(comb_s[:, tt, 0:NE], comb[:, tt, :]).then_inc(dve_done, 1)
                    did()
                v.tensor_copy(expert_f[:, 0:NE], iota8[:, :]).then_inc(dve_done, 1)
                eng.wait_ge(dve_done, did())
                v.tensor_copy(cum[:, 0:1], over[:, 0:1]).then_inc(dve_done, 1)
                eng.wait_ge(dve_done, did())
                for e in range(1, NE):
                    v.tensor_tensor(cum[:, e:e + 1], cum[:, e - 1:e], over[:, e:e + 1], ALU.add).then_inc(dve_done, 1)
                    eng.wait_ge(dve_done, did())
                for x in range(COLS - NE):
                    v.scalar_tensor_tensor(out=one, in0=cum, scalar=float(x + 1), in1=over, op0=ALU.is_equal,
                                           op1=ALU.mult).then_inc(dve_done, 1)
                    eng.wait_ge(dve_done, did())
                    for src, dst in ((iota8[:, :], expert_f[:, NE + x:NE + x + 1]),
                                     (place_s[:, 0, 0:NE], place_s[:, 0, NE + x:NE + x + 1]),
                                     (place_s[:, 1, 0:NE], place_s[:, 1, NE + x:NE + x + 1]),
                                     (comb[:, 0, :], comb_s[:, 0, NE + x:NE + x + 1]),
                                     (comb[:, 1, :], comb_s[:, 1, NE + x:NE + x + 1])):
                        v.tensor_tensor_reduce(rt[:, 40:48], one, src, 1.0, 0.0, ALU.mult, ALU.add,
                                               dst).then_inc(dve_done, 1)
                        eng.wait_ge(dve_done, did())
                v.tensor_scalar(place_s[:, :, 0:NE], place_s[:, :, 0:NE], 1.0, None, ALU.subtract).then_inc(dve_done, 1)
                did()
                v.tensor_scalar(place_s[:, :, NE:COLS], place_s[:, :, NE:COLS], 1.0 + P, None,
                                ALU.subtract).then_inc(dve_done, 1)
                eng.wait_ge(dve_done, did())
                v.tensor_copy(expert_i[:, :], expert_f[0:1, :]).then_inc(dve_done, 1)
                did()
                v.tensor_copy(second[:, :], cum[0:1, NE - 1:NE]).then_inc(dve_done, 1)
                eng.wait_ge(dve_done, did("plan"))

            def choose_tokens(i):
                if not (isinstance(i, int) and i == 0):
                    eng.wait_ge(x_pickT, i)
                for tt in range(2):
                    where = place_s[:, tt, i:i + 1] if isinstance(i, int) else place_s[:, tt, bass.ds(i, 1)]
                    last = v.tensor_scalar(pick[:, tt, :], iota, where, None, ALU.is_equal)
                last.then_inc(x_pick, 1)

            def gathered(i, par, q):
                eng.wait_ge(x_ghi, 2 * i + q + 1)
                for kk in range(4):
                    k = 4 * q + kk
                    last = v.tensor_scalar(gt[:, kk, :], PS[:, 3, P * kk:P * kk + P], gsc[:, 1, k, 1:2],
                                           mod[:, 24 + k, 1:2], ALU.mult, ALU.add)
                last.then_inc(x_gt, 1)
                eng.wait_ge(x_gt, 2 * i + q + 1)
                v.tensor_tensor(hT_lo[:, 4 * q:4 * q + 4, 256 + P * par:384 + P * par], gt,
                                hT_hi[:, 4 * q:4 * q + 4, 256 + P * par:384 + P * par].bitcast(F32),
                                ALU.subtract).then_inc(x_glo, 1)

            def add_up(i, tt):
                eng.wait_ge(x_z, 2 * i - 1 + tt)
                if not (isinstance(i, int) and i == 1):
                    eng.wait_ge(x_add, 2 * i - 2 + tt)
                weight = comb_s[:, tt, i - 1:i] if isinstance(i, int) else comb_s[:, tt, bass.ds(i - 1, 1)]
                for n in range(2):
                    a = acc[:, tt, 512 * n:512 * n + 512]
                    last = v.scalar_tensor_tensor(out=a, in0=PS[:, 6 + n, :], scalar=weight, in1=a,
                                                  op0=ALU.mult, op1=ALU.add)
                last.then_inc(x_add, 1)

            def expert_pass(i, par, follows):
                def low(j):
                    eng.wait_ge(x_hi, NGR * i + j + 1)
                    v.tensor_tensor(w_lo[:, j % RING, :], x_raw(NGR * par + j),
                                    w_hi[:, j % RING, :].bitcast(F32), ALU.subtract).then_inc(x_lo, 1)

                def low_turned(s):
                    eng.wait_ge(x_thi, FC * i + s + 1)
                    v.tensor_tensor(f_lo[:, 0:256], PS[:, 2, 0:256], f_hi[:, 0:256].bitcast(F32),
                                    ALU.subtract).then_inc(x_tlo, 1)

                for j in range(3):
                    low(j)
                for s in range(FC):
                    if s:
                        low_turned(s - 1)
                    if s + 1 < FC:
                        for j in range(fpos[("gu", s + 1, 0)] if s else RING, fpos[("gu", s + 1, 1)] + 1):
                            low(j)
                    eng.wait_ge(x_silu, FC * i + s + 1)
                    v.tensor_tensor(hh[:, s % 2, :], PS[:, s % 2, 256:512], sg[:, s % 2, :],
                                    ALU.mult).then_inc(x_h, 1)
                    low(fpos[("d", s, 0)])
                    if follows and s in (2, 4):
                        add_up(i, s // 4)
                    if s == 3:
                        choose_tokens(i + 1)
                    if s in (6, 8):
                        gathered(i + 1, 1 - par, s // 8)
                low_turned(FC - 1)

            for l in range(DEPTH):
                streams = layer_streams[l]
                modulation(l)
                filters(l)
                norm(l, 1, (0, 1))
                project_in(l, streams)
                hyena(l, streams)
                pooling(l, streams)
                latents(l, streams)
                attention(l, streams)
                project_out(l, streams)
                norm(l, 2, streams)
                if l == 0:
                    for s in (0, 1):
                        feed_forward(f"f{s}", gindex[("ffn", 0, 0, s)])
                        if s == 0:
                            diagonal(l, 1, 0)
                        for tt in range(2):
                            for n in range(2):
                                eng.wait_ge(pe_done, after(f"down f{s} {FC - 1}"))
                                dst = (acc if s == 0 else acc2)[:, tt, 512 * n:512 * n + 512]
                                v.tensor_copy(dst, PS[:, 4 + 2 * tt + n, :]).then_inc(dve_done, 1)
                                did(f"read y f{s} {tt} {n}")
                    for s in (0, 1):
                        if s == 1:
                            eng.wait_ge(pe_done, after(f"gate {l} 1 0 1"))
                            diagonal(l, 1, 1)
                        eng.wait_ge(act_done, after(f"gb {l} 1 {s}"))
                        eng.wait_ge(dve_done, did.count)
                        src = acc if s == 0 else acc2
                        for tt in range(2):
                            v.tensor_tensor(src[:, tt, :], src[:, tt, :], gbf, ALU.mult).then_inc(dve_done, 1)
                            eng.wait_ge(dve_done, did())
                            v.tensor_tensor(X[:, 2 * s + tt, :], X[:, 2 * s + tt, :], src[:, tt, :], ALU.add).then_inc(dve_done, 1)
                            eng.wait_ge(dve_done, did())
                        did.name(f"res {l} 1 {s}")
                    did.name("layer 0")
                else:
                    choose()
                    diagonal(l, 1, 1)
                    for tt in range(2):
                        eng.wait_ge(act_done, after("xhi"))
                        v.tensor_tensor(hT_lo[:, :, P * tt:P * tt + P],
                                        xn[:, 2 + tt, :].rearrange("p (k c) -> p k c", c=P),
                                        hT_hi[:, :, P * tt:P * tt + P].bitcast(F32), ALU.subtract).then_inc(dve_done, 1)
                        did("xlo")
                    plan_passes()
                    passes = NE + eng.value_load(second[0:1, 0:1], min_val=0, max_val=SLOTS - NE)
                    choose_tokens(0)
                    gathered(0, 0, 0)
                    gathered(0, 0, 1)
                    expert_pass(0, 0, False)
                    with eng.Fori(0, (SLOTS - 1) // 2) as j:
                        for odd in (1, 0):
                            i = 2 * j + (1 if odd else 2)
                            with eng.If(i < passes):
                                expert_pass(i, odd, True)
                    add_up(passes, 0)
                    add_up(passes, 1)
                    eng.wait_ge(x_add, 2 * passes)
                    eng.wait_ge(act_done, after(f"gb {l} 1 1"))
                    for tt in range(2):
                        v.tensor_tensor(acc[:, tt, :], acc[:, tt, :], gbf, ALU.mult).then_inc(dve_done, 1)
                        eng.wait_ge(dve_done, did())
                        v.tensor_tensor(X[:, 2 + tt, :], X[:, 2 + tt, :], acc[:, tt, :], ALU.add).then_inc(dve_done, 1)
                        eng.wait_ge(dve_done, did())
            for tt in range(2):
                v.tensor_tensor_reduce(acc[:, tt, :], X[:, 2 + tt, :], X[:, 2 + tt, :], 1.0, 0.0, ALU.mult,
                                            ALU.add, small[:, 34 + tt:35 + tt]).then_inc(dve_done, 1)
                eng.wait_ge(dve_done, did("ssf"))
            eng.wait_ge(act_done, after("stdf"))
            v.reciprocal(small[:, 36:38], small[:, 36:38]).then_inc(dve_done, 1)
            eng.wait_ge(dve_done, did())
            for tt in range(2):
                v.tensor_scalar(acc[:, tt, :], X[:, 2 + tt, :], small[:, 36 + tt:37 + tt], None, ALU.mult).then_inc(dve_done, 1)
                eng.wait_ge(dve_done, did())
                v.tensor_tensor(acc[:, tt, :], acc[:, tt, :], fing, ALU.mult).then_inc(dve_done, 1)
                eng.wait_ge(dve_done, did(f"out {tt}"))

        @blk.sync
        def _(eng):
            for g, (kind, e, i) in enumerate(plan):
                w = width(kind)
                if g >= RING:
                    eng.wait_ge(dve_done, after(f"lo {g - RING}"))
                eng.dma_start(raw[:, g % RING, 0:w], source(kind, e, i)).then_inc(raw_full[g % RING], 16)
            def expert_stream(i, par, pair, expert):
                for j in range(NGR):
                    n = NGR * par + j
                    if not isinstance(i, int) or j >= XRING:
                        eng.wait_ge(x_lo, NGR * i + j + 1 - XRING)
                    elif j < RING:
                        eng.wait_ge(dve_done, after(f"lo {NG - RING + (j - NG) % RING}"))
                    else:
                        eng.wait_ge(dve_done, after("projected 1"))
                    src = io["moe"][0, j] if expert is None else io["moe"][bass.ds(expert, 1), j].rearrange(
                        "a p n -> (a p) n")
                    eng.dma_start(x_raw(n), src).then_inc(x_full[n % XRING], 16)

            expert_stream(0, 0, 0, None)
            eng.wait_ge(dve_done, after("plan"))
            passes = NE + eng.value_load(second[0:1, 0:1], min_val=0, max_val=SLOTS - NE)
            with eng.Fori(0, (SLOTS - 1) // 2) as j:
                for odd in (1, 0):
                    i = 2 * j + (1 if odd else 2)
                    with eng.If(i < passes):
                        expert = eng.value_load(expert_i[0:1, bass.ds(i, 1)], min_val=0, max_val=NE - 1)
                        expert_stream(i, odd, j, expert)
            stored = loaded["stored"][0]
            for tt in range(2):
                eng.wait_ge(dve_done, after(f"out {tt}"))
                eng.dma_start(io["y"][P * tt:P * tt + P, :], acc[:, tt, :]).then_inc(stored, 16)
            eng.wait_ge(stored, 32)

        @blk.gpsimd
        def _(eng):
            def load(name, *pairs):
                s = loaded[name][0]
                for dst, src in pairs:
                    eng.dma_start(dst, src).then_inc(s, 16)
                assert loaded[name][1] == 16 * len(pairs)

            load("start", *((X[:, t, :], io["x"][P * t:P * t + P, :]) for t in range(NT)),
                 (par[:, :, :], io["par"]), (ident[:, :], io["ident"]), (ones[:, :], io["ones"]), (sel[:, :], io["sel"]),
                 (cvec[:, :, :], io["cvec"]), (iota8[:, :], io["iota8"]))
            for l in range(DEPTH):
                if l:
                    eng.wait_ge(dve_done, after("layer 0"))
                load(f"hy {l}", (hyc, io["hyc"]), (fw, io["fw"][l]))
                eng.wait_ge(dve_done, after(f"hyena {l}"))
                eng.wait_ge(pe_done, after(f"y {l} 1"))
                eng.wait_ge(pe_done, after(f"zT {l} 1"))
                eng.wait_ge(act_done, after(f"mixhi {l} 1"))
                load(f"pool {l}", (A(0, 2048), io["pm"]), (pwts[0:GROUP], io["pw"][l]))
                load(f"mla {l}", (A(7936, 3072), io["wuq"][l]), (A(11008, 2048), io["wukv"][l]), (A(19712, 512), io["ropeq"]),
                     (A(20224, 128), io["ropek"]))
            eng.wait_ge(act_done, after("mixhi 1 7"))
            load("route", (router, io["router"]), (iota, io["iota"]), (before, io["before"]), (fing, io["fing"]))


def lay(inputs):
    f = lambda n: np.asarray(inputs[n])
    c = np.ascontiguousarray
    io = {}
    io["x"] = c(np.concatenate([f("ctx")[0], f("x")[0]], axis=0))
    io["cvec"] = c(np.stack([f("c_ctx"), f("c")[0]], axis=-1).reshape(KD, P, 2).transpose(1, 0, 2))
    io["ada"] = c(f("w_ada").reshape(DEPTH, 2, 4, P, 12, 512).transpose(0, 4, 1, 3, 2, 5).reshape(DEPTH, 24, P, GRAN))
    w_in = f("w_in")
    io["ina"] = c(w_in[:, :, :3 * HY].reshape(DEPTH, KD, P, 3, 256).transpose(0, 3, 2, 1, 4).reshape(DEPTH, 3, P, GRAN))
    a = w_in.shape[2] - ROPE
    inb = np.concatenate([w_in[:, :, 3 * HY:], w_in[:, :, a + ROPE // 2:], w_in[:, :, a:a + ROPE // 2]], axis=2)
    io["inb"] = c(inb.reshape(DEPTH, 2, 4, P, 2, HB).transpose(0, 4, 1, 3, 2, 5).reshape(DEPTH, 4, P, 4 * HB))
    io["out"] = c(f("w_out").reshape(DEPTH, 2, 4, P, 2, 512).transpose(0, 4, 1, 3, 2, 5).reshape(DEPTH, 4, P, GRAN))

    def swiglu(wg, wu, wd):
        n = wg.shape[0]
        out = np.empty((n, 3 * FC, P, GRAN), wg.dtype)
        gu = out.reshape(n, 3 * FC, P, 4, 2, 256)
        g6, u6 = (w.reshape(n, 2, 4, P, FC, 256) for w in (wg, wu))
        d5 = wd.reshape(n, FC, 2, P, D)
        for i, (kind, s, half) in enumerate(ffn_order()):
            if kind == "gu":
                gu[:, i, :, :, 0, :] = g6[:, half, :, :, s, :].transpose(0, 2, 1, 3)
                gu[:, i, :, :, 1, :] = u6[:, half, :, :, s, :].transpose(0, 2, 1, 3)
            else:
                out[:, i] = d5[:, s].transpose(0, 2, 1, 3).reshape(n, P, GRAN)
        return out

    io["ffn"] = swiglu(f("ffn_wg"), f("ffn_wu"), f("ffn_wd"))
    io["moe"] = swiglu(f("moe_wg")[0], f("moe_wu")[0], f("moe_wd")[0])
    io["router"] = c(f("moe_router")[0].reshape(KD, P, NE).transpose(1, 0, 2))
    par = np.zeros((P, DEPTH, NPAR), np.float32)

    def put(name, a):
        lo, hi = PAR[name]
        par[:a.shape[-1], :, lo:hi] = a.reshape(DEPTH, hi - lo, a.shape[-1]).transpose(2, 0, 1)

    for name, src in (("g1", "norm1_g"), ("g2", "norm2_g"), ("bada", "b_ada"), ("qg", "q_norm_g"), ("kvg", "kv_norm_g"),
                      ("sw", "hy_short_w"), ("sb", "hy_short_b"), ("hyb", "hy_bias"), ("psc", "pool_scale")):
        put(name, f(src).reshape(DEPTH, -1, P))
    for name, src in (("b1", "filt_b1"), ("f1", "filt_freq1"), ("b2", "filt_b2"), ("f2", "filt_freq2")):
        put(name, f(src).reshape(DEPTH, 1, FH))
    io["par"] = par
    uq = f("w_uq").reshape(DEPTH, KQ, P, HEADS, NOPE + ROPE)
    uq = np.concatenate([uq, uq[..., NOPE + ROPE // 2:], uq[..., NOPE:NOPE + ROPE // 2]], axis=-1)
    io["wuq"] = c(uq.transpose(0, 2, 1, 3, 4).reshape(DEPTH, P, KQ * HEADS * P))
    ukv = f("w_ukv").reshape(DEPTH, KKV, P, HEADS, 2, NOPE)
    io["wukv"] = c(ukv.transpose(0, 2, 1, 4, 3, 5).reshape(DEPTH, P, KKV * 1024))
    io["pw"] = c(f("pool_w").transpose(0, 2, 1, 3))
    fw = np.zeros((DEPTH, P, 640), np.float32)
    fw[:, :FE, 0:64] = f("filt_w1")
    fw[:, :FH, 64:128] = f("filt_w2")
    fw[:, :FH, 128:640] = f("filt_w3")
    io["fw"] = fw
    io["iota"] = c(np.broadcast_to(np.arange(P, dtype=np.float32), (P, P)))
    io["before"] = np.triu(np.ones((P, P), np.float32), 1)
    io["fing"] = c(np.broadcast_to(f("final_g"), (P, D)))

    t = np.arange(L)
    fr = np.arange(L)
    sign = (-1.0) ** t
    ang = 2 * np.pi * ((np.outer(t, fr)) % (2 * L)) / (2 * L)
    C, S = np.cos(ang), np.sin(ang)
    Sn, Cn = S.copy(), C.copy()
    Sn[:, 0], Cn[:, 0] = sign, sign
    wt = np.full(L, 2.0 / (2 * L))
    wt[0] = 1.0 / (2 * L)
    tiles = lambda m: m.reshape(2, P, -1).transpose(1, 0, 2).reshape(P, -1)
    tt = (t / (L - 1)).astype(np.float32)
    deltas = np.linspace(math.log(1e-2) / 1.5, math.log(1e-2) / 0.3, HY)
    dec = np.exp(-tt[:, None].astype(np.float64) * np.abs(deltas))
    dec2 = np.concatenate([dec, dec], axis=1)
    dec2[0, HY:] = 0.0
    bands = (FE - 1) // 2
    w = 2.0 * math.pi * t[:, None] / L
    fb = np.linspace(1e-4, bands - 1, bands)[None, :]
    feat = np.concatenate([tt[:, None], np.cos(fb * w), -np.sin(fb * w)], axis=1)
    featT = np.zeros((P, L))
    featT[:FE] = feat.T
    io["hyc"] = np.concatenate([tiles(C), tiles(Sn), tiles(S[:, :P]), tiles(Cn[:, :P]), tiles((C * wt).T),
                                tiles((Sn * wt).T), tiles(dec2), featT], axis=1).astype(np.float32)
    pm = np.zeros((4, L, L))
    for g, win in enumerate(WINDOWS):
        for i in range(L):
            lo, hi = max(i - win // 2, 0), min(i + win // 2, L)
            pm[g, lo:hi, i] = 1.0 / (hi - lo)
            pm[g, i, i] -= 1.0
    io["pm"] = np.stack([tiles(m) for m in pm], axis=1).reshape(P, 4 * 2 * L).astype(np.float32)
    nf = ROPE // 4
    inv = 1.0 / (10000.0 ** (np.arange(nf) / nf))
    an = np.concatenate([(t // 64)[:, None] * inv, (t % 64)[:, None] * inv], axis=1)
    co, si = np.cos(an), np.sin(an)
    COS, SIN = np.concatenate([co, co], 1), np.concatenate([-si, si], 1)
    rq = np.zeros((P, 512), np.float32)
    rq[64:96, 0:256] = COS.T
    rq[96:128, 256:512] = SIN.T
    io["ropeq"] = rq
    io["ropek"] = np.concatenate([COS, SIN], axis=1).reshape(2, P, 64).transpose(1, 0, 2).astype(np.float32)
    io["ident"] = np.eye(P, dtype=np.float32)
    io["ones"] = np.ones((P, P), np.float32)
    io["sel"] = np.array([[1, 0], [0, 1], [1, 0], [0, 1]], np.float32)
    io["iota8"] = c(np.broadcast_to(np.arange(NE, dtype=np.float32), (P, NE)))
    return {k: c(v) for k, v in io.items()}


def kernel(**inputs):
    import concourse.bacc as _bacc
    from concourse.bass_utils import run_bass_kernel_spmd as _run

    data = lay(inputs)
    table = {"count": {}, "bank": {}, "final": False}
    for final in (False, True):
        nc = _bacc.Bacc("TRN2", target_bir_lowering=False, num_devices=1)
        io = {k: nc.dram_tensor(f"in_{k}", v.shape, F32, kind="ExternalInput").ap() for k, v in data.items()}
        io["y"] = nc.dram_tensor("out_y", (L, D), F32, kind="ExternalOutput").ap()
        build(nc, io, table)
        table["final"] = True
    r = _run(nc, [{f"in_{k}": v for k, v in data.items()}], core_ids=[0])
    return r.results[0]["out_y"].reshape(1, L, D)
```

```python
import math
from contextlib import ExitStack

import concourse.bass as bass
import numpy as np
from concourse import mybir

F32 = mybir.dt.float32
F32R = mybir.dt.float32r
U32 = mybir.dt.uint32
I32 = mybir.dt.int32
ALU = mybir.AluOpType
ACT = mybir.ActivationFunctionType
AX = mybir.AxisListType

P = 128
D = 1024
L = 256
DEPTH = 2
KD = D // P
NT = 4
HY = 256
POOLW = 256
WINDOWS = (2, 4, 8, 16)
GROUP = 64
HEADS = 8
NOPE, ROPE, VD = 64, 32, 64
QL, KVL = 384, 256
KQ, KKV = QL // P, KVL // P
SM_SCALE = (NOPE + ROPE) ** -0.5
INB = POOLW + QL + KVL + 2 * ROPE
HB = INB // 2
EPS = 1e-6
FF = 2816
NE = 8
FC = FF // 256
FH = 64
FE = 33
GRAN = 2048
RING = 3
FIRST_RING = 5
XRING = 2 * RING
SLOTS = NE + 3
COLS = SLOTS + 1
TWO_PI_A = 6.28125
TWO_PI_B = 2 * math.pi - TWO_PI_A
ROUND = 1.5 * 2 ** 23

PAR = {}
_at = 0
for _n, _w in (("g1", KD), ("g2", KD), ("bada", 48), ("qg", KQ), ("kvg", KKV), ("sw", 18), ("sb", 6), ("hyb", 2),
               ("psc", 2), ("b1", 1), ("f1", 1), ("b2", 1), ("f2", 1)):
    PAR[_n] = (_at, _at + _w)
    _at += _w
NPAR = _at


def stream_plan():
    plan = [("ada", 0, i) for i in range(24)]
    for l in range(DEPTH):
        plan += [("ina", l, i) for i in range(3)]
        plan += [("inb", l, i) for i in range(4)]
        plan += [("out", l, i) for i in range(4)]
        if l == 0:
            for p in range(2):
                for i, (kind, s, half) in enumerate(ffn_order()):
                    plan.append(("ffn", 0, i))
                    n = beside(p, s if kind == "gu" else s + 1)
                    if n is not None and (kind, half) in (("gu", 1), ("d", 0)):
                        plan.append(("ada", 1, 2 * n + (kind == "d")))
    return plan


def ffn_order():
    order = []
    for s in range(FC):
        order += [("gu", s, 0), ("gu", s, 1)]
        if s:
            order.append(("d", s - 1, 0))
    return order + [("d", FC - 1, 0)]


def beside(p, s):
    n = (FC - 1) * p + s - 1
    return n if 1 <= s < FC and n < 12 else None


class Steps:

    def __init__(self, table, key):
        self.table, self.key, self.count = table, key, 0

    def __call__(self, *names):
        self.count += 1
        for n in names:
            self.name(n)
        return self.count

    def name(self, n):
        if not self.table["final"]:
            self.table["count"][n] = (self.key, self.count)


def build(nc, io, table):
    with ExitStack() as ctx:
        def sb(name, shape, dt=F32):
            return ctx.enter_context(nc.sbuf_tensor(name, shape, dt))

        X = sb("X", [P, NT, D])
        hT_hi = sb("hT_hi", [P, KD, 512], F32R)
        hT_lo = sb("hT_lo", [P, KD, 512], F32R)
        raw = sb("raw", [P, RING, GRAN])
        w_hi = sb("w_hi", [P, RING, GRAN], F32R)
        w_lo = sb("w_lo", [P, RING, GRAN], F32R)
        f_hi = sb("f_hi", [P, 512], F32R)
        f_lo = sb("f_lo", [P, 512], F32R)
        par = sb("par", [P, DEPTH, NPAR])
        ident = sb("ident", [P, P])
        ones = sb("ones", [P, P])
        sel = sb("sel", [4, 2])
        cvec = sb("cvec", [P, KD, 2])
        csil = sb("csil", [P, KD, 2])
        mod = sb("mod", [P, 48, 2])
        gsc = sb("gsc", [P, 2, KD, 2])
        small = sb("small", [P, 256])
        r_hi = sb("r_hi", [P, KD, NE], F32R)
        r_lo = sb("r_lo", [P, KD, NE], F32R)
        iota8 = sb("iota8", [P, NE])
        idx8 = sb("idx8", [P, NE], U32)
        comb = sb("comb", [P, 2, NE])
        pick = f_hi[:, 256:512].rearrange("p (t c) -> p t c", c=P)
        expert_i = sb("expert_i", [1, COLS], I32)
        second = sb("second", [1, 1], I32)
        NA = 20352
        arena = sb("arena", [P, NA])
        PS = ctx.enter_context(nc.psum_tensor("PS", [P, 8, 512], F32))

        def sem(name):
            return ctx.enter_context(nc.semaphore(name))

        pe_done, act_done, dve_done = sem("pe_done"), sem("act_done"), sem("dve_done")
        raw_full = [sem(f"raw_full{i}") for i in range(FIRST_RING)]
        loaded = {"condition": (sem("condition_loaded"), 32), "start": (sem("start_loaded"), 16 * 8), "route": (sem("route_tables_loaded"), 64),
                "stored": (sem("stored"), 32)}
        for l in range(DEPTH):
            loaded[f"hy {l}"] = (sem(f"hyena_tables_loaded{l}"), 32)
            loaded[f"pool {l}"] = (sem(f"pool_tables_loaded{l}"), 32)
            loaded[f"mla {l}"] = (sem(f"attention_weights_loaded{l}"), 64)

        x_hi, x_lo, x_used = sem("x_hi"), sem("x_lo"), sem("x_used")
        x_silu, x_h = sem("x_silu"), sem("x_h")
        x_turned, x_thi, x_tlo = sem("x_turned"), sem("x_turned_hi"), sem("x_turned_lo")
        x_pick, x_gather = sem("x_pick"), sem("x_gather")
        x_gt = sem("x_gathered_modulated")
        x_ghi, x_glo = sem("x_gathered_hi"), sem("x_gathered_lo")
        x_pickT, x_pickTs = sem("x_pickT"), sem("x_pickT_saved")
        x_y, x_z, x_add = sem("x_y_saved"), sem("x_spread"), sem("x_added")
        NGR = 3 * FC
        x_full = [sem(f"x_full{i}") for i in range(XRING)]

        def after(name):
            return table["count"].get(name, (None, 1))[1]

        def reader_of(job):
            return act_done if table["count"].get("read " + job, ("act", 1))[0] == "act" else dve_done

        def bank_of(job):
            return PS[:, table["bank"][job], :]

        def A(off, *shape):
            n = int(np.prod(shape))
            assert off + n <= NA
            v = arena[:, off:off + n]
            if len(shape) == 1:
                return v
            letters = "abcd"[:len(shape)]
            kw = {c: s for c, s in zip(letters[1:], shape[1:])}
            return v.rearrange(f"p ({' '.join(letters)}) -> p {' '.join(letters)}", **kw)

        xn = A(0, NT, D)
        tn = A(4096, 2, 512)
        Bm = A(4096, NT, INB)
        uc = A(7936, 6, 512)
        upad = A(11008, 2, 2, 258)
        hyc = A(12040, 3840)
        Cf = A(12040, 2, 256)
        Sf = A(12552, 2, 256)
        Sz0 = A(13064, 2, 128)
        Cn0 = A(13320, 2, 128)
        IC = A(13576, 2, 256)
        IS = A(14088, 2, 256)
        decay = A(14600, 2, 512)
        featT = A(15624, 256)
        fw = A(15880, 640)
        fw1, fw2, fw3 = A(15880, 64), A(15944, 64), A(16008, 512)
        hfil = A(16520, 2, 512)
        hp, hm = A(17544, 2, 256), A(18056, 2, 256)
        HA, HBs = A(18568, 2, 256), A(19080, 2, 256)
        HD0 = A(19592, 256)
        farg = A(9216, 2, 256)
        fsc = A(9728, 2, 256)
        zT = A(0, 2, 512)
        Yc, Ys = A(1024, 2, 512), A(2048, 2, 512)
        ytmp = A(3072, 2, 512)
        pm = A(14600, 4, 2, 256)
        dT = A(2048, 2, 512)
        junk = A(3072, QL)
        pwts = A(16648, 4, GROUP)
        cs1 = r_hi[:, :, 0:4]
        mod1 = A(20224, 48, 2)
        row4 = arena[0:4, 11008:12032].rearrange("p (a b) -> p a b", b=512)
        wuq = A(7936, KQ, HEADS, P)
        wukv = A(11008, KKV, 1024)
        cqT = A(13056, KQ, 512)
        ckvT = A(14592, KKV, 512)
        qT = A(15616, HEADS, 512)
        ropeq = A(19712, 512)
        ropek = A(20224, 2, 64)
        KT = A(0, HEADS, 512)
        V = A(4096, NT, 512)
        qtmp = A(6144, 256)
        att = A(7936, NT, 512)
        prob = A(9984, 2, 512)
        probT = A(11008, 2, 512)
        gbc = A(12032, 2, D)
        diag = [A(6656, 8, P), A(14080, 8, P)]
        rtmp = A(15104, 2, 512)
        sg = A(4096, 2, 256)
        hh = A(4608, 2, 256)
        acc = A(5120, 2, D)
        gbf = A(7168, D)
        fdiag = A(8192, 8, P)
        ftmp = A(9216, 2, 512)
        ysb = A(9216, D)
        pickT = A(10240, 2, 256)
        rt = A(11264, 64)
        comb_s, place_s, expert_f = A(11328, 2, COLS), A(11352, 2, COLS), A(11376, COLS)
        gt = A(11520, 4, P)
        iota = A(16384, P)
        before = A(16512, P)
        fing = A(16640, D)
        router = A(17664, KD, NE)
        first_raw = [A(4096, GRAN), A(6144, GRAN)]
        more_raw = [A(12032, GRAN), A(14080, GRAN), A(17728, GRAN)]

        def x_raw(n):
            n = n % XRING
            return raw[:, n, :] if n < RING else more_raw[n - RING]

        acc2 = A(2048, 2, D)

        plan = stream_plan()
        gindex = {}
        counts = {}
        for g, (kind, e, i) in enumerate(plan):
            n = counts.get((kind, e, i), 0)
            counts[(kind, e, i)] = n + 1
            gindex[(kind, e, i, n)] = g
        NG = len(plan)
        place, use, before_it, users = [], [], [], [[] for _ in range(FIRST_RING)]
        for g in range(NG):
            p = g % (FIRST_RING if g < 24 else RING)
            place.append(p)
            use.append(len(users[p]) + 1)
            before_it.append(users[p][-1] if users[p] else None)
            users[p].append(g)

        def raw_at(g):
            return raw[:, place[g], :] if place[g] < RING else first_raw[place[g] - RING]

        order = ffn_order()
        fpos = {x: i for i, x in enumerate(order)}

        def width(kind):
            return 4 * HB if kind == "inb" else GRAN

        def source(kind, e, i):
            return io[kind][e, i]

        blk = ctx.enter_context(nc.Block())

        def last_group(p, s):
            n = beside(p, s - 1) if s else (beside(p - 1, FC - 1) if p else None)
            return n

        layer_streams = {0: (0, 1), 1: (1,)}

        def tiles_of(streams):
            return [2 * s + j for s in streams for j in range(2)]

        def span(streams):
            return slice(256 * streams[0], 512)

        @blk.tensor
        def _(eng):
            did = Steps(table, "pe")
            state = {"next": 0, "last": [None] * 8}

            def bank(job, b=None):
                if b is None:
                    b = state["next"]
                    state["next"] = (b + 1) % 8
                if state["last"][b]:
                    eng.wait_ge(reader_of(state["last"][b]), after("read " + state["last"][b]))
                state["last"][b] = job
                table["bank"][job] = b
                return PS[:, b, :]

            mm = nc.tensor.matmul

            def granule(g):
                eng.wait_ge(dve_done, after(f"lo {g}"))
                return w_hi[:, g % RING, :], w_lo[:, g % RING, :]

            def split3(out, s_hi, s_lo, m_hi, m_lo, start, stop):
                mm(out, s_hi, m_hi, start=start, stop=False)
                mm(out, s_hi, m_lo, start=False, stop=False)
                return mm(out, s_lo, m_hi, start=False, stop=stop)

            def group(l, n, half, o):
                c = cs1 if l else hT_hi
                g = gindex[("ada", l, 2 * n + half, 0)]
                hi, lo = granule(g)
                for k in range(4):
                    kk = 4 * half + k
                    mm(o[0:4, :], c[:, kk, 0:4], hi[:, 512 * k:512 * k + 512], start=kk == 0, stop=False)
                    i = mm(o[0:4, :], c[:, kk, 0:4], lo[:, 512 * k:512 * k + 512], start=False, stop=kk == 7)
                i.then_inc(pe_done, 1)
                did(f"used {g}", f"ada {l} {n}")

            def modulation():
                eng.wait_ge(dve_done, after("cs 0"))
                for n in range(12):
                    o = bank(f"ada 0 {n}")
                    for half in range(2):
                        group(0, n, half, o)
                    if n:
                        turn(0, n - 1)
                    filters(0, n)
                turn(0, 11)

            def turn(l, n):
                eng.wait_ge(act_done, after(f"row {l} {n}"))
                o = bank(f"modT {l} {n}", 3 if l else None)
                for j in range(4):
                    i = mm(o[:, 2 * j:2 * j + 2], row4[:, n % 2, P * j:P * j + P], sel[:, :], start=True, stop=True)
                i.then_inc(pe_done, 1)
                did(f"modT {l} {n}")

            def filters(l, n):
                b = 3 if l else None
                if n == 3:
                    eng.wait_ge(*loaded[f"hy {l}"])
                    mm(bank(f"f1 {l}", b)[0:FH, 0:L], fw1[0:FE, :], featT[0:FE, :], start=True, stop=True).then_inc(pe_done, 1)
                    did(f"f1 {l}")
                if n == 4:
                    eng.wait_ge(act_done, after(f"sin1 {l}"))
                    mm(bank(f"f2 {l}", b)[0:FH, 0:L], fw2[0:FH, :], farg[0:FH, 0, :], start=True, stop=True).then_inc(pe_done, 1)
                    did(f"f2 {l}")
                if n in (5, 6):
                    t = n - 5
                    eng.wait_ge(act_done, after(f"sin2 {l}"))
                    mm(bank(f"f3 {l} {t}", b), farg[0:FH, 1, P * t:P * t + P], fw3[0:FH, :], start=True, stop=True).then_inc(pe_done, 1)
                    did(f"f3 {l} {t}")
                if n == 7:
                    eng.wait_ge(*loaded["start"])
                    eng.wait_ge(dve_done, after(f"habs {l}"))
                    o = bank(f"fn {l}", b)
                    for ct in range(2):
                        for t in range(2):
                            i = mm(o[:, ct:ct + 1], fsc[:, t, P * ct:P * ct + P], ones[:, 0:1], start=t == 0, stop=t == 1)
                    i.then_inc(pe_done, 1)
                    did(f"fn {l}")
                if n in (8, 9):
                    ft = n - 8
                    s = slice(P * ft, P * ft + P)
                    o = bank(f"fA {l} {ft}", b)
                    for t in range(2):
                        mm(o[:, 0:L], Cf[:, t, s], hp[:, t, :], start=t == 0, stop=t == 1)
                    for t in range(2):
                        basis = Sz0[:, t, :] if ft == 0 else Sf[:, t, s]
                        i = mm(o[:, L:2 * L], basis, hm[:, t, :], start=t == 0, stop=t == 1)
                    i.then_inc(pe_done, 1)
                    did(f"fA {l} {ft}")
                if n == 10:
                    o = bank(f"fD {l}", b)
                    for t in range(2):
                        i = mm(o[:, 0:L], Cn0[:, t, :], hp[:, t, :], start=t == 0, stop=t == 1)
                    i.then_inc(pe_done, 1)
                    did(f"fD {l}")

            def norm_turn(l, w, streams):
                for k in range(KD):
                    for t in tiles_of(streams):
                        eng.wait_ge(dve_done, after(f"xn {l} {w} {t}"))
                    o = bank(f"nT {l} {w} {k}")
                    for t in tiles_of(streams):
                        i = nc.tensor.transpose(o[:, P * t:P * t + P], xn[:, t, P * k:P * k + P], ident[:, :])
                    i.then_inc(pe_done, 1)
                    did(f"nT {l} {w} {k}")

            def project_in(l, streams):
                sp = span(streams)
                for ct in range(6):
                    g = gindex[("ina", l, ct // 2, 0)]
                    hi, lo = granule(g)
                    o = bank(f"u {l} {ct}")
                    for k in range(KD):
                        if ct == 0:
                            eng.wait_ge(dve_done, after(f"hT {l} 1 {k}"))
                        s = slice(256 * k + P * (ct % 2), 256 * k + P * (ct % 2) + P)
                        i = split3(o[:, sp], hi[:, s], lo[:, s], hT_hi[:, k, sp], hT_lo[:, k, sp], k == 0, k == 7)
                    i.then_inc(pe_done, 1)
                    did(f"u {l} {ct}", f"used {g}")
                for b in range(2):
                    ts = tiles_of(streams) if b == 0 else range(NT)
                    os = {t: bank(f"B {l} {b} {t}") for t in ts}
                    for half in range(2):
                        g = gindex[("inb", l, 2 * b + half, 0)]
                        hi, lo = granule(g)
                        for t in ts:
                            for k in range(4):
                                kk, s = 4 * half + k, slice(HB * k, HB * k + HB)
                                i = split3(os[t][:, 0:HB], hT_hi[:, kk, P * t:P * t + P], hT_lo[:, kk, P * t:P * t + P],
                                           hi[:, s], lo[:, s], kk == 0, kk == 7)
                            if half:
                                i.then_inc(pe_done, 1)
                                did(f"B {l} {b} {t}")
                        if half:
                            did.name(f"used {g}")
                        else:
                            i.then_inc(pe_done, 1)
                            did(f"used {g}")

            def hyena(l, streams):
                sp = span(streams)
                n = 256 * len(streams)
                for ct in range(2):
                    eng.wait_ge(dve_done, after(f"z {l} {ct}"))
                    o = bank(f"zT {l} {ct}")
                    for j, s in enumerate(streams):
                        for t in range(2):
                            i = nc.tensor.transpose(o[:, 256 * s + P * t:256 * s + P * t + P],
                                                    uc[:, 2 + ct, 256 * s + P * t:256 * s + P * t + P], ident[:, :])
                    i.then_inc(pe_done, 1)
                    did(f"zT {l} {ct}")
                for ft in range(2):
                    for nm, basis in (("c", Cf), ("s", Sf)):
                        eng.wait_ge(act_done, after(f"zTs {l} 0"))
                        eng.wait_ge(act_done, after(f"zTs {l} 1"))
                        o = bank(f"Z{nm} {l} {ft}")
                        for t in range(2):
                            i = mm(o[:, sp], basis[:, t, P * ft:P * ft + P], zT[:, t, sp], start=t == 0, stop=t == 1)
                        i.then_inc(pe_done, 1)
                        did(f"Z{nm} {l} {ft}")
                eng.wait_ge(dve_done, after(f"Y {l}"))
                for ct in range(2):
                    o = bank(f"y {l} {ct}")
                    for s in streams:
                        for ft in range(2):
                            a = slice(256 * s + P * ct, 256 * s + P * ct + P)
                            mm(o[:, 256 * s:256 * s + 256], Yc[:, ft, a], IC[:, ft, :], start=ft == 0, stop=False)
                            i = mm(o[:, 256 * s:256 * s + 256], Ys[:, ft, a], IS[:, ft, :], start=False, stop=ft == 1)
                    i.then_inc(pe_done, 1)
                    did(f"y {l} {ct}")

            def pooling(l, streams):
                eng.wait_ge(*loaded[f"pool {l}"])
                sp = span(streams)
                for t in tiles_of(streams):
                    eng.wait_ge(act_done, after(f"Bs {l} 0 {t}"))
                for g in range(4):
                    o = bank(f"d {l} {g}")
                    for s in streams:
                        for t in range(2):
                            i = mm(o[0:GROUP, 256 * s:256 * s + 256], Bm[:, 2 * s + t, GROUP * g:GROUP * g + GROUP],
                                   pm[:, g, t, :], start=t == 0, stop=t == 1)
                    i.then_inc(pe_done, 1)
                    did(f"d {l} {g}")
                for pair in range(2):
                    o = bank(f"yp {l} {pair}")
                    for j in range(2):
                        g = 2 * pair + j
                        eng.wait_ge(act_done, after(f"dT {l} {g}"))
                        i = mm(o[GROUP * j:GROUP * j + GROUP, sp], pwts[0:GROUP, g, :], dT[0:GROUP, g % 2, sp],
                               start=True, stop=True)
                        i.then_inc(pe_done, 1)
                        did(f"yp {l} {pair}", f"yp {l} {pair} {j}")

            def latents(l, streams):
                sp = span(streams)
                for k in range(KQ):
                    o = bank(f"cqT {l} {k}")
                    for t in tiles_of(streams):
                        eng.wait_ge(dve_done, after(f"cqn {l} {t}"))
                        i = nc.tensor.transpose(o[:, P * t:P * t + P], Bm[:, t, 256 + P * k:256 + P * k + P], ident[:, :])
                    i.then_inc(pe_done, 1)
                    did(f"cqT {l} {k}")
                for k in range(KKV):
                    o = bank(f"ckvT {l} {k}")
                    for t in range(NT):
                        eng.wait_ge(dve_done, after(f"ckvn {l} {t}"))
                        i = nc.tensor.transpose(o[:, P * t:P * t + P], Bm[:, t, 640 + P * k:640 + P * k + P], ident[:, :])
                    i.then_inc(pe_done, 1)
                    did(f"ckvT {l} {k}")
                o = bank(f"kpT {l}")
                for t in range(NT):
                    eng.wait_ge(dve_done, after(f"kpe {l}"))
                    i = nc.tensor.transpose(o[0:ROPE, P * t:P * t + P], Bm[:, t, 896:896 + ROPE], ident[:, :])
                i.then_inc(pe_done, 1)
                did(f"kpT {l}")
                for k in range(KQ):
                    eng.wait_ge(act_done, after(f"cqTs {l} {k}"))
                eng.wait_ge(*loaded[f"mla {l}"])
                for h in range(HEADS):
                    o = bank(f"q {l} {h}")
                    for k in range(KQ):
                        i = mm(o[:, sp], wuq[:, k, h, :], cqT[:, k, sp], start=k == 0, stop=k == KQ - 1)
                    i.then_inc(pe_done, 1)
                    did(f"q {l} {h}")
                for k in range(KKV):
                    eng.wait_ge(act_done, after(f"ckvTs {l} {k}"))
                for pr in range(4):
                    o = bank(f"k {l} {pr}")
                    for k in range(KKV):
                        i = mm(o, wukv[:, k, P * pr:P * pr + P], ckvT[:, k, :], start=k == 0, stop=k == KKV - 1)
                    i.then_inc(pe_done, 1)
                    did(f"k {l} {pr}")
                for t in range(NT):
                    o = bank(f"v {l} {t}")
                    for k in range(KKV):
                        i = mm(o, ckvT[:, k, P * t:P * t + P], wukv[:, k, 512:1024], start=k == 0, stop=k == KKV - 1)
                    i.then_inc(pe_done, 1)
                    did(f"v {l} {t}")

            def attention(l, streams):
                units = [(t, h) for t in tiles_of(streams) for h in range(HEADS)]

                def score(n):
                    t, h = units[n]
                    eng.wait_ge(dve_done, after(f"qTs {l} {h}"))
                    eng.wait_ge(act_done, after(f"KTs {l}"))
                    nk = 256 if t < 2 else 512
                    o = bank(f"s {l} {n}", n % 3)
                    mm(o[:, 0:nk], qT[0:96, h, P * t:P * t + P], KT[0:96, h, 0:nk], start=True, stop=True).then_inc(pe_done, 1)
                    did(f"s {l} {n}")

                def turn_p(n):
                    t, h = units[n]
                    eng.wait_ge(act_done, after(f"p {l} {n}"))
                    o = bank(f"pT {l} {n}", 3 + n % 3)
                    for b in range(2 if t < 2 else 4):
                        i = nc.tensor.transpose(o[:, P * b:P * b + P], prob[:, n % 2, P * b:P * b + P], ident[:, :])
                    i.then_inc(pe_done, 1)
                    did(f"pT {l} {n}")

                def pv(n):
                    t, h = units[n]
                    eng.wait_ge(dve_done, after(f"pTs {l} {n}"))
                    eng.wait_ge(act_done, after(f"Vs {l}"))
                    if h == 0:
                        state["pv"] = bank(f"pv {l} {t}", 6 + t % 2)
                    o = state["pv"]
                    nb = 2 if t < 2 else 4
                    for b in range(nb):
                        i = mm(o[:, VD * h:VD * h + VD], probT[:, n % 2, P * b:P * b + P], V[:, b, VD * h:VD * h + VD],
                               start=b == 0, stop=b == nb - 1)
                    i.then_inc(pe_done, 1)
                    did(f"pvn {l} {n}", *([f"pv {l} {t}"] if h == HEADS - 1 else []))

                score(0)
                for n in range(len(units)):
                    if n + 1 < len(units):
                        score(n + 1)
                    turn_p(n)
                    if n:
                        pv(n - 1)
                pv(len(units) - 1)
                for s in streams:
                    gates(l, 0, s)
                for k in range(4):
                    o = bank(f"aT {l} {k}")
                    for t in tiles_of(streams):
                        eng.wait_ge(dve_done, after(f"att {l} {t}"))
                        i = nc.tensor.transpose(o[:, P * t:P * t + P], att[:, t, P * k:P * k + P], ident[:, :])
                    i.then_inc(pe_done, 1)
                    did(f"aT {l} {k}")

            def gates(l, w, s, halves=(0, 1), b=None):
                for half in halves:
                    eng.wait_ge(dve_done, after(f"diag {l} {w} {s}"))
                    o = bank(f"gate {l} {w} {s} {half}", 2 * s + half if w == 0 else b)
                    for j in range(4):
                        k = 4 * half + j
                        dg = diag[s] if w == 0 else fdiag
                        i = mm(o[:, P * j:P * j + P], ones[:, :], dg[:, k, :], start=True, stop=True)
                    i.then_inc(pe_done, 1)
                    did(f"gate {l} {w} {s} {half}")

            def project_out(l, streams):
                for k in range(KD):
                    eng.wait_ge(dve_done, after(f"mix {l} {k}"))
                ts = tiles_of(streams)
                for n in range(2):
                    os = {t: bank(f"o {l} {n} {t}") for t in ts}
                    for half in range(2):
                        g = gindex[("out", l, 2 * n + half, 0)]
                        hi, lo = granule(g)
                        for t in ts:
                            for k in range(4):
                                kk, s = 4 * half + k, slice(512 * k, 512 * k + 512)
                                i = split3(os[t], hT_hi[:, kk, P * t:P * t + P], hT_lo[:, kk, P * t:P * t + P],
                                           hi[:, s], lo[:, s], kk == 0, kk == 7)
                            if half:
                                i.then_inc(pe_done, 1)
                                did(f"o {l} {n} {t}")
                        if half:
                            did.name(f"used {g}")
                        else:
                            i.then_inc(pe_done, 1)
                            did(f"used {g}")

            def feed_forward(name, stream):
                y = {}

                def gate_up(s, half, os):
                    if s == 0 and stream == 0:
                        for k in range(4 * half, 4 * half + 4):
                            eng.wait_ge(dve_done, after(f"hT 0 2 {k}"))
                    g = gindex[("ffn", 0, fpos[("gu", s, half)], stream)]
                    hi, lo = granule(g)
                    for tt in range(2):
                        t = 2 * stream + tt
                        for k in range(4):
                            kk, cs = 4 * half + k, slice(512 * k, 512 * k + 512)
                            i = split3(os[tt], hT_hi[:, kk, P * t:P * t + P], hT_lo[:, kk, P * t:P * t + P],
                                       hi[:, cs], lo[:, cs], kk == 0, kk == 7)
                        if half:
                            i.then_inc(pe_done, 1)
                            did(f"gu {name} {s} {tt}")
                    if half:
                        did.name(f"used {g}")
                    else:
                        i.then_inc(pe_done, 1)
                        did(f"used {g}")

                def turn_h(s):
                    o = bank(f"hh {name} {s}", 2)
                    for tt in range(2):
                        eng.wait_ge(dve_done, after(f"h {name} {s} {tt}"))
                        for f in range(2):
                            i = nc.tensor.transpose(o[:, 256 * f + P * tt:256 * f + P * tt + P],
                                                    hh[:, tt, P * f:P * f + P], ident[:, :])
                    i.then_inc(pe_done, 1)
                    did(f"hh {name} {s}")

                def down(s):
                    g = gindex[("ffn", 0, fpos[("d", s, 0)], stream)]
                    if s == 0:
                        for tt in range(2):
                            for n in range(2):
                                y[(tt, n)] = bank(f"y {name} {tt} {n}", 4 + 2 * tt + n)
                    hi, lo = granule(g)
                    eng.wait_ge(dve_done, after(f"fs {name} {s}"))
                    for f in range(2):
                        for tt in range(2):
                            a = slice(256 * f + P * tt, 256 * f + P * tt + P)
                            for n in range(2):
                                cs = slice(1024 * f + 512 * n, 1024 * f + 512 * n + 512)
                                i = split3(y[(tt, n)], f_hi[:, a], f_lo[:, a], hi[:, cs], lo[:, cs],
                                           s == 0 and f == 0, s == FC - 1 and f == 1)
                    i.then_inc(pe_done, 1)
                    did(f"used {g}", f"down {name} {s}")

                for s in range(FC):
                    os = [bank(f"gu {name} {s} {tt}", tt) for tt in range(2)]
                    n = beside(stream, s)
                    gate_up(s, 0, os)
                    if last_group(stream, s) is not None:
                        turn(1, last_group(stream, s))
                    if stream == 1 and s in (4, 5):
                        gates(0, 1, 0, (s - 4,), 3)
                    if stream == 1 and s in (8, 9):
                        gates(0, 1, 1, (s - 8,), 3)
                    if s:
                        turn_h(s - 1)
                    gate_up(s, 1, os)
                    if n is not None:
                        a = bank(f"ada 1 {n}", 3)
                        group(1, n, 0, a)
                    if s:
                        down(s - 1)
                    if n is not None:
                        group(1, n, 1, a)
                    if stream == 1:
                        filters(1, s)
                turn_h(FC - 1)
                down(FC - 1)

            def route():
                eng.wait_ge(dve_done, after("router split"))
                for k in range(KD):
                    eng.wait_ge(dve_done, after(f"hT 1 2 {k}"))
                o = bank("logits")
                for tt in range(2):
                    t = 2 + tt
                    for k in range(KD):
                        a = slice(P * t, P * t + P)
                        q = o[:, NE * tt:NE * tt + NE]
                        split3(q, hT_hi[:, k, a], hT_lo[:, k, a], r_hi[:, k, :], r_lo[:, k, :], k == 0, False)
                        i = mm(q, hT_lo[:, k, a], r_lo[:, k, :], start=False, stop=k == 7)
                i.then_inc(pe_done, 1)
                did("logits")

            def rank():
                eng.wait_ge(*loaded["route"])
                eng.wait_ge(dve_done, after("mask"))
                o = bank("rank")
                mask = rt[:, 0:2 * NE].rearrange("p (t e) -> p t e", e=NE)
                mm(o[:, 0:NE], before, mask[:, 0, :], start=True, stop=True)
                mm(o[:, NE:2 * NE], ones[:, :], mask[:, 0, :], start=True, stop=False)
                mm(o[:, NE:2 * NE], before, mask[:, 1, :], start=False, stop=True)
                mm(o[:, 2 * NE:3 * NE], ones[:, :], mask[:, 0, :], start=True, stop=False)
                mm(o[:, 2 * NE:3 * NE], ones[:, :], mask[:, 1, :], start=False, stop=True).then_inc(pe_done, 1)
                did("rank")

            def gather(i, par, q):
                if q == 0:
                    eng.wait_ge(x_pick, i + 1)
                    for part in ("hi", "lo"):
                        eng.wait_ge(act_done if part == "hi" else dve_done, after(f"x{part}"))
                if not (isinstance(i, int) and i == 0 and q == 0):
                    eng.wait_ge(x_glo, 2 * i + q)
                    if q == 0:
                        eng.wait_ge(x_pickTs, i)
                first = isinstance(i, int) and i == 0 and q == 0
                o = PS[:, 3, :]
                for kk in range(4):
                    k = 4 * q + kk
                    for tt in range(2):
                        high = mm(o[:, P * kk:P * kk + P], hT_hi[:, k, P * tt:P * tt + P], pick[:, tt, :],
                                  start=tt == 0, stop=False)
                        if first and kk == 0:
                            high.then_inc(x_z, 1)
                        last = mm(o[:, P * kk:P * kk + P], hT_lo[:, k, P * tt:P * tt + P], pick[:, tt, :],
                                  start=False, stop=tt == 1)
                last.then_inc(x_gather, 1)

            def turn_pick(i, par):
                eng.wait_ge(x_glo, 2 * i + 2)
                for tt in range(2):
                    last = nc.tensor.transpose(PS[:, 3, P * tt:P * tt + P], pick[:, tt, :].bitcast(F32), ident[:, :])
                last.then_inc(x_pickT, 1)

            def spread(i, par, tt):
                eng.wait_ge(x_y, 2 * i)
                eng.wait_ge(x_pickTs, i)
                eng.wait_ge(x_add, 2 * i + tt)
                for n in range(2):
                    if par is None:
                        break
                    last = mm(PS[:, 6 + n, :], pickT[:, 1 - par, P * tt:P * tt + P], ysb[:, 512 * n:512 * n + 512],
                              start=True, stop=True)
                if par is None:
                    for odd in range(2):
                        with eng.If((i & 1) == odd):
                            for n in range(2):
                                last = mm(PS[:, 6 + n, :], pickT[:, 1 - odd, P * tt:P * tt + P],
                                          ysb[:, 512 * n:512 * n + 512], start=True, stop=True)
                            last.then_inc(x_z, 1)
                else:
                    last.then_inc(x_z, 1)

            def expert_pass(i, par, follows):
                xa = slice(256 + P * par, 384 + P * par)

                def granule_of(j):
                    eng.wait_ge(x_lo, NGR * i + j + 1)
                    return w_hi[:, j % RING, :], w_lo[:, j % RING, :]

                def gate_up(s, half):
                    j = fpos[("gu", s, half)]
                    hi, lo = granule_of(j)
                    if half == 0 and (follows or s >= 2):
                        eng.wait_ge(x_h, FC * i + max(s - 1, 0))
                    for k in range(4):
                        kk, cs = 4 * half + k, slice(512 * k, 512 * k + 512)
                        last = split3(PS[:, s % 2, :], hT_hi[:, kk, xa], hT_lo[:, kk, xa], hi[:, cs], lo[:, cs],
                                      kk == 0, kk == 7)
                    last.then_inc(x_used, 1)

                def turn_h(s):
                    eng.wait_ge(x_h, FC * i + s + 1)
                    if follows or s:
                        eng.wait_ge(x_tlo, FC * i + s)
                    for f in range(2):
                        last = nc.tensor.transpose(PS[:, 2, P * f:P * f + P], hh[:, s % 2, P * f:P * f + P],
                                                   ident[:, :])
                    last.then_inc(x_turned, 1)

                def down(s):
                    j = fpos[("d", s, 0)]
                    hi, lo = granule_of(j)
                    eng.wait_ge(x_tlo, FC * i + s + 1)
                    if s == 0 and follows:
                        eng.wait_ge(x_y, 2 * i)
                    for f in range(2):
                        a = slice(P * f, P * f + P)
                        for n in range(2):
                            cs = slice(1024 * f + 512 * n, 1024 * f + 512 * n + 512)
                            last = split3(PS[:, 4 + n, :], f_hi[:, a], f_lo[:, a], hi[:, cs], lo[:, cs],
                                          s == 0 and f == 0, s == FC - 1 and f == 1)
                    last.then_inc(x_used, 1)

                eng.wait_ge(x_glo, 2 * i + 2)
                for s in range(FC):
                    gate_up(s, 0)
                    if s:
                        turn_h(s - 1)
                    gate_up(s, 1)
                    if s:
                        down(s - 1)
                    if follows and s in (2, 4):
                        spread(i, par, s // 4)
                    if s in (6, 8):
                        gather(i + 1, 1 - par, s // 8)
                    if s == 10:
                        turn_pick(i + 1, 1 - par)
                turn_h(FC - 1)
                down(FC - 1)

            eng.wait_ge(*loaded["condition"])
            for l in range(DEPTH):
                streams = layer_streams[l]
                if l == 0:
                    modulation()
                norm_turn(l, 1, (0, 1))
                project_in(l, streams)
                hyena(l, streams)
                pooling(l, streams)
                latents(l, streams)
                attention(l, streams)
                project_out(l, streams)
                norm_turn(l, 2, streams)
                if l == 0:
                    for s in (0, 1):
                        feed_forward(f"f{s}", s)
                else:
                    route()
                    rank()
                    gates(l, 1, 1)
                    for b in range(8):
                        eng.wait_ge(reader_of(state["last"][b]), after("read " + state["last"][b]))
                    eng.wait_ge(dve_done, after("plan"))
                    passes = NE + eng.value_load(second[0:1, 0:1], min_val=0, max_val=SLOTS - NE)
                    gather(0, 0, 0)
                    gather(0, 0, 1)
                    turn_pick(0, 0)
                    expert_pass(0, 0, False)
                    with eng.Fori(0, (SLOTS - 1) // 2) as j:
                        for odd in (1, 0):
                            i = 2 * j + (1 if odd else 2)
                            with eng.If(i < passes):
                                expert_pass(i, odd, True)
                    spread(passes, None, 0)
                    spread(passes, None, 1)

        @blk.scalar
        def _(eng):
            did = Steps(table, "act")
            act = nc.scalar.activation
            split = {"next": 0}

            def upto(g):
                while split["next"] <= min(g, NG - 1):
                    n = split["next"]
                    w = width(plan[n][0])
                    if n >= RING:
                        eng.wait_ge(pe_done, after(f"used {n - RING}"))
                    eng.wait_ge(raw_full[place[n]], 16 * use[n])
                    nc.scalar.copy(w_hi[:, n % RING, 0:w], raw_at(n)[:, 0:w]).then_inc(act_done, 1)
                    did(f"hi {n}")
                    split["next"] += 1


            def condition(l):
                if l == 0:
                    eng.wait_ge(*loaded["condition"])
                    act(csil[:, :, :], cvec[:, :, :], ACT.Silu).then_inc(act_done, 1)
                    eng.wait_ge(act_done, did("csil"))
                nc.scalar.copy((cs1 if l else hT_hi)[:, :, 0:2], csil[:, :, :]).then_inc(act_done, 1)
                did(f"cshi {l}")

            def save_row(l, n):
                eng.wait_ge(pe_done, after(f"ada {l} {n}"))
                o = bank_of(f"ada {l} {n}")
                if n >= 2:
                    eng.wait_ge(pe_done, after(f"modT {l} {n - 2}"))
                nc.scalar.copy(row4[:, n % 2, :], o[0:4, :]).then_inc(act_done, 1)
                did(f"row {l} {n}", f"read ada {l} {n}")

            def modulation():
                condition(0)
                for n in range(12):
                    filters(0, n - 1)
                    upto(gindex[("ada", 0, 0, 0)] + 2 * n + 3)
                    if n == 9:
                        deviation(0, 1, (0, 1))
                    save_row(0, n)

            def filters(l, n):
                if n in (3, 4):
                    i = n - 2
                    eng.wait_ge(dve_done, after(f"arg{i} {l}"))
                    act(farg[0:FH, i - 1, :], fsc[0:FH, 0, :], ACT.Sin).then_inc(act_done, 1)
                    did(f"sin{i} {l}")
                if n in (5, 6):
                    t = n - 5
                    eng.wait_ge(dve_done, after(f"hfil {l} {t}"))
                    act(fsc[:, t, :], hfil[:, t, 0:L], ACT.Abs).then_inc(act_done, 1)
                    did()
                    if n == 6:
                        eng.wait_ge(pe_done, after(f"f3 {l} 1"))
                        for t in range(2):
                            act(farg[:, t, :], hfil[:, t, L:2 * L], ACT.Abs).then_inc(act_done, 1)
                            did(f"abs {l}")
                if n in (8, 9):
                    ft = n - 8
                    eng.wait_ge(pe_done, after(f"fA {l} {ft}"))
                    o = bank_of(f"fA {l} {ft}")
                    nc.scalar.copy(HA[:, ft, :], o[:, 0:L]).then_inc(act_done, 1)
                    did()
                    nc.scalar.copy(HBs[:, ft, :], o[:, L:2 * L]).then_inc(act_done, 1)
                    did(f"read fA {l} {ft}")
                if n == 10:
                    eng.wait_ge(pe_done, after(f"fD {l}"))
                    o = bank_of(f"fD {l}")
                    nc.scalar.copy(HD0, o[:, 0:L]).then_inc(act_done, 1)
                    did(f"read fD {l}", f"H {l}")

            def deviation(l, w, streams):
                eng.wait_ge(dve_done, after(f"ss {l} {w}"))
                ts = tiles_of(streams)
                a, b = ts[0], ts[-1] + 1
                act(small[:, 8 + a:8 + b], small[:, a:b], ACT.Sqrt, bias=epsb[:, 0:1], scale=1.0 / D).then_inc(act_done, 1)
                did(f"std {l} {w}")

            def norm(l, w, streams):
                if w == 2:
                    deviation(l, w, streams)
                    if l == 0:
                        upto(gindex[("ffn", 0, 0, 0)])
                for k in range(KD):
                    eng.wait_ge(pe_done, after(f"nT {l} {w} {k}"))
                    o = bank_of(f"nT {l} {w} {k}")
                    if k == 0:
                        eng.wait_ge(dve_done, after(f"gs {l}"))
                    for s in streams:
                        q = slice(256 * s, 256 * s + 256)
                        j = 3 * (w - 1)
                        act(hT_hi[:, k, q], o[:, q], ACT.Identity, bias=mod[:, 8 * j + k, s:s + 1],
                                 scale=gsc[:, w - 1, k, s:s + 1]).then_inc(act_done, 1)
                        did(f"hThi {l} {w} {k}")

            def project_in(l, streams):
                sp = span(streams)
                for ct in range(6):
                    upto(gindex[("ina", l, 0, 0)] + (ct // 2 + 1 if ct < 5 else 5))
                    eng.wait_ge(pe_done, after(f"u {l} {ct}"))
                    o = bank_of(f"u {l} {ct}")
                    if ct == 0:
                        eng.wait_ge(dve_done, after(f"upad {l}"))
                    if ct >= 2:
                        eng.wait_ge(dve_done, after(f"conv {l} {ct - 2}"))
                    for s in streams:
                        nc.scalar.copy(upad[:, ct % 2, s, 1:257], o[:, 256 * s:256 * s + 256]).then_inc(act_done, 1)
                        did(f"us {l} {ct}", f"read u {l} {ct}")
                for b in range(2):
                    upto(gindex[("inb", l, 2 * b + 1, 0)])
                    for t in (tiles_of(streams) if b == 0 else range(NT)):
                        eng.wait_ge(pe_done, after(f"B {l} {b} {t}"))
                        o = bank_of(f"B {l} {b} {t}")
                        nc.scalar.copy(Bm[:, t, HB * b:HB * b + HB], o[:, 0:HB]).then_inc(act_done, 1)
                        did(f"Bs {l} {b} {t}", f"read B {l} {b} {t}")

            def hyena(l, streams):
                sp = span(streams)
                for ct in range(2):
                    eng.wait_ge(pe_done, after(f"zT {l} {ct}"))
                    o = bank_of(f"zT {l} {ct}")
                    for s in streams:
                        for t in range(2):
                            nc.scalar.copy(zT[:, t, 256 * s + P * ct:256 * s + P * ct + P],
                                                o[:, 256 * s + P * t:256 * s + P * t + P]).then_inc(act_done, 1)
                            did(f"zTs {l} {ct}", f"read zT {l} {ct}")
                for ct in range(2):
                    eng.wait_ge(dve_done, after(f"yh {l} {ct}"))
                    nc.scalar.copy(hT_hi[:, ct, sp], ytmp[:, ct, sp]).then_inc(act_done, 1)
                    did(f"mixhi {l} {ct}")

            def pooling(l, streams):
                sp = span(streams)
                for g in range(4):
                    eng.wait_ge(pe_done, after(f"d {l} {g}"))
                    o = bank_of(f"d {l} {g}")
                    if g >= 2:
                        eng.wait_ge(pe_done, after(f"yp {l} {(g - 2) // 2} {g % 2}"))
                    nc.scalar.copy(dT[0:GROUP, g % 2, sp], o[0:GROUP, sp]).then_inc(act_done, 1)
                    did(f"dT {l} {g}", f"read d {l} {g}")
                for pair in range(2):
                    eng.wait_ge(pe_done, after(f"yp {l} {pair}"))
                    o = bank_of(f"yp {l} {pair}")
                    a = PAR["psc"][0] + pair
                    act(hT_hi[:, 2 + pair, sp], o[:, sp], ACT.Copy, scale=par[:, l, a:a + 1]).then_inc(act_done, 1)
                    did(f"mixhi {l} {2 + pair}")

            def latents(l, streams):
                sp = span(streams)
                eng.wait_ge(dve_done, after(f"ssq {l}"))
                act(small[:, 24:28], small[:, 16:20], ACT.Sqrt, bias=epsb[:, 0:1], scale=1.0 / QL).then_inc(act_done, 1)
                did()
                act(small[:, 28:32], small[:, 20:24], ACT.Sqrt, bias=epsb[:, 0:1], scale=1.0 / KVL).then_inc(act_done, 1)
                did(f"stdq {l}")
                for k in range(KQ):
                    eng.wait_ge(pe_done, after(f"cqT {l} {k}"))
                    o = bank_of(f"cqT {l} {k}")
                    a = PAR["qg"][0] + k
                    act(cqT[:, k, sp], o[:, sp], ACT.Copy, scale=par[:, l, a:a + 1]).then_inc(act_done, 1)
                    did(f"cqTs {l} {k}", f"read cqT {l} {k}")
                for k in range(KKV):
                    eng.wait_ge(pe_done, after(f"ckvT {l} {k}"))
                    o = bank_of(f"ckvT {l} {k}")
                    a = PAR["kvg"][0] + k
                    act(ckvT[:, k, :], o, ACT.Copy, scale=par[:, l, a:a + 1]).then_inc(act_done, 1)
                    did(f"ckvTs {l} {k}", f"read ckvT {l} {k}")
                eng.wait_ge(pe_done, after(f"kpT {l}"))
                o = bank_of(f"kpT {l}")
                for h in range(HEADS):
                    nc.scalar.copy(KT[64:96, h, :], o[0:ROPE, :]).then_inc(act_done, 1)
                    did(f"KTpe {l}", f"read kpT {l}")
                for pr in range(4):
                    eng.wait_ge(pe_done, after(f"k {l} {pr}"))
                    o = bank_of(f"k {l} {pr}")
                    for j in range(2):
                        nc.scalar.copy(KT[0:64, 2 * pr + j, :], o[64 * j:64 * j + 64, :]).then_inc(act_done, 1)
                        did(f"KTs {l}", f"read k {l} {pr}")
                for t in range(NT):
                    eng.wait_ge(pe_done, after(f"v {l} {t}"))
                    o = bank_of(f"v {l} {t}")
                    nc.scalar.copy(V[:, t, :], o).then_inc(act_done, 1)
                    did(f"Vs {l}", f"read v {l} {t}")

            def attention(l, streams):
                units = [(t, h) for t in tiles_of(streams) for h in range(HEADS)]
                for n, (t, h) in enumerate(units):
                    nk = 256 if t < 2 else 512
                    eng.wait_ge(pe_done, after(f"s {l} {n}"))
                    o = bank_of(f"s {l} {n}")
                    eng.wait_ge(dve_done, after(f"nmax {l} {n}"))
                    if n >= 2:
                        eng.wait_ge(pe_done, after(f"pT {l} {n - 2}"))
                    if n == 0:
                        eng.wait_ge(pe_done, after(f"q {l} {HEADS - 1}"))
                    if n == 2:
                        upto(gindex[("out", l, 2, 0)])
                    act(prob[:, n % 2, 0:nk], o[:, 0:nk], ACT.Exp, bias=small[:, 64 + n:65 + n], scale=SM_SCALE,
                             accum_out=small[:, 128 + n:129 + n]).then_inc(act_done, 1)
                    did(f"p {l} {n}", f"read s {l} {n}")
                for s in streams:
                    gates(l, 0, s)
                for k in range(4):
                    eng.wait_ge(pe_done, after(f"aT {l} {k}"))
                    o = bank_of(f"aT {l} {k}")
                    sp = span(streams)
                    nc.scalar.copy(hT_hi[:, 4 + k, sp], o[:, sp]).then_inc(act_done, 1)
                    did(f"mixhi {l} {4 + k}")

            def gates(l, w, s, halves=(0, 1)):
                for half in halves:
                    eng.wait_ge(pe_done, after(f"gate {l} {w} {s} {half}"))
                    o = bank_of(f"gate {l} {w} {s} {half}")
                    dst = gbc[:, s, 512 * half:512 * half + 512] if w == 0 else gbf[:, 512 * half:512 * half + 512]
                    if w == 1 and s == 1 and l == 0:
                        eng.wait_ge(dve_done, after("res 0 1"))
                    nc.scalar.copy(dst, o).then_inc(act_done, 1)
                    did(f"gb {l} {w} {s}", f"read gate {l} {w} {s} {half}")

            def project_out(l, streams):
                upto(gindex[("out", l, 3, 0)])

            def feed_forward(name, p):
                def high_turned(s):
                    eng.wait_ge(pe_done, after(f"hh {name} {s}"))
                    o = bank_of(f"hh {name} {s}")
                    if s:
                        eng.wait_ge(pe_done, after(f"down {name} {s - 1}"))
                    nc.scalar.copy(f_hi[:, :], o).then_inc(act_done, 1)
                    did(f"fhi {name} {s}")

                upto(gindex[("ffn", 0, 2, p)])
                for s in range(FC):
                    if s:
                        high_turned(s - 1)
                    if p == 1 and s in (4, 5):
                        gates(0, 1, 0, (s - 4,))
                    if p == 1 and s in (8, 9):
                        gates(0, 1, 1, (s - 8,))
                    if beside(p, s) is not None:
                        upto(gindex[("ada", 1, 2 * beside(p, s) + 1, 0)])
                    elif s + 1 < FC:
                        upto(gindex[("ffn", 0, fpos[("gu", s + 1, 1)], p)])
                    for tt in range(2):
                        eng.wait_ge(pe_done, after(f"gu {name} {s} {tt}"))
                        o = bank_of(f"gu {name} {s} {tt}")
                        act(sg[:, tt, :], o[:, 0:256], ACT.Silu).then_inc(act_done, 1)
                        did(f"sg {name} {s} {tt}")
                    if s + 1 < FC:
                        upto(gindex[("ffn", 0, fpos[("gu", s + 1, 1)], p)])
                    if beside(p, s) is not None:
                        save_row(1, beside(p, s))
                    upto(gindex[("ffn", 0, fpos[("d", s, 0)], p)])
                    if p == 1:
                        filters(1, s)
                if p == 0:
                    upto(gindex[("ffn", 0, 0, 1)])
                high_turned(FC - 1)
                upto(gindex[("ffn", 0, 1, 1) if p == 0 else ("ina", 1, 1, 0)])

            def first_high(j):
                eng.wait_ge(pe_done, after(f"used {NG - RING + j}"))
                eng.wait_ge(x_full[j], 16)
                nc.scalar.copy(w_hi[:, j, :], x_raw(j)).then_inc(x_hi, 1)

            def gathered(i, par, q):
                eng.wait_ge(x_gather, 2 * i + q + 1)
                for kk in range(4):
                    k = 4 * q + kk
                    last = act(hT_hi[:, k, 256 + P * par:384 + P * par], PS[:, 3, P * kk:P * kk + P], ACT.Identity,
                               bias=mod[:, 24 + k, 1:2], scale=gsc[:, 1, k, 1:2])
                last.then_inc(x_ghi, 1)

            def save_pick(i, par):
                eng.wait_ge(x_pickT, i + 1)
                nc.scalar.copy(pickT[:, par, :], PS[:, 3, 0:256]).then_inc(x_pickTs, 1)

            def save_y(i):
                eng.wait_ge(x_used, NGR * i)
                eng.wait_ge(x_z, 2 * i)
                for n in range(2):
                    nc.scalar.copy(ysb[:, 512 * n:512 * n + 512], PS[:, 4 + n, :]).then_inc(x_y, 1)

            def expert_pass(i, par, follows, pair):
                def high(j):
                    eng.wait_ge(x_used, NGR * i + j + 1 - RING)
                    n = NGR * par + j
                    eng.wait_ge(x_full[n % XRING], 16 * (FC * pair + n // XRING + 1))
                    nc.scalar.copy(w_hi[:, j % RING, :], x_raw(n)).then_inc(x_hi, 1)

                def high_turned(s):
                    eng.wait_ge(x_turned, FC * i + s + 1)
                    if follows or s:
                        j = fpos[("d", s - 1, 0)] + 1 if s else 0
                        eng.wait_ge(x_used, NGR * i + j)
                    nc.scalar.copy(f_hi[:, 0:256], PS[:, 2, 0:256]).then_inc(x_thi, 1)

                if follows:
                    for j in range(RING):
                        high(j)
                    save_y(i)
                for s in range(FC):
                    if s:
                        high_turned(s - 1)
                    if s + 1 < FC:
                        for j in range(fpos[("gu", s + 1, 0)] if s else RING, fpos[("gu", s + 1, 1)] + 1):
                            high(j)
                    eng.wait_ge(x_used, NGR * i + fpos[("gu", s, 1)] + 1)
                    act(sg[:, s % 2, :], PS[:, s % 2, 0:256], ACT.Silu).then_inc(x_silu, 1)
                    high(fpos[("d", s, 0)])
                    if s in (6, 8):
                        gathered(i + 1, 1 - par, s // 8)
                    if s == 10:
                        save_pick(i + 1, 1 - par)
                high_turned(FC - 1)

            epsb = small[:, 250:251]
            for l in range(DEPTH):
                streams = layer_streams[l]
                if l == 0:
                    eng.wait_ge(dve_done, after("eps"))
                    modulation()
                else:
                    deviation(1, 1, (0, 1))
                norm(l, 1, (0, 1))
                project_in(l, streams)
                hyena(l, streams)
                pooling(l, streams)
                latents(l, streams)
                attention(l, streams)
                project_out(l, streams)
                norm(l, 2, streams)
                if l == 0:
                    condition(1)
                    for s in (0, 1):
                        feed_forward(f"f{s}", s)
                else:
                    for j in range(RING):
                        first_high(j)
                    eng.wait_ge(*loaded["route"])
                    nc.scalar.copy(r_hi[:, :, :], router).then_inc(act_done, 1)
                    did("rhi")
                    eng.wait_ge(dve_done, after("dlogit"))
                    act(small[:, 40:42], small[:, 38:40], ACT.Exp).then_inc(act_done, 1)
                    did("elogit")
                    for tt in range(2):
                        eng.wait_ge(pe_done, after("logits"))
                        nc.scalar.copy(hT_hi[:, :, P * tt:P * tt + P],
                                       xn[:, 2 + tt, :].rearrange("p (k c) -> p k c", c=P)).then_inc(act_done, 1)
                        did("xhi")
                    gates(l, 1, 1)
                    eng.wait_ge(dve_done, after("plan"))
                    passes = NE + eng.value_load(second[0:1, 0:1], min_val=0, max_val=SLOTS - NE)
                    gathered(0, 0, 0)
                    gathered(0, 0, 1)
                    save_pick(0, 0)
                    expert_pass(0, 0, False, 0)
                    with eng.Fori(0, (SLOTS - 1) // 2) as j:
                        for odd in (1, 0):
                            i = 2 * j + (1 if odd else 2)
                            with eng.If(i < passes):
                                expert_pass(i, odd, True, j if odd else j + 1)
                    save_y(passes)
            eng.wait_ge(dve_done, after("ssf"))
            act(small[:, 36:38], small[:, 34:36], ACT.Sqrt, bias=epsb[:, 0:1], scale=1.0 / D).then_inc(act_done, 1)
            did("stdf")

        @blk.vector
        def _(eng):
            did = Steps(table, "dve")
            v = nc.vector
            split = {"next": 0}

            def upto(g):
                while split["next"] <= min(g, NG - 1):
                    n = split["next"]
                    w = width(plan[n][0])
                    eng.wait_ge(act_done, after(f"hi {n}"))
                    v.tensor_tensor(w_lo[:, n % RING, 0:w], raw_at(n)[:, 0:w],
                                         w_hi[:, n % RING, 0:w].bitcast(F32), ALU.subtract).then_inc(dve_done, 1)
                    did(f"lo {n}")
                    split["next"] += 1



            def condition(l):
                c = cs1 if l else hT_hi
                eng.wait_ge(act_done, after(f"cshi {l}"))
                v.tensor_tensor(c[:, :, 2:4], csil[:, :, :], c[:, :, 0:2].bitcast(F32), ALU.subtract).then_inc(dve_done, 1)
                did(f"cs {l}")

            def modulation():
                v.memset(small[:, :], 0.0).then_inc(dve_done, 1)
                eng.wait_ge(dve_done, did())
                v.memset(small[:, 250:251], EPS).then_inc(dve_done, 1)
                did("eps")
                condition(0)
                for n in range(12):
                    filters(0, n - 1)
                    upto(gindex[("ada", 0, 0, 0)] + 2 * n + 3)
                    if n == 0:
                        eng.wait_ge(*loaded["start"])
                    if n == 9:
                        squares(0, 1, (0, 1))
                    if n == 10:
                        normalise(0, 1, (0, 1))
                    if n:
                        bias_mod(0, n - 1)
                bias_mod(0, 11)
                scales(0)

            def scales(l):
                eng.wait_ge(dve_done, did.count)
                for w in range(2):
                    g0 = PAR["g1"][0] + KD * w
                    j = 3 * w + 1
                    for s in range(2):
                        v.scalar_tensor_tensor(out=gsc[:, w, :, s], in0=mod[:, 8 * j:8 * j + 8, s], scalar=1.0,
                                                    in1=par[:, l, g0:g0 + KD], op0=ALU.add, op1=ALU.mult).then_inc(dve_done, 1)
                        did(f"gs {l}")

            def bias_mod(l, n):
                eng.wait_ge(pe_done, after(f"modT {l} {n}"))
                o = bank_of(f"modT {l} {n}")
                b = PAR["bada"][0] + 4 * n
                for s in range(2):
                    q = o[:, 0:8].rearrange("p (j s) -> p j s", s=2)
                    v.tensor_tensor((mod1 if l else mod)[:, 4 * n:4 * n + 4, s], q[:, :, s], par[:, l, b:b + 4],
                                    ALU.add).then_inc(dve_done, 1)
                    did(f"read modT {l} {n}")

            def filters(l, n):
                if n in (3, 4):
                    i = n - 2
                    nm = f"f{i}"
                    eng.wait_ge(pe_done, after(f"{nm} {l}"))
                    o = bank_of(f"{nm} {l}")[0:FH, 0:L]
                    b, f = PAR[f"b{i}"][0], PAR[f"f{i}"][0]
                    ar, rt = fsc[0:FH, 0, :], fsc[0:FH, 1, :]
                    v.tensor_scalar(ar, o, par[0:FH, l, b:b + 1], par[0:FH, l, f:f + 1], ALU.add, ALU.mult).then_inc(dve_done, 1)
                    eng.wait_ge(dve_done, did(f"read {nm} {l}"))
                    v.tensor_scalar(rt, ar, 1 / (2 * math.pi), ROUND, ALU.mult, ALU.add).then_inc(dve_done, 1)
                    eng.wait_ge(dve_done, did())
                    v.tensor_scalar(rt, rt, ROUND, None, ALU.subtract).then_inc(dve_done, 1)
                    eng.wait_ge(dve_done, did())
                    v.scalar_tensor_tensor(out=ar, in0=rt, scalar=-TWO_PI_A, in1=ar, op0=ALU.mult, op1=ALU.add).then_inc(dve_done, 1)
                    eng.wait_ge(dve_done, did())
                    v.scalar_tensor_tensor(out=ar, in0=rt, scalar=-TWO_PI_B, in1=ar, op0=ALU.mult, op1=ALU.add).then_inc(dve_done, 1)
                    eng.wait_ge(dve_done, did())
                    v.tensor_scalar(ar, ar, 3.1415925, -3.1415925, ALU.min, ALU.max).then_inc(dve_done, 1)
                    eng.wait_ge(dve_done, did(f"arg{i} {l}"))
                if n in (5, 6):
                    eng.wait_ge(act_done, after(f"sin2 {l}"))
                    for t in (n - 5,):
                        eng.wait_ge(pe_done, after(f"f3 {l} {t}"))
                        o = bank_of(f"f3 {l} {t}")
                        v.tensor_tensor(hfil[:, t, :], o, decay[:, t, :], ALU.mult).then_inc(dve_done, 1)
                        eng.wait_ge(dve_done, did(f"read f3 {l} {t}", f"hfil {l} {t}"))
                        v.tensor_tensor(hp[:, t, :], hfil[:, t, 0:L], hfil[:, t, L:2 * L], ALU.add).then_inc(dve_done, 1)
                        did()
                        v.tensor_tensor(hm[:, t, :], hfil[:, t, 0:L], hfil[:, t, L:2 * L], ALU.subtract).then_inc(dve_done, 1)
                        did()
                if n == 6:
                    eng.wait_ge(act_done, after(f"abs {l}"))
                    for t in range(2):
                        v.tensor_tensor(fsc[:, t, :], fsc[:, t, :], farg[:, t, :], ALU.add).then_inc(dve_done, 1)
                        did(f"habs {l}")
                if n == 7:
                    eng.wait_ge(pe_done, after(f"fn {l}"))
                    o = bank_of(f"fn {l}")
                    v.reciprocal(small[:, 32:34], o[:, 0:2]).then_inc(dve_done, 1)
                    eng.wait_ge(dve_done, did(f"read fn {l}", f"rn {l}"))

            def squares(l, w, streams):
                for t in tiles_of(streams):
                    v.tensor_tensor_reduce(xn[:, t, :], X[:, t, :], X[:, t, :], 1.0, 0.0, ALU.mult, ALU.add,
                                                small[:, t:t + 1]).then_inc(dve_done, 1)
                    did(f"ss {l} {w}")

            def normalise(l, w, streams):
                ts = tiles_of(streams)
                a, b = ts[0], ts[-1] + 1
                eng.wait_ge(act_done, after(f"std {l} {w}"))
                v.reciprocal(small[:, 12:12 + b - a], small[:, 8 + a:8 + b]).then_inc(dve_done, 1)
                eng.wait_ge(dve_done, did())
                for t in ts:
                    v.tensor_scalar(xn[:, t, :], X[:, t, :], small[:, 12 + t - a:13 + t - a], None, ALU.mult).then_inc(dve_done, 1)
                    did(f"xn {l} {w} {t}")

            def norm(l, w, streams):
                if w == 2:
                    squares(l, w, streams)
                    if l == 0:
                        upto(gindex[("ffn", 0, 0, 0)])
                    normalise(l, w, streams)
                for k in range(KD):
                    eng.wait_ge(act_done, after(f"hThi {l} {w} {k}"))
                    eng.wait_ge(pe_done, after(f"nT {l} {w} {k}"))
                    o = bank_of(f"nT {l} {w} {k}")
                    j = 3 * (w - 1)
                    for s in streams:
                        q = slice(256 * s, 256 * s + 256)
                        v.tensor_scalar(tn[:, k % 2, q], o[:, q], gsc[:, w - 1, k, s:s + 1],
                                             mod[:, 8 * j + k, s:s + 1], ALU.mult, ALU.add).then_inc(dve_done, 1)
                        did(f"read nT {l} {w} {k}")
                    eng.wait_ge(dve_done, did.count)
                    q = span(streams)
                    v.tensor_tensor(hT_lo[:, k, q], tn[:, k % 2, q], hT_hi[:, k, q].bitcast(F32), ALU.subtract).then_inc(dve_done, 1)
                    did(f"hT {l} {w} {k}")

            def project_in(l, streams):
                for b in range(2):
                    for s in streams:
                        v.memset(upad[:, b, s, 0:1], 0.0).then_inc(dve_done, 1)
                        did()
                        v.memset(upad[:, b, s, 257:258], 0.0).then_inc(dve_done, 1)
                        did(f"upad {l}")
                a0, b0 = PAR["sw"][0], PAR["sb"][0]
                for ct in range(6):
                    upto(gindex[("ina", l, 0, 0)] + (ct // 2 + 1 if ct < 5 else 5))
                    eng.wait_ge(act_done, after(f"us {l} {ct}"))
                    for s in streams:
                        q = uc[:, ct, 256 * s:256 * s + 256]
                        u = lambda j: upad[:, ct % 2, s, j:j + 256]
                        w = lambda j: par[:, l, a0 + 6 * j + ct:a0 + 6 * j + ct + 1]
                        v.tensor_scalar(q, u(0), w(0), None, ALU.mult).then_inc(dve_done, 1)
                        eng.wait_ge(dve_done, did())
                        v.scalar_tensor_tensor(out=q, in0=u(1), scalar=w(1), in1=q, op0=ALU.mult, op1=ALU.add).then_inc(dve_done, 1)
                        eng.wait_ge(dve_done, did())
                        v.scalar_tensor_tensor(out=q, in0=u(2), scalar=w(2), in1=q, op0=ALU.mult, op1=ALU.add).then_inc(dve_done, 1)
                        eng.wait_ge(dve_done, did())
                        v.tensor_scalar(q, q, par[:, l, b0 + ct:b0 + ct + 1], None, ALU.add).then_inc(dve_done, 1)
                        eng.wait_ge(dve_done, did(f"conv {l} {ct}"))
                        if ct >= 4:
                            z = uc[:, ct - 2, 256 * s:256 * s + 256]
                            v.tensor_tensor(z, z, q, ALU.mult).then_inc(dve_done, 1)
                            did(f"z {l} {ct - 4}")
                upto(gindex[("inb", l, 3, 0)])

            def hyena(l, streams):
                sp = span(streams)
                eng.wait_ge(act_done, after(f"H {l}"))
                t1, t2 = ytmp[:, 0, :], ytmp[:, 1, :]
                for ft in range(2):
                    eng.wait_ge(pe_done, after(f"Zs {l} {ft}"))
                    zc, zs = bank_of(f"Zc {l} {ft}"), bank_of(f"Zs {l} {ft}")
                    dd = HD0 if ft == 0 else HA[:, 1, :]
                    for s in streams:
                        q = slice(256 * s, 256 * s + 256)
                        v.tensor_tensor(Yc[:, ft, q], zc[:, q], HA[:, ft, :], ALU.mult).then_inc(dve_done, 1)
                        did()
                        v.tensor_tensor(t1[:, q], zs[:, q], HBs[:, ft, :], ALU.mult).then_inc(dve_done, 1)
                        did()
                        v.tensor_tensor(Ys[:, ft, q], zc[:, q], HBs[:, ft, :], ALU.mult).then_inc(dve_done, 1)
                        did(f"read Zc {l} {ft}")
                        v.tensor_tensor(t2[:, q], zs[:, q], dd, ALU.mult).then_inc(dve_done, 1)
                        eng.wait_ge(dve_done, did(f"read Zs {l} {ft}"))
                    v.tensor_tensor(Yc[:, ft, sp], Yc[:, ft, sp], t1[:, sp], ALU.subtract).then_inc(dve_done, 1)
                    did()
                    v.tensor_tensor(Ys[:, ft, sp], Ys[:, ft, sp], t2[:, sp], ALU.add).then_inc(dve_done, 1)
                    eng.wait_ge(dve_done, did(f"Y {l}"))
                b0 = PAR["hyb"][0]
                for ct in range(2):
                    eng.wait_ge(pe_done, after(f"y {l} {ct}"))
                    o = bank_of(f"y {l} {ct}")
                    y = ytmp[:, ct, sp]
                    z = uc[:, 2 + ct, sp]
                    v.tensor_scalar(z, z, par[:, l, b0 + ct:b0 + ct + 1], None, ALU.mult).then_inc(dve_done, 1)
                    eng.wait_ge(dve_done, did())
                    v.scalar_tensor_tensor(out=y, in0=o[:, sp], scalar=small[:, 32 + ct:33 + ct], in1=z,
                                                op0=ALU.mult, op1=ALU.add).then_inc(dve_done, 1)
                    eng.wait_ge(dve_done, did(f"read y {l} {ct}"))
                    v.tensor_tensor(y, y, uc[:, ct, sp], ALU.mult).then_inc(dve_done, 1)
                    eng.wait_ge(dve_done, did(f"yh {l} {ct}"))
                    eng.wait_ge(act_done, after(f"mixhi {l} {ct}"))
                    v.tensor_tensor(hT_lo[:, ct, sp], y, hT_hi[:, ct, sp].bitcast(F32), ALU.subtract).then_inc(dve_done, 1)
                    did(f"mix {l} {ct}")
                did.name(f"hyena {l}")

            def pooling(l, streams):
                sp = span(streams)
                for pair in range(2):
                    eng.wait_ge(act_done, after(f"mixhi {l} {2 + pair}"))
                    eng.wait_ge(pe_done, after(f"yp {l} {pair}"))
                    o = bank_of(f"yp {l} {pair}")
                    a = PAR["psc"][0] + pair
                    v.scalar_tensor_tensor(out=hT_lo[:, 2 + pair, sp], in0=o[:, sp], scalar=par[:, l, a:a + 1],
                                                in1=hT_hi[:, 2 + pair, sp].bitcast(F32), op0=ALU.mult,
                                                op1=ALU.subtract).then_inc(dve_done, 1)
                    did(f"mix {l} {2 + pair}", f"read yp {l} {pair}")

            def latents(l, streams):
                sp = span(streams)
                for t in range(NT):
                    eng.wait_ge(act_done, after(f"Bs {l} 1 {t}"))
                    if t in tiles_of(streams):
                        v.tensor_tensor_reduce(junk, Bm[:, t, 256:640], Bm[:, t, 256:640], 1.0, 0.0, ALU.mult,
                                                    ALU.add, small[:, 16 + t:17 + t]).then_inc(dve_done, 1)
                        eng.wait_ge(dve_done, did())
                    v.tensor_tensor_reduce(junk[:, 0:KVL], Bm[:, t, 640:896], Bm[:, t, 640:896], 1.0, 0.0,
                                                ALU.mult, ALU.add, small[:, 20 + t:21 + t]).then_inc(dve_done, 1)
                    eng.wait_ge(dve_done, did(f"ssq {l}"))
                eng.wait_ge(act_done, after(f"stdq {l}"))
                v.reciprocal(small[:, 24:32], small[:, 24:32]).then_inc(dve_done, 1)
                eng.wait_ge(dve_done, did())
                for t in range(NT):
                    if t in tiles_of(streams):
                        v.tensor_scalar(Bm[:, t, 256:640], Bm[:, t, 256:640], small[:, 24 + t:25 + t], None,
                                             ALU.mult).then_inc(dve_done, 1)
                        did(f"cqn {l} {t}")
                    v.tensor_scalar(Bm[:, t, 640:896], Bm[:, t, 640:896], small[:, 28 + t:29 + t], None,
                                         ALU.mult).then_inc(dve_done, 1)
                    did(f"ckvn {l} {t}")
                eng.wait_ge(*loaded[f"mla {l}"])
                for j in range(2):
                    k1, k2 = Bm[:, 2 + j, 896:928], Bm[:, 2 + j, 928:960]
                    v.tensor_tensor(k1, k1, ropek[:, j, 0:32], ALU.mult).then_inc(dve_done, 1)
                    did()
                    v.tensor_tensor(k2, k2, ropek[:, j, 32:64], ALU.mult).then_inc(dve_done, 1)
                    eng.wait_ge(dve_done, did())
                    v.tensor_tensor(k1, k1, k2, ALU.add).then_inc(dve_done, 1)
                    did(f"kpe {l}")
                for h in range(HEADS):
                    eng.wait_ge(pe_done, after(f"q {l} {h}"))
                    o = bank_of(f"q {l} {h}")
                    if 0 in streams:
                        v.tensor_copy(qT[0:96, h, 0:256], o[0:96, 0:256]).then_inc(dve_done, 1)
                        did()
                    q = slice(256, 512)
                    v.tensor_copy(qT[0:64, h, q], o[0:64, q]).then_inc(dve_done, 1)
                    did()
                    v.tensor_tensor(qT[64:96, h, q], o[64:96, q], ropeq[64:96, 0:256], ALU.mult).then_inc(dve_done, 1)
                    did()
                    v.tensor_tensor(qtmp[64:96, :], o[96:128, q], ropeq[96:128, 256:512], ALU.mult).then_inc(dve_done, 1)
                    eng.wait_ge(dve_done, did(f"read q {l} {h}"))
                    v.tensor_tensor(qT[64:96, h, q], qT[64:96, h, q], qtmp[64:96, :], ALU.add).then_inc(dve_done, 1)
                    eng.wait_ge(dve_done, did(f"qTs {l} {h}"))

            def attention(l, streams):
                units = [(t, h) for t in tiles_of(streams) for h in range(HEADS)]
                N = len(units)

                def copy_p(n):
                    eng.wait_ge(pe_done, after(f"pT {l} {n}"))
                    o = bank_of(f"pT {l} {n}")
                    nk = 256 if units[n][0] < 2 else 512
                    if n >= 2:
                        eng.wait_ge(pe_done, after(f"pvn {l} {n - 2}"))
                    v.tensor_copy(probT[:, n % 2, 0:nk], o[:, 0:nk]).then_inc(dve_done, 1)
                    did(f"pTs {l} {n}", f"read pT {l} {n}")

                def finish(t):
                    eng.wait_ge(pe_done, after(f"pv {l} {t}"))
                    o = bank_of(f"pv {l} {t}")
                    n0 = units.index((t, 0))
                    v.reciprocal(small[:, 192:200], small[:, 128 + n0:136 + n0]).then_inc(dve_done, 1)
                    eng.wait_ge(dve_done, did())
                    for h in range(HEADS):
                        v.tensor_scalar(att[:, t, VD * h:VD * h + VD], o[:, VD * h:VD * h + VD],
                                             small[:, 192 + h:193 + h], None, ALU.mult).then_inc(dve_done, 1)
                        did(f"att {l} {t}", f"read pv {l} {t}")

                for n in range(N + 2):
                    if n < N:
                        t, h = units[n]
                        nk = 256 if t < 2 else 512
                        eng.wait_ge(pe_done, after(f"s {l} {n}"))
                        o = bank_of(f"s {l} {n}")
                        v.reduce_max(small[:, 64 + n:65 + n], o[:, 0:nk], AX.X).then_inc(dve_done, 1)
                        eng.wait_ge(dve_done, did())
                        v.tensor_scalar(small[:, 64 + n:65 + n], small[:, 64 + n:65 + n], -SM_SCALE, None, ALU.mult).then_inc(dve_done, 1)
                        did(f"nmax {l} {n}")
                    if 1 <= n <= N:
                        copy_p(n - 1)
                    if n == 2:
                        upto(gindex[("out", l, 2, 0)])
                    if n - 4 in streams:
                        diagonal(l, 0, n - 4)
                    if n >= 2 and units[n - 2][1] == HEADS - 1:
                        finish(units[n - 2][0])
                sp = span(streams)
                for k in range(4):
                    eng.wait_ge(act_done, after(f"mixhi {l} {4 + k}"))
                    eng.wait_ge(pe_done, after(f"aT {l} {k}"))
                    o = bank_of(f"aT {l} {k}")
                    v.tensor_tensor(hT_lo[:, 4 + k, sp], o[:, sp], hT_hi[:, 4 + k, sp].bitcast(F32),
                                         ALU.subtract).then_inc(dve_done, 1)
                    did(f"mix {l} {4 + k}", f"read aT {l} {k}")

            def diagonal(l, w, s):
                dg = diag[s] if w == 0 else fdiag
                j = 16 if w == 0 else 40
                for k in range(KD):
                    v.tensor_scalar(dg[:, k, :], ident[:, :], mod[:, j + k, s:s + 1], None, ALU.mult).then_inc(dve_done, 1)
                    did(f"diag {l} {w} {s}")

            def project_out(l, streams):
                upto(gindex[("out", l, 3, 0)])
                eng.wait_ge(act_done, after(f"gb {l} 0 {streams[-1]}"))
                for n in range(2):
                    for j, t in enumerate(tiles_of(streams)):
                        eng.wait_ge(pe_done, after(f"o {l} {n} {t}"))
                        o = bank_of(f"o {l} {n} {t}")
                        q = slice(512 * n, 512 * n + 512)
                        v.tensor_tensor(rtmp[:, j % 2, :], o, gbc[:, t // 2, q], ALU.mult).then_inc(dve_done, 1)
                        eng.wait_ge(dve_done, did(f"read o {l} {n} {t}"))
                        v.tensor_tensor(X[:, t, q], X[:, t, q], rtmp[:, j % 2, :], ALU.add).then_inc(dve_done, 1)
                        did(f"projected {l}")
                eng.wait_ge(dve_done, did.count)

            def residual(s, tt):
                if s == 0:
                    eng.wait_ge(act_done, after("gb 0 1 0"))
                    v.tensor_tensor(acc[:, tt, :], acc[:, tt, :], gbf, ALU.mult).then_inc(dve_done, 1)
                    eng.wait_ge(dve_done, did(f"res {s} {tt}"))
                    v.tensor_tensor(X[:, tt, :], X[:, tt, :], acc[:, tt, :], ALU.add).then_inc(dve_done, 1)
                    eng.wait_ge(dve_done, did())
                else:
                    eng.wait_ge(act_done, after("gb 0 1 1"))
                    eng.wait_ge(pe_done, after(f"down f1 {FC - 1}"))
                    for n in range(2):
                        q = slice(512 * n, 512 * n + 512)
                        v.tensor_tensor(acc2[:, tt, q], PS[:, 4 + 2 * tt + n, :], gbf[:, q], ALU.mult).then_inc(dve_done, 1)
                        did(f"read y f1 {tt} {n}")
                    eng.wait_ge(dve_done, did.count)
                    v.tensor_tensor(X[:, 2 + tt, :], X[:, 2 + tt, :], acc2[:, tt, :], ALU.add).then_inc(dve_done, 1)
                    eng.wait_ge(dve_done, did())

            def feed_forward(name, p):
                def turned(s):
                    eng.wait_ge(act_done, after(f"fhi {name} {s}"))
                    eng.wait_ge(pe_done, after(f"hh {name} {s}"))
                    o = bank_of(f"hh {name} {s}")
                    v.tensor_tensor(f_lo[:, :], o, f_hi[:, :].bitcast(F32), ALU.subtract).then_inc(dve_done, 1)
                    did(f"fs {name} {s}", f"read hh {name} {s}")

                upto(gindex[("ffn", 0, 2, p)])
                for s in range(FC):
                    if s:
                        turned(s - 1)
                    if last_group(p, s) is not None:
                        bias_mod(1, last_group(p, s))
                    if beside(p, s) is not None:
                        upto(gindex[("ada", 1, 2 * beside(p, s) + 1, 0)])
                    elif s + 1 < FC:
                        upto(gindex[("ffn", 0, fpos[("gu", s + 1, 1)], p)])
                    for tt in range(2):
                        eng.wait_ge(act_done, after(f"sg {name} {s} {tt}"))
                        eng.wait_ge(pe_done, after(f"gu {name} {s} {tt}"))
                        o = bank_of(f"gu {name} {s} {tt}")
                        v.tensor_tensor(hh[:, tt, :], o[:, 256:512], sg[:, tt, :], ALU.mult).then_inc(dve_done, 1)
                        did(f"h {name} {s} {tt}", f"read gu {name} {s} {tt}")
                    upto(gindex[("ffn", 0, fpos[("d", s, 0)], p)])
                    if p == 1:
                        filters(1, s)
                        if s in (6, 7):
                            residual(0, s - 6)
                        if s == 6:
                            diagonal(0, 1, 1)
                        if s == 8:
                            squares(1, 1, (0,))
                if p == 0:
                    upto(gindex[("ffn", 0, 0, 1)])
                turned(FC - 1)
                upto(gindex[("ffn", 0, 1, 1) if p == 0 else ("ina", 1, 1, 0)])

            def choose():
                eng.wait_ge(act_done, after("rhi"))
                v.tensor_tensor(r_lo[:, :, :], router, r_hi[:, :, :].bitcast(F32), ALU.subtract).then_inc(dve_done, 1)
                did("router split")
                for j in range(RING):
                    eng.wait_ge(x_hi, j + 1)
                    v.tensor_tensor(w_lo[:, j, :], x_raw(j), w_hi[:, j, :].bitcast(F32), ALU.subtract).then_inc(x_lo, 1)
                eng.wait_ge(pe_done, after("logits"))
                o = bank_of("logits")
                lg = small[:, 204:220]
                v.tensor_copy(lg, o[:, 0:16]).then_inc(dve_done, 1)
                eng.wait_ge(dve_done, did("read logits"))
                for tt in range(2):
                    v.max(small[:, 220:228], lg[:, 8 * tt:8 * tt + 8]).then_inc(dve_done, 1)
                    eng.wait_ge(dve_done, did())
                    v.max_index(idx8[:, :], small[:, 220:228], lg[:, 8 * tt:8 * tt + 8]).then_inc(dve_done, 1)
                    eng.wait_ge(dve_done, did())
                    v.tensor_copy(small[:, 42 + 2 * tt:44 + 2 * tt], idx8[:, 0:2]).then_inc(dve_done, 1)
                    eng.wait_ge(dve_done, did())
                    v.tensor_tensor(small[:, 38 + tt:39 + tt], small[:, 221:222], small[:, 220:221],
                                         ALU.subtract).then_inc(dve_done, 1)
                    eng.wait_ge(dve_done, did("dlogit"))
                eng.wait_ge(act_done, after("elogit"))
                v.tensor_scalar(small[:, 46:48], small[:, 40:42], 1.0, None, ALU.add).then_inc(dve_done, 1)
                eng.wait_ge(dve_done, did())
                v.reciprocal(small[:, 46:48], small[:, 46:48]).then_inc(dve_done, 1)
                eng.wait_ge(dve_done, did())
                v.tensor_tensor(small[:, 48:50], small[:, 40:42], small[:, 46:48], ALU.mult).then_inc(dve_done, 1)
                eng.wait_ge(dve_done, did())
                mask = rt[:, 0:2 * NE].rearrange("p (t e) -> p t e", e=NE)
                for tt in range(2):
                    for n in range(2):
                        v.tensor_scalar(rt[:, 48 + 8 * n:56 + 8 * n], iota8[:, :],
                                        small[:, 42 + 2 * tt + n:43 + 2 * tt + n], None,
                                        ALU.is_equal).then_inc(dve_done, 1)
                        eng.wait_ge(dve_done, did())
                    v.tensor_tensor(mask[:, tt, :], rt[:, 48:56], rt[:, 56:64], ALU.add).then_inc(dve_done, 1)
                    eng.wait_ge(dve_done, did("mask"))
                for tt in range(2):
                    v.tensor_scalar(comb[:, tt, :], iota8[:, :], small[:, 42 + 2 * tt:43 + 2 * tt],
                                         small[:, 46 + tt:47 + tt], ALU.is_equal, ALU.mult).then_inc(dve_done, 1)
                    eng.wait_ge(dve_done, did())
                    v.tensor_scalar(small[:, 228:236], iota8[:, :], small[:, 43 + 2 * tt:44 + 2 * tt],
                                         small[:, 48 + tt:49 + tt], ALU.is_equal, ALU.mult).then_inc(dve_done, 1)
                    eng.wait_ge(dve_done, did())
                    v.tensor_tensor(comb[:, tt, :], comb[:, tt, :], small[:, 228:236], ALU.add).then_inc(dve_done, 1)
                    eng.wait_ge(dve_done, did())

            def plan_passes():
                mask = rt[:, 0:2 * NE].rearrange("p (t e) -> p t e", e=NE)
                eng.wait_ge(pe_done, after("rank"))
                o = bank_of("rank")
                over, cum, one = rt[:, 16:24], rt[:, 24:32], rt[:, 32:40]
                for tt in range(2):
                    v.memset(acc[:, tt, :], 0.0).then_inc(x_add, 1)
                v.tensor_scalar(over, o[:, 16:24], float(P), None, ALU.is_gt).then_inc(dve_done, 1)
                did()
                for tt in range(2):
                    v.scalar_tensor_tensor(out=place_s[:, tt, 0:NE], in0=o[:, NE * tt:NE * tt + NE], scalar=1.0,
                                           in1=mask[:, tt, :], op0=ALU.add, op1=ALU.mult).then_inc(dve_done, 1)
                    did("read rank")
                    v.tensor_copy(comb_s[:, tt, 0:NE], comb[:, tt, :]).then_inc(dve_done, 1)
                    did()
                v.tensor_copy(expert_f[:, 0:NE], iota8[:, :]).then_inc(dve_done, 1)
                eng.wait_ge(dve_done, did())
                v.tensor_copy(cum[:, 0:1], over[:, 0:1]).then_inc(dve_done, 1)
                eng.wait_ge(dve_done, did())
                for e in range(1, NE):
                    v.tensor_tensor(cum[:, e:e + 1], cum[:, e - 1:e], over[:, e:e + 1], ALU.add).then_inc(dve_done, 1)
                    eng.wait_ge(dve_done, did())
                for x in range(COLS - NE):
                    v.scalar_tensor_tensor(out=one, in0=cum, scalar=float(x + 1), in1=over, op0=ALU.is_equal,
                                           op1=ALU.mult).then_inc(dve_done, 1)
                    eng.wait_ge(dve_done, did())
                    for src, dst in ((iota8[:, :], expert_f[:, NE + x:NE + x + 1]),
                                     (place_s[:, 0, 0:NE], place_s[:, 0, NE + x:NE + x + 1]),
                                     (place_s[:, 1, 0:NE], place_s[:, 1, NE + x:NE + x + 1]),
                                     (comb[:, 0, :], comb_s[:, 0, NE + x:NE + x + 1]),
                                     (comb[:, 1, :], comb_s[:, 1, NE + x:NE + x + 1])):
                        v.tensor_tensor_reduce(rt[:, 40:48], one, src, 1.0, 0.0, ALU.mult, ALU.add,
                                               dst).then_inc(dve_done, 1)
                        eng.wait_ge(dve_done, did())
                v.tensor_scalar(place_s[:, :, 0:NE], place_s[:, :, 0:NE], 1.0, None, ALU.subtract).then_inc(dve_done, 1)
                did()
                v.tensor_scalar(place_s[:, :, NE:COLS], place_s[:, :, NE:COLS], 1.0 + P, None,
                                ALU.subtract).then_inc(dve_done, 1)
                eng.wait_ge(dve_done, did())
                v.tensor_copy(expert_i[:, :], expert_f[0:1, :]).then_inc(dve_done, 1)
                did()
                v.tensor_copy(second[:, :], cum[0:1, NE - 1:NE]).then_inc(dve_done, 1)
                eng.wait_ge(dve_done, did("plan"))

            def choose_tokens(i):
                if not (isinstance(i, int) and i == 0):
                    eng.wait_ge(x_pickT, i)
                for tt in range(2):
                    where = place_s[:, tt, i:i + 1] if isinstance(i, int) else place_s[:, tt, bass.ds(i, 1)]
                    last = v.tensor_scalar(pick[:, tt, :], iota, where, None, ALU.is_equal)
                last.then_inc(x_pick, 1)

            def gathered(i, par, q):
                eng.wait_ge(x_ghi, 2 * i + q + 1)
                for kk in range(4):
                    k = 4 * q + kk
                    last = v.tensor_scalar(gt[:, kk, :], PS[:, 3, P * kk:P * kk + P], gsc[:, 1, k, 1:2],
                                           mod[:, 24 + k, 1:2], ALU.mult, ALU.add)
                last.then_inc(x_gt, 1)
                eng.wait_ge(x_gt, 2 * i + q + 1)
                v.tensor_tensor(hT_lo[:, 4 * q:4 * q + 4, 256 + P * par:384 + P * par], gt,
                                hT_hi[:, 4 * q:4 * q + 4, 256 + P * par:384 + P * par].bitcast(F32),
                                ALU.subtract).then_inc(x_glo, 1)

            def add_up(i, tt):
                eng.wait_ge(x_z, 2 * i + 1 + tt)
                eng.wait_ge(x_add, 2 * i + tt)
                weight = comb_s[:, tt, i - 1:i] if isinstance(i, int) else comb_s[:, tt, bass.ds(i - 1, 1)]
                for n in range(2):
                    a = acc[:, tt, 512 * n:512 * n + 512]
                    last = v.scalar_tensor_tensor(out=a, in0=PS[:, 6 + n, :], scalar=weight, in1=a,
                                                  op0=ALU.mult, op1=ALU.add)
                last.then_inc(x_add, 1)

            def expert_pass(i, par, follows):
                def low(j):
                    eng.wait_ge(x_hi, NGR * i + j + 1)
                    v.tensor_tensor(w_lo[:, j % RING, :], x_raw(NGR * par + j),
                                    w_hi[:, j % RING, :].bitcast(F32), ALU.subtract).then_inc(x_lo, 1)

                def low_turned(s):
                    eng.wait_ge(x_thi, FC * i + s + 1)
                    v.tensor_tensor(f_lo[:, 0:256], PS[:, 2, 0:256], f_hi[:, 0:256].bitcast(F32),
                                    ALU.subtract).then_inc(x_tlo, 1)

                if follows:
                    for j in range(RING):
                        low(j)
                for s in range(FC):
                    if s:
                        low_turned(s - 1)
                    if s + 1 < FC:
                        for j in range(fpos[("gu", s + 1, 0)] if s else RING, fpos[("gu", s + 1, 1)] + 1):
                            low(j)
                    eng.wait_ge(x_silu, FC * i + s + 1)
                    v.tensor_tensor(hh[:, s % 2, :], PS[:, s % 2, 256:512], sg[:, s % 2, :],
                                    ALU.mult).then_inc(x_h, 1)
                    low(fpos[("d", s, 0)])
                    if follows and s in (2, 4):
                        add_up(i, s // 4)
                    if s == 3:
                        choose_tokens(i + 1)
                    if s in (6, 8):
                        gathered(i + 1, 1 - par, s // 8)
                low_turned(FC - 1)

            for l in range(DEPTH):
                streams = layer_streams[l]
                if l == 0:
                    modulation()
                else:
                    squares(1, 1, (1,))
                    v.tensor_copy(mod[:, :, :], mod1).then_inc(dve_done, 1)
                    did()
                    scales(1)
                    normalise(1, 1, (0, 1))
                norm(l, 1, (0, 1))
                project_in(l, streams)
                hyena(l, streams)
                pooling(l, streams)
                latents(l, streams)
                attention(l, streams)
                project_out(l, streams)
                norm(l, 2, streams)
                if l == 0:
                    condition(1)
                    for s in (0, 1):
                        feed_forward(f"f{s}", s)
                        if s == 0:
                            diagonal(l, 1, 0)
                            for tt in range(2):
                                for n in range(2):
                                    eng.wait_ge(pe_done, after(f"down f0 {FC - 1}"))
                                    v.tensor_copy(acc[:, tt, 512 * n:512 * n + 512], PS[:, 4 + 2 * tt + n, :]).then_inc(dve_done, 1)
                                    did(f"read y f0 {tt} {n}")
                        else:
                            residual(1, 0)
                            residual(1, 1)
                    did.name("layer 0")
                else:
                    choose()
                    diagonal(l, 1, 1)
                    for tt in range(2):
                        eng.wait_ge(act_done, after("xhi"))
                        v.tensor_tensor(hT_lo[:, :, P * tt:P * tt + P],
                                        xn[:, 2 + tt, :].rearrange("p (k c) -> p k c", c=P),
                                        hT_hi[:, :, P * tt:P * tt + P].bitcast(F32), ALU.subtract).then_inc(dve_done, 1)
                        did("xlo")
                    plan_passes()
                    passes = NE + eng.value_load(second[0:1, 0:1], min_val=0, max_val=SLOTS - NE)
                    choose_tokens(0)
                    gathered(0, 0, 0)
                    gathered(0, 0, 1)
                    expert_pass(0, 0, False)
                    with eng.Fori(0, (SLOTS - 1) // 2) as j:
                        for odd in (1, 0):
                            i = 2 * j + (1 if odd else 2)
                            with eng.If(i < passes):
                                expert_pass(i, odd, True)
                    add_up(passes, 0)
                    add_up(passes, 1)
                    eng.wait_ge(x_add, 2 * passes + 2)
                    eng.wait_ge(act_done, after(f"gb {l} 1 1"))
                    for tt in range(2):
                        v.tensor_tensor(acc[:, tt, :], acc[:, tt, :], gbf, ALU.mult).then_inc(dve_done, 1)
                        eng.wait_ge(dve_done, did())
                        v.tensor_tensor(X[:, 2 + tt, :], X[:, 2 + tt, :], acc[:, tt, :], ALU.add).then_inc(dve_done, 1)
                        eng.wait_ge(dve_done, did())
            for tt in range(2):
                v.tensor_tensor_reduce(acc[:, tt, :], X[:, 2 + tt, :], X[:, 2 + tt, :], 1.0, 0.0, ALU.mult,
                                            ALU.add, small[:, 34 + tt:35 + tt]).then_inc(dve_done, 1)
                eng.wait_ge(dve_done, did("ssf"))
            eng.wait_ge(act_done, after("stdf"))
            v.reciprocal(small[:, 36:38], small[:, 36:38]).then_inc(dve_done, 1)
            eng.wait_ge(dve_done, did())
            for tt in range(2):
                v.tensor_scalar(acc[:, tt, :], X[:, 2 + tt, :], small[:, 36 + tt:37 + tt], None, ALU.mult).then_inc(dve_done, 1)
                eng.wait_ge(dve_done, did())
                v.tensor_tensor(acc[:, tt, :], acc[:, tt, :], fing, ALU.mult).then_inc(dve_done, 1)
                eng.wait_ge(dve_done, did(f"out {tt}"))

        @blk.sync
        def _(eng):
            for g, (kind, e, i) in enumerate(plan):
                w = width(kind)
                if before_it[g] is not None:
                    eng.wait_ge(dve_done, after(f"lo {before_it[g]}"))
                eng.dma_start(raw_at(g)[:, 0:w], source(kind, e, i)).then_inc(raw_full[place[g]], 16)
            def expert_stream(i, par, pair, expert):
                for j in range(NGR):
                    n = NGR * par + j
                    if not isinstance(i, int) or j >= XRING:
                        eng.wait_ge(x_lo, NGR * i + j + 1 - XRING)
                    elif j < RING:
                        eng.wait_ge(dve_done, after(f"lo {NG - RING + (j - NG) % RING}"))
                    else:
                        eng.wait_ge(dve_done, after("projected 1"))
                    src = io["moe"][0, j] if expert is None else io["moe"][bass.ds(expert, 1), j].rearrange(
                        "a p n -> (a p) n")
                    eng.dma_start(x_raw(n), src).then_inc(x_full[n % XRING], 16)

            expert_stream(0, 0, 0, None)
            eng.wait_ge(dve_done, after("plan"))
            passes = NE + eng.value_load(second[0:1, 0:1], min_val=0, max_val=SLOTS - NE)
            with eng.Fori(0, (SLOTS - 1) // 2) as j:
                for odd in (1, 0):
                    i = 2 * j + (1 if odd else 2)
                    with eng.If(i < passes):
                        expert = eng.value_load(expert_i[0:1, bass.ds(i, 1)], min_val=0, max_val=NE - 1)
                        expert_stream(i, odd, j, expert)
            stored = loaded["stored"][0]
            for tt in range(2):
                eng.wait_ge(dve_done, after(f"out {tt}"))
                eng.dma_start(io["y"][P * tt:P * tt + P, :], acc[:, tt, :]).then_inc(stored, 16)
            eng.wait_ge(stored, 32)

        @blk.gpsimd
        def _(eng):
            def load(name, *pairs):
                s = loaded[name][0]
                for dst, src in pairs:
                    eng.dma_start(dst, src).then_inc(s, 16)
                assert loaded[name][1] == 16 * len(pairs)

            load("condition", (cvec[:, :, :], io["cvec"]), (sel[:, :], io["sel"]))
            load("start", (par[:, :, :], io["par"]), (ident[:, :], io["ident"]), (ones[:, :], io["ones"]),
                 (iota8[:, :], io["iota8"]), *((X[:, t, :], io["x"][P * t:P * t + P, :]) for t in range(NT)))
            for l in range(DEPTH):
                if l:
                    eng.wait_ge(dve_done, after("projected 0"))
                load(f"hy {l}", (hyc, io["hyc"]), (fw, io["fw"][l]))
                eng.wait_ge(pe_done, after(f"fD {l}"))
                eng.wait_ge(dve_done, after(f"habs {l}"))
                eng.wait_ge(act_done, after(f"abs {l}"))
                load(f"pool {l}", (A(14600, 2048), io["pm"]), (pwts[0:GROUP], io["pw"][l]))
                eng.wait_ge(dve_done, after(f"hyena {l}"))
                eng.wait_ge(pe_done, after(f"y {l} 1"))
                eng.wait_ge(pe_done, after(f"zT {l} 1"))
                eng.wait_ge(act_done, after(f"mixhi {l} 1"))
                load(f"mla {l}", (A(7936, 3072), io["wuq"][l]), (A(11008, 2048), io["wukv"][l]), (A(19712, 512), io["ropeq"]),
                     (A(20224, 128), io["ropek"]))
            eng.wait_ge(act_done, after("mixhi 1 7"))
            load("route", (router, io["router"]), (iota, io["iota"]), (before, io["before"]), (fing, io["fing"]))


def lay(inputs):
    f = lambda n: np.asarray(inputs[n])
    c = np.ascontiguousarray
    io = {}
    io["x"] = c(np.concatenate([f("ctx")[0], f("x")[0]], axis=0))
    io["cvec"] = c(np.stack([f("c_ctx"), f("c")[0]], axis=-1).reshape(KD, P, 2).transpose(1, 0, 2))
    io["ada"] = c(f("w_ada").reshape(DEPTH, 2, 4, P, 12, 512).transpose(0, 4, 1, 3, 2, 5).reshape(DEPTH, 24, P, GRAN))
    w_in = f("w_in")
    io["ina"] = c(w_in[:, :, :3 * HY].reshape(DEPTH, KD, P, 3, 256).transpose(0, 3, 2, 1, 4).reshape(DEPTH, 3, P, GRAN))
    a = w_in.shape[2] - ROPE
    inb = np.concatenate([w_in[:, :, 3 * HY:], w_in[:, :, a + ROPE // 2:], w_in[:, :, a:a + ROPE // 2]], axis=2)
    io["inb"] = c(inb.reshape(DEPTH, 2, 4, P, 2, HB).transpose(0, 4, 1, 3, 2, 5).reshape(DEPTH, 4, P, 4 * HB))
    io["out"] = c(f("w_out").reshape(DEPTH, 2, 4, P, 2, 512).transpose(0, 4, 1, 3, 2, 5).reshape(DEPTH, 4, P, GRAN))

    def swiglu(wg, wu, wd):
        n = wg.shape[0]
        out = np.empty((n, 3 * FC, P, GRAN), wg.dtype)
        gu = out.reshape(n, 3 * FC, P, 4, 2, 256)
        g6, u6 = (w.reshape(n, 2, 4, P, FC, 256) for w in (wg, wu))
        d5 = wd.reshape(n, FC, 2, P, D)
        for i, (kind, s, half) in enumerate(ffn_order()):
            if kind == "gu":
                gu[:, i, :, :, 0, :] = g6[:, half, :, :, s, :].transpose(0, 2, 1, 3)
                gu[:, i, :, :, 1, :] = u6[:, half, :, :, s, :].transpose(0, 2, 1, 3)
            else:
                out[:, i] = d5[:, s].transpose(0, 2, 1, 3).reshape(n, P, GRAN)
        return out

    io["ffn"] = swiglu(f("ffn_wg"), f("ffn_wu"), f("ffn_wd"))
    io["moe"] = swiglu(f("moe_wg")[0], f("moe_wu")[0], f("moe_wd")[0])
    io["router"] = c(f("moe_router")[0].reshape(KD, P, NE).transpose(1, 0, 2))
    par = np.zeros((P, DEPTH, NPAR), np.float32)

    def put(name, a):
        lo, hi = PAR[name]
        par[:a.shape[-1], :, lo:hi] = a.reshape(DEPTH, hi - lo, a.shape[-1]).transpose(2, 0, 1)

    for name, src in (("g1", "norm1_g"), ("g2", "norm2_g"), ("bada", "b_ada"), ("qg", "q_norm_g"), ("kvg", "kv_norm_g"),
                      ("sw", "hy_short_w"), ("sb", "hy_short_b"), ("hyb", "hy_bias"), ("psc", "pool_scale")):
        put(name, f(src).reshape(DEPTH, -1, P))
    for name, src in (("b1", "filt_b1"), ("f1", "filt_freq1"), ("b2", "filt_b2"), ("f2", "filt_freq2")):
        put(name, f(src).reshape(DEPTH, 1, FH))
    io["par"] = par
    uq = f("w_uq").reshape(DEPTH, KQ, P, HEADS, NOPE + ROPE)
    uq = np.concatenate([uq, uq[..., NOPE + ROPE // 2:], uq[..., NOPE:NOPE + ROPE // 2]], axis=-1)
    io["wuq"] = c(uq.transpose(0, 2, 1, 3, 4).reshape(DEPTH, P, KQ * HEADS * P))
    ukv = f("w_ukv").reshape(DEPTH, KKV, P, HEADS, 2, NOPE)
    io["wukv"] = c(ukv.transpose(0, 2, 1, 4, 3, 5).reshape(DEPTH, P, KKV * 1024))
    io["pw"] = c(f("pool_w").transpose(0, 2, 1, 3))
    fw = np.zeros((DEPTH, P, 640), np.float32)
    fw[:, :FE, 0:64] = f("filt_w1")
    fw[:, :FH, 64:128] = f("filt_w2")
    fw[:, :FH, 128:640] = f("filt_w3")
    io["fw"] = fw
    io["iota"] = c(np.broadcast_to(np.arange(P, dtype=np.float32), (P, P)))
    io["before"] = np.triu(np.ones((P, P), np.float32), 1)
    io["fing"] = c(np.broadcast_to(f("final_g"), (P, D)))

    t = np.arange(L)
    fr = np.arange(L)
    sign = (-1.0) ** t
    ang = 2 * np.pi * ((np.outer(t, fr)) % (2 * L)) / (2 * L)
    C, S = np.cos(ang), np.sin(ang)
    Sn, Cn = S.copy(), C.copy()
    Sn[:, 0], Cn[:, 0] = sign, sign
    wt = np.full(L, 2.0 / (2 * L))
    wt[0] = 1.0 / (2 * L)
    tiles = lambda m: m.reshape(2, P, -1).transpose(1, 0, 2).reshape(P, -1)
    tt = (t / (L - 1)).astype(np.float32)
    deltas = np.linspace(math.log(1e-2) / 1.5, math.log(1e-2) / 0.3, HY)
    dec = np.exp(-tt[:, None].astype(np.float64) * np.abs(deltas))
    dec2 = np.concatenate([dec, dec], axis=1)
    dec2[0, HY:] = 0.0
    bands = (FE - 1) // 2
    w = 2.0 * math.pi * t[:, None] / L
    fb = np.linspace(1e-4, bands - 1, bands)[None, :]
    feat = np.concatenate([tt[:, None], np.cos(fb * w), -np.sin(fb * w)], axis=1)
    featT = np.zeros((P, L))
    featT[:FE] = feat.T
    io["hyc"] = np.concatenate([tiles(C), tiles(Sn), tiles(S[:, :P]), tiles(Cn[:, :P]), tiles((C * wt).T),
                                tiles((Sn * wt).T), tiles(dec2), featT], axis=1).astype(np.float32)
    pm = np.zeros((4, L, L))
    for g, win in enumerate(WINDOWS):
        for i in range(L):
            lo, hi = max(i - win // 2, 0), min(i + win // 2, L)
            pm[g, lo:hi, i] = 1.0 / (hi - lo)
            pm[g, i, i] -= 1.0
    io["pm"] = np.stack([tiles(m) for m in pm], axis=1).reshape(P, 4 * 2 * L).astype(np.float32)
    nf = ROPE // 4
    inv = 1.0 / (10000.0 ** (np.arange(nf) / nf))
    an = np.concatenate([(t // 64)[:, None] * inv, (t % 64)[:, None] * inv], axis=1)
    co, si = np.cos(an), np.sin(an)
    COS, SIN = np.concatenate([co, co], 1), np.concatenate([-si, si], 1)
    rq = np.zeros((P, 512), np.float32)
    rq[64:96, 0:256] = COS.T
    rq[96:128, 256:512] = SIN.T
    io["ropeq"] = rq
    io["ropek"] = np.concatenate([COS, SIN], axis=1).reshape(2, P, 64).transpose(1, 0, 2).astype(np.float32)
    io["ident"] = np.eye(P, dtype=np.float32)
    io["ones"] = np.ones((P, P), np.float32)
    io["sel"] = np.array([[1, 0], [0, 1], [1, 0], [0, 1]], np.float32)
    io["iota8"] = c(np.broadcast_to(np.arange(NE, dtype=np.float32), (P, NE)))
    return {k: c(v) for k, v in io.items()}


def kernel(**inputs):
    import concourse.bacc as _bacc
    from concourse.bass_utils import run_bass_kernel_spmd as _run

    data = lay(inputs)
    table = {"count": {}, "bank": {}, "final": False}
    for final in (False, True):
        nc = _bacc.Bacc("TRN2", target_bir_lowering=False, num_devices=1)
        io = {k: nc.dram_tensor(f"in_{k}", v.shape, F32, kind="ExternalInput").ap() for k, v in data.items()}
        io["y"] = nc.dram_tensor("out_y", (L, D), F32, kind="ExternalOutput").ap()
        build(nc, io, table)
        table["final"] = True
    r = _run(nc, [{f"in_{k}": v for k, v in data.items()}], core_ids=[0])
    return r.results[0]["out_y"].reshape(1, L, D)
```
